# Optimizing a Trainium2 kernel written in Bass

```python
import math, functools
import jax, jax.numpy as jnp
from jax import lax
import numpy as np

D_MODEL = 1024
BATCH = 1
SEQ = 128
DEPTH = 2
DEC_BATCH = 1
DEC_SEQ = 512
PAST_LEN = 256

GRID_W = 64
HEAD_DIM = 64
MIX_WIDTH = D_MODEL
GROUP_WIDTH = MIX_WIDTH // 4
GROUP_HEADS = GROUP_WIDTH // HEAD_DIM
GLA_HEADS = GROUP_HEADS
GLA_LOWRANK = 16
GLA_TAU = 16.0
GLA_CHUNK = 64
SWA_HEADS = GROUP_HEADS
SWA_KV_HEADS = 2
SWA_WINDOW = 128
SWA_BLOCK = 128
NA_HEADS = GROUP_HEADS
NA_KH = 8
NA_KW = 16
GDN_HEADS = GROUP_HEADS
GDN_CONV = 3
GDN_CHUNK = 64
D_FF = 2816
N_EXPERTS = 8
TOP_K = 2
D_FF_EXPERT = 1024
N_DENSE = (DEPTH + 1) // 2
N_MOE = DEPTH // 2
ROPE_BASE = 10000.0
CTX_BLOCK = 128
EPS = 1e-6
NEG_INF = -1e30
SWA_KV_WIDTH = SWA_KV_HEADS * HEAD_DIM
IN_SPLITS = [GROUP_WIDTH] * 4 + [GLA_LOWRANK] * 2 + [GROUP_WIDTH, SWA_KV_WIDTH, SWA_KV_WIDTH] + [GROUP_WIDTH] * 3 + [GROUP_WIDTH] * 4 + [GDN_HEADS] * 4
IN_COLS = sum(IN_SPLITS)

kernel_name = 'hybrid_parallel_heads_diffusion_step'

def _rmsnorm(x, g):
    xf = x.astype(jnp.float32)
    y = xf * lax.rsqrt(jnp.mean(xf * xf, axis=-1, keepdims=True) + EPS)
    return (y * g.astype(jnp.float32)).astype(x.dtype)

def _l2norm(x):
    xf = x.astype(jnp.float32)
    return (xf * lax.rsqrt(jnp.sum(xf * xf, axis=-1, keepdims=True) + EPS)).astype(x.dtype)

def _split(x, sizes):
    cuts = [int(s) for s in np.cumsum(sizes)[:-1]]
    return jnp.split(x, cuts, axis=-1)

def _heads(t, n):
    b, s, _ = t.shape
    return t.reshape(b, s, n, -1).transpose(0, 2, 1, 3)

def _merge(t):
    b, h, s, d = t.shape
    return t.transpose(0, 2, 1, 3).reshape(b, s, h * d)

def _flip(t):
    return jnp.flip(t, axis=2)

def _rope_2d(x):
    n = x.shape[2]
    t = jnp.arange(n)
    rows = (t // GRID_W).astype(jnp.float32)
    cols = (t % GRID_W).astype(jnp.float32)
    half = HEAD_DIM // 2
    nf = half // 2
    inv = 1.0 / (ROPE_BASE ** (jnp.arange(nf, dtype=jnp.float32) / nf))

    def rot(xp, pos):
        ang = pos[:, None] * inv[None, :]
        cos, sin = jnp.cos(ang), jnp.sin(ang)
        x1, x2 = xp[..., :nf], xp[..., nf:]
        return jnp.concatenate([x1 * cos - x2 * sin, x1 * sin + x2 * cos], axis=-1)

    xf = x.astype(jnp.float32)
    out = jnp.concatenate([rot(xf[..., :half], rows), rot(xf[..., half:], cols)], axis=-1)
    return out.astype(x.dtype)

def _dwconv(x, w):
    k, c = w.shape
    return lax.conv_general_dilated(x, w[:, None, :].astype(x.dtype), window_strides=(1,),
                                    padding=[(k // 2, k // 2)],
                                    dimension_numbers=('NWC', 'WIO', 'NWC'),
                                    feature_group_count=c)

def _gla_chunked(q, k, v, log_a, s0):
    b, h, n, dk = q.shape
    dv = v.shape[-1]
    L = GLA_CHUNK
    nc = n // L
    f32 = jnp.float32
    qf = q.astype(f32).reshape(b, h, nc, L, dk) * (dk ** -0.5)
    kf = k.astype(f32).reshape(b, h, nc, L, dk)
    vf = v.astype(f32).reshape(b, h, nc, L, dv)
    cum = jnp.cumsum(log_a.astype(f32).reshape(b, h, nc, L, dk), axis=3)
    last = cum[:, :, :, -1:, :]
    q_dec = qf * jnp.exp(cum)
    k_inv = kf * jnp.exp(-cum)
    k_end = kf * jnp.exp(last - cum)
    causal = jnp.tril(jnp.ones((L, L), bool))
    att = jnp.where(causal, jnp.einsum('bhcid,bhcjd->bhcij', q_dec, k_inv), 0.0)
    o_intra = jnp.einsum('bhcij,bhcjv->bhciv', att, vf)

    def step(s, xs):
        qd, ke, dl, vc, oi = xs
        o = oi + jnp.einsum('bhid,bhdv->bhiv', qd, s)
        s = dl[..., None] * s + jnp.einsum('bhjd,bhjv->bhdv', ke, vc)
        return s, o

    xs = tuple(jnp.moveaxis(t, 2, 0) for t in (q_dec, k_end, jnp.exp(last[:, :, :, 0, :]), vf, o_intra))
    s_fin, o = lax.scan(step, s0.astype(f32), xs)
    o = jnp.moveaxis(o, 0, 2).reshape(b, h, n, dv)
    return o.astype(v.dtype), s_fin.astype(s0.dtype)

def _gdn_chunked(q, k, v, g, beta, s0):
    b, h, n, dk = q.shape
    dv = v.shape[-1]
    L = GDN_CHUNK
    nc = n // L
    f32 = jnp.float32
    qf = q.astype(f32).reshape(b, h, nc, L, dk)
    kf = k.astype(f32).reshape(b, h, nc, L, dk)
    vf = v.astype(f32).reshape(b, h, nc, L, dv)
    bf = beta.astype(f32).reshape(b, h, nc, L)
    gc = jnp.cumsum(g.astype(f32).reshape(b, h, nc, L), axis=-1)
    incl = jnp.tril(jnp.ones((L, L), bool))
    strict = jnp.tril(jnp.ones((L, L), bool), -1)
    diff = gc[..., :, None] - gc[..., None, :]
    dec = jnp.where(incl, jnp.exp(jnp.where(incl, diff, 0.0)), 0.0)
    kk = jnp.einsum('bhcid,bhcjd->bhcij', kf, kf)
    a_mat = jnp.where(strict, bf[..., :, None] * dec * kk, 0.0)
    eye = jnp.eye(L, dtype=f32)
    t_inv = lax.linalg.triangular_solve(eye + a_mat, jnp.broadcast_to(eye, a_mat.shape),
                                        left_side=True, lower=True, unit_diagonal=True)
    w_v = jnp.einsum('bhcij,bhcjv->bhciv', t_inv, bf[..., None] * vf)
    w_k = jnp.einsum('bhcij,bhcjd->bhcid', t_inv, (bf * jnp.exp(gc))[..., None] * kf)
    qk = jnp.einsum('bhcid,bhcjd->bhcij', qf, kf) * dec
    q_dec = qf * jnp.exp(gc)[..., None]
    k_end = kf * jnp.exp(gc[..., -1:] - gc)[..., None]
    g_last = jnp.exp(gc[..., -1])

    def step(s, xs):
        qd, qkc, wv, wk, ke, gl = xs
        u = wv - jnp.einsum('bhid,bhdv->bhiv', wk, s)
        o = jnp.einsum('bhid,bhdv->bhiv', qd, s) + jnp.einsum('bhij,bhjv->bhiv', qkc, u)
        s = gl[..., None, None] * s + jnp.einsum('bhjd,bhjv->bhdv', ke, u)
        return s, o

    xs = tuple(jnp.moveaxis(t, 2, 0) for t in (q_dec, qk, w_v, w_k, k_end, g_last))
    s_fin, o = lax.scan(step, s0.astype(f32), xs)
    o = jnp.moveaxis(o, 0, 2).reshape(b, h, n, dv)
    return o.astype(v.dtype), s_fin.astype(s0.dtype)

def _ctx_attention(q, k, v, sink):
    b, h, s, d = q.shape
    kvh = k.shape[1]
    g = h // kvh
    nqb = s // CTX_BLOCK
    scale = d ** -0.5
    qb = jnp.moveaxis(q.reshape(b, kvh, g, nqb, CTX_BLOCK, d), 3, 0)

    def block(qi):
        logits = jnp.einsum('bkgqd,bksd->bkgqs', qi, k).astype(jnp.float32) * scale
        if sink is not None:
            sk = jnp.broadcast_to(sink.astype(jnp.float32).reshape(1, kvh, g, 1, 1), logits.shape[:-1] + (1,))
            logits = jnp.concatenate([logits, sk], axis=-1)
        p = jax.nn.softmax(logits, axis=-1)[..., :s].astype(v.dtype)
        return jnp.einsum('bkgqs,bksd->bkgqd', p, v)

    out = lax.map(block, qb)
    return jnp.moveaxis(out, 0, 3).reshape(b, h, s, d)

def _swa_latent(q, k, v, ck, cv, sink):
    b, h, n, d = q.shape
    kvh = k.shape[1]
    g = h // kvh
    nb = n // SWA_BLOCK
    span = SWA_BLOCK + 2 * SWA_WINDOW
    scale = d ** -0.5
    qg = q.reshape(b, kvh, g, n, d)
    pad = ((0, 0), (0, 0), (SWA_WINDOW, SWA_WINDOW), (0, 0))
    kp = jnp.pad(k, pad)
    vp = jnp.pad(v, pad)
    sk = jnp.broadcast_to(sink.astype(jnp.float32).reshape(1, kvh, g, 1, 1), (b, kvh, g, SWA_BLOCK, 1))

    def block(i):
        start = i * SWA_BLOCK
        qi = lax.dynamic_slice_in_dim(qg, start, SWA_BLOCK, axis=3)
        ki = lax.dynamic_slice_in_dim(kp, start, span, axis=2)
        vi = lax.dynamic_slice_in_dim(vp, start, span, axis=2)
        qpos = start + jnp.arange(SWA_BLOCK)
        kpos = start - SWA_WINDOW + jnp.arange(span)
        mask = (jnp.abs(qpos[:, None] - kpos[None, :]) <= SWA_WINDOW) & (kpos[None, :] >= 0) & (kpos[None, :] < n)
        l_loc = jnp.where(mask, jnp.einsum('bkgqd,bksd->bkgqs', qi, ki).astype(jnp.float32) * scale, NEG_INF)
        l_ctx = jnp.einsum('bkgqd,bkpd->bkgqp', qi, ck).astype(jnp.float32) * scale
        p = jax.nn.softmax(jnp.concatenate([l_loc, l_ctx, sk], axis=-1), axis=-1).astype(v.dtype)
        return (jnp.einsum('bkgqs,bksd->bkgqd', p[..., :span], vi)
                + jnp.einsum('bkgqp,bkpd->bkgqd', p[..., span:-1], cv))

    out = lax.map(block, jnp.arange(nb))
    return out.transpose(1, 2, 3, 0, 4, 5).reshape(b, h, n, d)

def _na_latent(q, k, v, ck, cv, rpb):
    b, h, n, d = q.shape
    rows = n // GRID_W
    kh = min(NA_KH, rows)
    scale = d ** -0.5
    qg = q.reshape(b, h, rows, GRID_W, d)
    kg = k.reshape(b, h, rows, GRID_W, d)
    vg = v.reshape(b, h, rows, GRID_W, d)
    col = jnp.arange(GRID_W)
    cs = jnp.clip(col - NA_KW // 2, 0, GRID_W - NA_KW)
    col_mask = (col[None, :] >= cs[:, None]) & (col[None, :] < cs[:, None] + NA_KW)
    dc = jnp.clip(col[None, :] - col[:, None], -(NA_KW - 1), NA_KW - 1) + NA_KW - 1
    rpb_c = rpb.astype(jnp.float32)[:, :, dc]
    nloc = kh * GRID_W

    def row(r):
        rs = jnp.clip(r - kh // 2, 0, rows - kh)
        qr = lax.dynamic_index_in_dim(qg, r, axis=2, keepdims=False)
        kr = lax.dynamic_slice_in_dim(kg, rs, kh, axis=2)
        vr = lax.dynamic_slice_in_dim(vg, rs, kh, axis=2)
        dr = rs + jnp.arange(kh) - r + NA_KH - 1
        bias = jnp.take(rpb_c, dr, axis=1).transpose(0, 2, 1, 3)
        l_loc = jnp.einsum('bhqd,bhrkd->bhqrk', qr, kr).astype(jnp.float32) * scale + bias[None]
        l_loc = jnp.where(col_mask[:, None, :], l_loc, NEG_INF).reshape(b, h, GRID_W, nloc)
        l_ctx = jnp.einsum('bhqd,bhpd->bhqp', qr, ck).astype(jnp.float32) * scale
        p = jax.nn.softmax(jnp.concatenate([l_loc, l_ctx], axis=-1), axis=-1).astype(v.dtype)
        p_loc = p[..., :nloc].reshape(b, h, GRID_W, kh, GRID_W)
        return (jnp.einsum('bhqrk,bhrkd->bhqd', p_loc, vr)
                + jnp.einsum('bhqp,bhpd->bhqd', p[..., nloc:], cv))

    out = lax.map(row, jnp.arange(rows))
    return out.transpose(1, 2, 0, 3, 4).reshape(b, h, n, d)

def _decay(a, alog, dtb):
    g = -jnp.exp(alog.astype(jnp.float32)) * jax.nn.softplus(a.astype(jnp.float32) + dtb.astype(jnp.float32))
    return g.transpose(0, 2, 1)

def _token_mixers(h, p, cache):
    b, n, _ = h.shape
    latent = cache is not None
    (a_q, a_k, a_v, a_r, a_lf, a_lb,
     s_q, s_k, s_v,
     n_q, n_k, n_v,
     d_q, d_k, d_v, d_r, d_af, d_ab, d_bf, d_bb) = _split(h @ p['w_in'], IN_SPLITS)

    q, k, v = _heads(a_q, GLA_HEADS), _heads(a_k, GLA_HEADS), _heads(a_v, GLA_HEADS)
    la_f = _heads(jax.nn.log_sigmoid(a_lf @ p['gla_wup'][0] + p['gla_bup'][0]) / GLA_TAU, GLA_HEADS)
    la_b = _heads(jax.nn.log_sigmoid(a_lb @ p['gla_wup'][1] + p['gla_bup'][1]) / GLA_TAU, GLA_HEADS)
    s0 = cache['gla'] if latent else jnp.zeros((b, 2, GLA_HEADS, HEAD_DIM, HEAD_DIM), h.dtype)
    o_f, sa_f = _gla_chunked(q, k, v, la_f, s0[:, 0])
    o_b, sa_b = _gla_chunked(_flip(q), _flip(k), _flip(v), _flip(la_b), s0[:, 1])
    out_a = _rmsnorm(o_f + _flip(o_b), p['gla_onorm']) * jax.nn.silu(_heads(a_r, GLA_HEADS))

    q = _rmsnorm(_heads(s_q, SWA_HEADS), p['swa_qnorm'])
    swa_k = _rmsnorm(_heads(s_k, SWA_KV_HEADS), p['swa_knorm'])
    swa_v = _heads(s_v, SWA_KV_HEADS)
    if latent:
        out_b = _swa_latent(_rope_2d(q), _rope_2d(swa_k), swa_v, cache['swa_k'], cache['swa_v'], p['swa_sink'])
    else:
        out_b = _ctx_attention(q, swa_k, swa_v, p['swa_sink'])

    q = _rmsnorm(_heads(n_q, NA_HEADS), p['na_qnorm'])
    na_k = _rmsnorm(_heads(n_k, NA_HEADS), p['na_knorm'])
    na_v = _heads(n_v, NA_HEADS)
    if latent:
        out_c = _na_latent(q, na_k, na_v, cache['na_k'], cache['na_v'], p['na_rpb'])
    else:
        out_c = _ctx_attention(q, na_k, na_v, None)

    qkv = jax.nn.silu(_dwconv(jnp.concatenate([d_q, d_k, d_v], axis=-1), p['gdn_conv']))
    q, k, v = jnp.split(qkv, 3, axis=-1)
    q = _l2norm(_heads(q, GDN_HEADS)) * (HEAD_DIM ** -0.5)
    k = _l2norm(_heads(k, GDN_HEADS))
    v = _heads(v, GDN_HEADS)
    g_f = _decay(d_af, p['gdn_alog'][0], p['gdn_dtbias'][0])
    g_b = _decay(d_ab, p['gdn_alog'][1], p['gdn_dtbias'][1])
    beta_f = jax.nn.sigmoid(d_bf.astype(jnp.float32)).transpose(0, 2, 1)
    beta_b = jax.nn.sigmoid(d_bb.astype(jnp.float32)).transpose(0, 2, 1)
    s0 = cache['gdn'] if latent else jnp.zeros((b, 2, GDN_HEADS, HEAD_DIM, HEAD_DIM), h.dtype)
    o_f, sd_f = _gdn_chunked(q, k, v, g_f, beta_f, s0[:, 0])
    o_b, sd_b = _gdn_chunked(_flip(q), _flip(k), _flip(v), _flip(g_b), _flip(beta_b), s0[:, 1])
    out_d = _rmsnorm(o_f + _flip(o_b), p['gdn_onorm']) * jax.nn.silu(_heads(d_r, GDN_HEADS))

    y = jnp.concatenate([_merge(out_a), _merge(out_b), _merge(out_c), _merge(out_d)], axis=-1) @ p['w_out']
    if latent:
        return y, None
    return y, (swa_k, swa_v, na_k, na_v, jnp.stack([sa_f, sa_b], axis=1), jnp.stack([sd_f, sd_b], axis=1))

def _swiglu(h, w1, w3, w2):
    return (jax.nn.silu(h @ w1) * (h @ w3)) @ w2

def _moe(h, router, w1, w3, w2):
    logits = (h @ router).astype(jnp.float32)
    top_v, top_i = lax.top_k(logits, TOP_K)
    top_w = jax.nn.softmax(top_v, axis=-1)
    gates = jnp.sum(jax.nn.one_hot(top_i, N_EXPERTS, dtype=jnp.float32) * top_w[..., None], axis=-2)
    out = jnp.zeros_like(h)
    for e in range(N_EXPERTS):
        out = out + gates[..., e:e + 1].astype(h.dtype) * _swiglu(h, w1[e], w3[e], w2[e])
    return out

def _modulation(cvec, w, b):
    return (jax.nn.silu(cvec) @ w + b)[:, None, :]

def _layer(x, mod, p, cache, ffn):
    sh1, sc1, g1, sh2, sc2, g2 = jnp.split(mod, 6, axis=-1)
    y, ctx_state = _token_mixers(_rmsnorm(x, p['norm1']) * (1 + sc1) + sh1, p, cache)
    x = x + g1 * y
    x = x + g2 * ffn(_rmsnorm(x, p['norm2']) * (1 + sc2) + sh2)
    return x, ctx_state

def setup_inputs(seed: int = 0) -> dict:
    key = jax.random.key(seed)
    keys = iter(jax.random.split(key, 48))
    f32 = jnp.float32

    def nrm(shape, scale=1.0):
        return jax.random.normal(next(keys), shape, f32) * scale

    def gain(shape):
        return 1.0 + nrm(shape, 0.02)

    lo, hi = math.log(1e-3), math.log(1e-1)
    dt = jnp.exp(jax.random.uniform(next(keys), (DEPTH, 2, GDN_HEADS), f32) * (hi - lo) + lo)
    return {
        'x_prompt': nrm((BATCH, SEQ, D_MODEL)),
        'x_sample': nrm((DEC_BATCH, DEC_SEQ, D_MODEL)),
        'cache_swa_k': nrm((DEC_BATCH, DEPTH, SWA_KV_HEADS, PAST_LEN, HEAD_DIM)),
        'cache_swa_v': nrm((DEC_BATCH, DEPTH, SWA_KV_HEADS, PAST_LEN, HEAD_DIM)),
        'cache_na_k': nrm((DEC_BATCH, DEPTH, NA_HEADS, PAST_LEN, HEAD_DIM)),
        'cache_na_v': nrm((DEC_BATCH, DEPTH, NA_HEADS, PAST_LEN, HEAD_DIM)),
        'state_gla': nrm((DEC_BATCH, DEPTH, 2, GLA_HEADS, HEAD_DIM, HEAD_DIM), 0.3),
        'state_gdn': nrm((DEC_BATCH, DEPTH, 2, GDN_HEADS, HEAD_DIM, HEAD_DIM), 0.1),
        'c': nrm((DEC_BATCH, D_MODEL)),
        'c_ctx': nrm((D_MODEL,)),
        'w_mod': nrm((DEPTH, D_MODEL, 6 * D_MODEL), 0.5 * D_MODEL ** -0.5),
        'b_mod': nrm((DEPTH, 6 * D_MODEL), 0.02),
        'norm1_g': gain((DEPTH, D_MODEL)),
        'norm2_g': gain((DEPTH, D_MODEL)),
        'w_in': nrm((DEPTH, D_MODEL, IN_COLS), D_MODEL ** -0.5),
        'w_out': nrm((DEPTH, MIX_WIDTH, D_MODEL), MIX_WIDTH ** -0.5),
        'gla_wup': nrm((DEPTH, 2, GLA_LOWRANK, GROUP_WIDTH), GLA_LOWRANK ** -0.5),
        'gla_bup': nrm((DEPTH, 2, GROUP_WIDTH), 0.1),
        'gla_onorm': gain((DEPTH, HEAD_DIM)),
        'swa_qnorm': gain((DEPTH, HEAD_DIM)),
        'swa_knorm': gain((DEPTH, HEAD_DIM)),
        'swa_sink': nrm((DEPTH, SWA_HEADS), 0.5),
        'na_qnorm': gain((DEPTH, HEAD_DIM)),
        'na_knorm': gain((DEPTH, HEAD_DIM)),
        'na_rpb': nrm((DEPTH, NA_HEADS, 2 * NA_KH - 1, 2 * NA_KW - 1), 0.2),
        'gdn_conv': nrm((DEPTH, GDN_CONV, 3 * GROUP_WIDTH), GDN_CONV ** -0.5),
        'gdn_alog': jnp.log(jax.random.uniform(next(keys), (DEPTH, 2, GDN_HEADS), f32, 1.0, 16.0)),
        'gdn_dtbias': dt + jnp.log(-jnp.expm1(-dt)),
        'gdn_onorm': gain((DEPTH, HEAD_DIM)),
        'ffn_w1': nrm((N_DENSE, D_MODEL, D_FF), D_MODEL ** -0.5),
        'ffn_w3': nrm((N_DENSE, D_MODEL, D_FF), D_MODEL ** -0.5),
        'ffn_w2': nrm((N_DENSE, D_FF, D_MODEL), D_FF ** -0.5),
        'moe_router': nrm((N_MOE, D_MODEL, N_EXPERTS), D_MODEL ** -0.5),
        'moe_w1': nrm((N_MOE, N_EXPERTS, D_MODEL, D_FF_EXPERT), D_MODEL ** -0.5),
        'moe_w3': nrm((N_MOE, N_EXPERTS, D_MODEL, D_FF_EXPERT), D_MODEL ** -0.5),
        'moe_w2': nrm((N_MOE, N_EXPERTS, D_FF_EXPERT, D_MODEL), D_FF_EXPERT ** -0.5),
    }

def reference(x_prompt, x_sample, cache_swa_k, cache_swa_v, cache_na_k, cache_na_v, state_gla, state_gdn,
              c, c_ctx, w_mod, b_mod, norm1_g, norm2_g, w_in, w_out, gla_wup, gla_bup, gla_onorm,
              swa_qnorm, swa_knorm, swa_sink, na_qnorm, na_knorm, na_rpb, gdn_conv, gdn_alog, gdn_dtbias,
              gdn_onorm, ffn_w1, ffn_w3, ffn_w2, moe_router, moe_w1, moe_w3, moe_w2):
    xp, xs = x_prompt, x_sample
    l_swa_k, l_swa_v, l_na_k, l_na_v, l_gla, l_gdn = [], [], [], [], [], []
    for l in range(DEPTH):
        p = {'norm1': norm1_g[l], 'norm2': norm2_g[l], 'w_in': w_in[l], 'w_out': w_out[l],
             'gla_wup': gla_wup[l], 'gla_bup': gla_bup[l], 'gla_onorm': gla_onorm[l],
             'swa_qnorm': swa_qnorm[l], 'swa_knorm': swa_knorm[l], 'swa_sink': swa_sink[l],
             'na_qnorm': na_qnorm[l], 'na_knorm': na_knorm[l], 'na_rpb': na_rpb[l],
             'gdn_conv': gdn_conv[l], 'gdn_alog': gdn_alog[l], 'gdn_dtbias': gdn_dtbias[l],
             'gdn_onorm': gdn_onorm[l]}
        if l % 2 == 0:
            ffn = functools.partial(_swiglu, w1=ffn_w1[l // 2], w3=ffn_w3[l // 2], w2=ffn_w2[l // 2])
        else:
            ffn = functools.partial(_moe, router=moe_router[l // 2], w1=moe_w1[l // 2],
                                    w3=moe_w3[l // 2], w2=moe_w2[l // 2])
        cache = {'swa_k': cache_swa_k[:, l], 'swa_v': cache_swa_v[:, l],
                 'na_k': cache_na_k[:, l], 'na_v': cache_na_v[:, l],
                 'gla': state_gla[:, l], 'gdn': state_gdn[:, l]}
        xp, st = _layer(xp, _modulation(c_ctx[None, :], w_mod[l], b_mod[l]), p, None, ffn)
        xs, _ = _layer(xs, _modulation(c, w_mod[l], b_mod[l]), p, cache, ffn)
        for lst, t in zip((l_swa_k, l_swa_v, l_na_k, l_na_v, l_gla, l_gdn), st):
            lst.append(t)
    new_swa_k = jnp.stack(l_swa_k, axis=1)
    new_swa_v = jnp.stack(l_swa_v, axis=1)
    new_na_k = jnp.stack(l_na_k, axis=1)
    new_na_v = jnp.stack(l_na_v, axis=1)
    new_gla = jnp.stack(l_gla, axis=1)
    new_gdn = jnp.stack(l_gdn, axis=1)
    return (xp, xs, new_swa_k, new_swa_v, new_na_k, new_na_v, new_gla, new_gdn)


_drawn_inputs = setup_inputs


def setup_inputs(seed=0):
    import zlib

    import numpy as np

    out = dict(_drawn_inputs(seed))
    spreads = {}
    factors = {'cache_swa_k': 4.442,
     'cache_swa_v': 4.244,
     'cache_na_k': 3.966,
     'cache_na_v': 3.125,
     'state_gla': 8.0,
     'state_gdn': 3.775,
     'norm2_g': 4.302,
     'gla_onorm': 8.0,
     'swa_qnorm': 8.0,
     'swa_knorm': 2.805,
     'swa_sink': 8.0,
     'na_qnorm': 8.0,
     'na_knorm': 7.954,
     'na_rpb': 8.0,
     'gdn_onorm': 8.0}
    for name, (base, spread) in spreads.items():
        noise = np.random.default_rng([zlib.crc32(name.encode()), seed]).standard_normal(out[name].shape)
        drawn = base * np.exp(spread * noise) if base else spread * noise
        out[name] = __import__('jax').numpy.asarray(drawn.astype(out[name].dtype))
    for name, factor in factors.items():
        out[name] = (out[name] * factor).astype(out[name].dtype)
    return out
```

```python
from contextlib import ExitStack

import numpy as np

import concourse.bass as bass
from concourse import mybir

F32 = mybir.dt.float32
BF16 = mybir.dt.bfloat16
ALU = mybir.AluOpType
ACT = mybir.ActivationFunctionType
AX = mybir.AxisListType

P = 128
D = 1024
KT = D // P
NP_TOK, NS_TOK = 128, 512
T = NP_TOK + NS_TOK
STREAMS = ((0, NP_TOK), (NP_TOK, T))
PIECES = ((0, 512), (512, T))
DEPTH = 2
L = 64
PAST = 256
EPS = 1e-6
NEG = -1e30
FF = 2816
NE = 8
WCOL = 256
SLOT = KT * WCOL
NSLOT = 4
N_MOD, N_IN, N_OUT = 6 * D // WCOL, 12, D // WCOL
DENSE_ITEMS = FF // WCOL
EXPERT_ITEMS = 4
V_COLS = 384

AQ, AK, AV, AR, SQ, SK, NQ, NK, DQ, DK, DV, DR, SMALL = 0, 2, 4, 6, 8, 10, 11, 13, 15, 17, 19, 21, 23
NBLK = 24
R_BETA, R_DEC = 32, (64, 96)

C_N1, C_N2, C_BMOD, C_BUP, C_AON, C_SQN, C_SKN, C_SINK, C_NQN, C_NKN, C_CONV, C_ALOG, C_DTB, C_DON, C_EPS, C_ONE, \
    C_ZERO = 0, 8, 16, 64, 68, 69, 70, 71, 75, 76, 77, 95, 96, 97, 98, 99, 100
NPAR = 101
OA, OB, OC, OD = 0, 2, 4, 6


def build(nc, A):
    with ExitStack() as ctx:
        def sb(name, shape, dt=F32):
            return ctx.enter_context(nc.sbuf_tensor(name, shape, dt))

        def sem(name):
            return ctx.enter_context(nc.semaphore(name))

        xT = sb("xT", [P, KT, T])
        hT = sb("hT", [P, KT, T])
        pj = sb("pj", [P, NBLK, T])
        vtok = sb("vtok", [P, 5, V_COLS])
        scan = sb("scan", [P, 8, T])
        ring = sb("ring", [P, NSLOT, SLOT])
        work = sb("work", [P, 20, 256])
        ident = sb("ident", [P, P])
        ones = sb("ones", [P, P])
        blk = sb("blk", [P, P])
        sel = sb("sel", [P, 4, P])
        rot = sb("rot", [P, P])
        cmask = sb("cmask", [P, 2, T], BF16)
        incl = sb("incl", [P, 2, 2, L], BF16)
        lvl = sb("lvl", [P, 6, 2, 2, L], BF16)
        swamask = sb("swamask", [P, 3 * P])
        nmask = sb("nmask", [P, 2, L])
        ck = sb("ck", [P, 3, PAST])
        cv = sb("cv", [P, 2, V_COLS])
        st_a = [sb(f"st_a{s}", [P, 2, 2, L]) for s in range(2)]
        st_d = [sb(f"st_d{s}", [P, 2, 2, L]) for s in range(2)]
        par = sb("par", [P, DEPTH, NPAR])
        wup = sb("wup", [32, DEPTH, 4, P])
        cT = sb("cT", [P, KT, 2])
        cE = sb("cE", [P, KT, 2])
        mod = sb("mod", [P, 48, 2])
        s1 = sb("s1", [P, 2, KT, 2])
        cols = sb("cols", [P, 32])
        att = sb("att", [P, 16])
        rt = sb("rt", [P, KT, NE])
        tri = sb("tri", [P, NE, NE], BF16)
        ps = ctx.enter_context(nc.psum_tensor("ps", [P, 8 * 512], F32))

        cossin = scan[:, 6:8, 0:NS_TOK]
        wk = work[:, :, :].rearrange("p a b -> p (a b)")
        scr = scan[:, :, :].rearrange("p a b -> p (a b)")
        rpb = pj[:, 0:8, :].rearrange("p a b -> p (a b)")[:, 0:4 * 16 * L].rearrange(
            "p (h m c) -> p h m c", h=4, m=16)

        def tmp(n):
            return wk[:, n * T:(n + 1) * T]

        def pair(n):
            return ps[:, (n % 4) * 1024:(n % 4) * 1024 + T]

        def bank(n, w=512):
            return ps[:, n * 512:n * 512 + w]

        def slot3(n):
            return ring[:, n % NSLOT, :].rearrange("p (k c) -> p k c", k=KT)

        def slot2(n):
            return ring[:, n % NSLOT, :].rearrange("p (c n) -> p c n", c=2)

        consts_loaded = sem("consts_loaded")
        w_loaded = [sem(f"w_loaded{i}") for i in range(NSLOT)]
        w_used = sem("w_used")
        meeting = sem("meeting")
        names = """silu_c ssq_in ssq_out rstd_ready normed_v prod_ready prod_free_v prod_free_a
            hn_sq hn_sum hn_r gla_exp gla_staged gla_prod gla_evac_v gla_evac_a gla_out gla_done
            conv_ready conv_exp gdn_staged_v gdn_staged_a gdn_dif gdn_prod gdn_at gdn_u gdn_us
            gdn_x gdn_xs gdn_r0 gdn_tok gdn_rs gdn_u1 gdn_us1 gdn_o gdn_done gate_exp rope_ready rope_out
            sc_ready lg_ready p_ready pn_ready pt_ready pt_copied pv_ready pv_free mixer_a_done mixer_d_done
            rpb_loaded out_ready out_free f_ready f_free f_exp hid_ready out_stored states_out new_kv final_x
            cache_in attn_done""".split()
        S = {n: sem(n) for n in names}

        block = ctx.enter_context(nc.Block())
        met = {"pe": 0, "dve": 0, "act": 0}

        def meet(who, eng):
            met[who] += 1
            eng.drain().then_inc(meeting, 1)
            eng.wait_ge(meeting, 3 * met[who])

        base_mod = [0, 0]
        base_in, base_out, base_ffn = [0, 0], [0, 0], [0, 0]
        n = 0
        for l in range(DEPTH):
            base_mod[l] = n
            n += N_MOD
            base_in[l] = n
            n += N_IN + 2
            base_out[l] = n
            n += N_OUT
            base_ffn[l] = n
            n += 3 * (DENSE_ITEMS if l == 0 else EXPERT_ITEMS * NE)

        def uses(n):
            return n // NSLOT + 1

        @block.sync
        def _(sp):
            def load(n, src, width=None, shift=0):
                if isinstance(shift, int) and shift == 0 and n < NSLOT:
                    pass
                else:
                    sp.wait_ge(w_used, shift + (n - NSLOT + 1))
                dst = ring[:, n % NSLOT, :] if width is None else slot3(n)[:, :, 0:width]
                sp.dma_start(dst, src).then_inc(w_loaded[n % NSLOT], 16)

            consts = [(ident, "ident"), (ones, "ones"), (blk, "blk"), (rot, "rot"), (sel, "sel"),
                      (cmask, "cmask"), (incl, "incl"), (lvl, "lvl"), (swamask, "swamask"), (nmask, "nmask"),
                      (par, "par"), (wup, "wup"), (cT, "cT"), (rt, "router"), (tri, "tri"), (xT, "xT")]
            for dst, name in consts:
                sp.dma_start(dst[:], A[name]).then_inc(consts_loaded, 16)
            for l in range(DEPTH):
                for j in range(N_MOD):
                    load(base_mod[l] + j, A["wmod"][l, j])
                for j in range(N_IN):
                    load(base_in[l] + j, A["win"][l, j])
                for j in range(2):
                    load(base_in[l] + N_IN + j, A["wv"][l, :, :, j * WCOL:min((j + 1) * WCOL, V_COLS)],
                         min(WCOL, V_COLS - j * WCOL))
                for j in range(N_OUT):
                    load(base_out[l] + j, A["wout"][l, j])
                b = base_ffn[l]
                if l == 0:
                    load(b, A["d1"][0])
                    load(b + 1, A["d3"][0])
                    b += 2
                    for i in range(DENSE_ITEMS):
                        if i + 1 < DENSE_ITEMS:
                            load(b, A["d1"][i + 1])
                            load(b + 1, A["d3"][i + 1])
                            b += 2
                        load(b, A["d2"][i])
                        b += 1
                else:
                    load(b, A["e1"][0])
                    load(b + 1, A["e3"][0])
                    b += 2
                    with sp.Fori(0, NE - 1) as e:
                        for j in range(EXPERT_ITEMS):
                            it = e * EXPERT_ITEMS + j
                            load(b + 3 * j, A["e1"][bass.ds(it + 1, 1)].rearrange("a p n -> p (a n)"), None, e * 12)
                            load(b + 3 * j + 1, A["e3"][bass.ds(it + 1, 1)].rearrange("a p n -> p (a n)"), None, e * 12)
                            load(b + 3 * j + 2, A["e2"][bass.ds(it, 1)].rearrange("a p n -> p (a n)"), None, e * 12)
                    b += 12 * (NE - 1)
                    for i in range(EXPERT_ITEMS * (NE - 1), EXPERT_ITEMS * NE):
                        if i + 1 < EXPERT_ITEMS * NE:
                            load(b, A["e1"][i + 1])
                            load(b + 1, A["e3"][i + 1])
                            b += 2
                        load(b, A["e2"][i])
                        b += 1

        @block.gpsimd
        def _(pool):
            for l in range(DEPTH):
                if l > 0:
                    pool.wait_ge(S["attn_done"], l)
                pool.dma_start(cossin, A["cossin"]).then_inc(S["cache_in"], 16)
                for dst, name in ((ck, "ck"), (cv, "cv"), (st_a[1], "sta"), (st_d[1], "std")):
                    pool.dma_start(dst[:], A[name][l]).then_inc(S["cache_in"], 16)
                pool.wait_ge(S["mixer_a_done"], l + 1)
                pool.dma_start(rpb.rearrange("p h m c -> p (h m c)"), A["rpb"][l]).then_inc(S["rpb_loaded"], 16)
                pool.dma_start(A["new_sta"][l], st_a[0][:]).then_inc(S["states_out"], 16)
                pool.wait_ge(S["new_kv"], l + 1)
                pool.dma_start(A["new_k"][l], pj[:, SK, 0:NP_TOK]).then_inc(S["states_out"], 16)
                pool.dma_start(A["new_nk"][l], pj[:, NK:NK + 2, 0:NP_TOK]).then_inc(S["states_out"], 16)
                pool.dma_start(A["new_v"][l], vtok[:, 0, :]).then_inc(S["states_out"], 16)
                pool.wait_ge(S["mixer_d_done"], l + 1)
                pool.dma_start(A["new_std"][l], st_d[0][:]).then_inc(S["states_out"], 16)
            pool.wait_ge(S["final_x"], 1)
            pool.dma_start(A["yT"], xT[:]).then_inc(S["out_stored"], 16)
            pool.wait_ge(S["out_stored"], 16)
            pool.wait_ge(S["states_out"], 80 * DEPTH)

        def mod_pe(pe, l):
            pe.wait_ge(S["silu_c"], 1)
            for j in range(N_MOD):
                pe.wait_ge(w_loaded[(base_mod[l] + j) % NSLOT], 16 * uses(base_mod[l] + j))
                w = slot3(base_mod[l] + j)
                for m in range(WCOL // P):
                    b = j * (WCOL // P) + m
                    for k in range(KT):
                        mm = nc.tensor.matmul(ps[:, 2 * b:2 * b + 2], w[:, k, m * P:(m + 1) * P], cT[:, k, :],
                                              start=(k == 0), stop=(k == KT - 1))
                mm.then_inc(w_used, 1)
            meet("pe", pe)
            meet("pe", pe)

        def mod_dve(dve, l):
            meet("dve", dve)
            nc.vector.tensor_tensor(mod[:, :, :], ps[:, 0:96].rearrange("p (b s) -> p b s", s=2),
                                    par[:, l, C_BMOD:C_BMOD + 48].unsqueeze(2).to_broadcast([P, 48, 2]), ALU.add)
            dve.drain()
            for w, c in ((0, C_N1), (1, C_N2)):
                nc.vector.scalar_tensor_tensor(s1[:, w], mod[:, 24 * w + 8:24 * w + 16, :], 1.0,
                                               par[:, l, c:c + 8].unsqueeze(2).to_broadcast([P, 8, 2]),
                                               ALU.add, ALU.mult)
            meet("dve", dve)

        def mod_act(act, l):
            meet("act", act)
            meet("act", act)

        def norm_dve(dve, call):
            w = call % 2
            nc.vector.tensor_tensor(hT[:, :, :], xT[:, :, :], xT[:, :, :], ALU.mult).then_inc(S["ssq_in"], 1)
            dve.wait_ge(S["rstd_ready"], call + 1)
            nc.vector.tensor_tensor(hT[:, :, :], xT[:, :, :], tmp(0).unsqueeze(1).to_broadcast([P, KT, T]),
                                    ALU.mult).then_inc(S["normed_v"], 1)
            dve.wait_ge(S["normed_v"], call + 1)
            for k in range(0, KT, 2):
                for s, (a, b) in enumerate(STREAMS):
                    nc.vector.tensor_scalar(hT[:, k, a:b], hT[:, k, a:b], s1[:, w, k, s:s + 1],
                                            mod[:, 24 * w + k, s:s + 1], ALU.mult, ALU.add)
            meet("dve", dve)

        def norm_pe(pe, call):
            pe.wait_ge(S["ssq_in"], call + 1)
            for a, b in PIECES:
                for k in range(KT):
                    mm = nc.tensor.matmul(pair(0)[:, a:b], ones[:, :], hT[:, k, a:b],
                                          start=(k == 0), stop=(k == KT - 1))
            mm.then_inc(S["ssq_out"], 1)
            meet("pe", pe)

        def norm_act(act, call, l):
            w = call % 2
            act.wait_ge(S["ssq_out"], call + 1)
            nc.scalar.activation(tmp(1), pair(0), ACT.Ln, bias=par[:, l, C_EPS:C_EPS + 1], scale=1.0 / D)
            act.drain()
            nc.scalar.activation(tmp(0), tmp(1), ACT.Exp, bias=par[:, l, C_ZERO:C_ZERO + 1],
                                 scale=-0.5).then_inc(S["rstd_ready"], 1)
            act.wait_ge(S["normed_v"], call + 1)
            for k in range(1, KT, 2):
                for s, (a, b) in enumerate(STREAMS):
                    nc.scalar.activation(hT[:, k, a:b], hT[:, k, a:b], ACT.Identity,
                                         bias=mod[:, 24 * w + k, s:s + 1], scale=s1[:, w, k, s:s + 1])
            meet("act", act)

        N_PROD = NBLK + 5

        def in_pe(pe, l):
            for j in range(N_PROD):
                if j >= 4:
                    free = S["prod_free_v"] if j % 2 == 0 else S["prod_free_a"]
                    per = (N_PROD + 1) // 2 if j % 2 == 0 else N_PROD // 2
                    pe.wait_ge(free, l * per + (j - 4) // 2 + 1)
                if j < NBLK:
                    n, m = base_in[l] + j // 2, j % 2
                    pe.wait_ge(w_loaded[n % NSLOT], 16 * uses(n))
                    for a, b in PIECES:
                        for k in range(KT):
                            mm = nc.tensor.matmul(pair(j)[:, a:b], slot3(n)[:, k, m * P:(m + 1) * P], hT[:, k, a:b],
                                                  start=(k == 0), stop=(k == KT - 1))
                    mm.then_inc(S["prod_ready"], 1)
                    if m == 1:
                        pe.wait_ge(S["prod_ready"], l * N_PROD + j + 1)
                        pe.sem_inc(w_used, 1)
                else:
                    t = j - NBLK
                    for h, (c0, c1) in enumerate(((0, WCOL), (WCOL, V_COLS))):
                        n = base_in[l] + N_IN + h
                        pe.wait_ge(w_loaded[n % NSLOT], 16 * uses(n))
                        for k in range(KT):
                            mm = nc.tensor.matmul(pair(j)[:, c0:c1], hT[:, k, t * P:(t + 1) * P],
                                                  slot3(n)[:, k, 0:c1 - c0], start=(k == 0), stop=(k == KT - 1))
                    mm.then_inc(S["prod_ready"], 1)
            pe.wait_ge(S["prod_ready"], (l + 1) * N_PROD)
            pe.sem_inc(w_used, 2)
            meet("pe", pe)

        def in_evac(who, eng, l):
            for j in range(0 if who == "dve" else 1, N_PROD, 2):
                eng.wait_ge(S["prod_ready"], l * N_PROD + j + 1)
                src = pair(j) if j < NBLK else pair(j)[:, 0:V_COLS]
                dst = pj[:, j, :] if j < NBLK else vtok[:, j - NBLK, :]
                if who == "dve":
                    nc.vector.tensor_copy(dst, src).then_inc(S["prod_free_v"], 1)
                else:
                    nc.scalar.copy(dst, src).then_inc(S["prod_free_a"], 1)
            meet(who, eng)

        hn = {"pe": 0, "dve": 0, "act": 0}

        def head_norm_dve(dve, x, nb, finish):
            hn["dve"] += 1
            nc.vector.tensor_tensor(wk[:, 0:nb * T].rearrange("p (b t) -> p b t", b=nb), x, x,
                                    ALU.mult).then_inc(S["hn_sq"], 1)
            dve.wait_ge(S["hn_r"], hn["dve"])
            for b in range(nb):
                finish(b, tmp(4 + b))
            dve.drain()

        def head_norm_pe(pe, nb):
            hn["pe"] += 1
            pe.wait_ge(S["hn_sq"], hn["pe"])
            for b in range(nb):
                for p0, p1 in PIECES:
                    mm = nc.tensor.matmul(pair(b)[:, p0:p1], blk[:, :], tmp(b)[:, p0:p1], start=True, stop=True)
            mm.then_inc(S["hn_sum"], 1)

        def head_norm_act(act, l, nb, div):
            hn["act"] += 1
            act.wait_ge(S["hn_sum"], hn["act"])
            for b in range(nb):
                nc.scalar.activation(tmp(4 + b), pair(b), ACT.Ln, bias=par[:, l, C_EPS:C_EPS + 1], scale=1.0 / div)
            act.drain()
            r = wk[:, 4 * T:(4 + nb) * T]
            nc.scalar.activation(r, r, ACT.Exp, bias=par[:, l, C_ZERO:C_ZERO + 1], scale=-0.5).then_inc(S["hn_r"], 1)

        def gained(x, col):
            def f(b, r):
                g = col(b)
                nc.vector.scalar_tensor_tensor(x[:, b, :], x[:, b, :], g, r, ALU.mult, ALU.mult)
            return f

        QKN = [(SQ, 3), (NQ, 4)]

        def qk_dve(dve, l):
            def pc(c):
                return par[:, l, c:c + 1]
            head_norm_dve(dve, pj[:, SQ:SQ + 3, :], 3, gained(pj[:, SQ:SQ + 3, :],
                                                              lambda b: pc(C_SQN if b < 2 else C_SKN)))
            head_norm_dve(dve, pj[:, NQ:NQ + 4, :], 4, gained(pj[:, NQ:NQ + 4, :],
                                                              lambda b: pc(C_NQN if b < 2 else C_NKN)))
            dve.drain().then_inc(S["new_kv"], 1)
            dve.drain().then_inc(S["rope_ready"], 1)
            dve.wait_ge(S["rope_out"], l + 1)
            dve.wait_ge(S["cache_in"], 80 * (l + 1))
            x = pj[:, SQ:SQ + 3, NP_TOK:T]
            r = wk[:, 0:3 * NS_TOK].rearrange("p (b t) -> p b t", b=3)
            nc.vector.tensor_tensor(r, ps[:, 0:3 * 512].rearrange("p (b t) -> p b t", b=3),
                                    cossin[:, 1, :].unsqueeze(1).to_broadcast([P, 3, NS_TOK]), ALU.mult)
            nc.vector.tensor_tensor(x, x, cossin[:, 0, :].unsqueeze(1).to_broadcast([P, 3, NS_TOK]), ALU.mult)
            dve.drain()
            nc.vector.tensor_tensor(x, x, r, ALU.add)
            meet("dve", dve)

        def qk_pe(pe, l):
            head_norm_pe(pe, 3)
            head_norm_pe(pe, 4)
            pe.wait_ge(S["rope_ready"], l + 1)
            for b in range(3):
                mm = nc.tensor.matmul(bank(b), rot[:, :], pj[:, SQ + b, NP_TOK:T], start=True, stop=True)
            mm.then_inc(S["rope_out"], 1)
            meet("pe", pe)

        def qk_act(act, l):
            head_norm_act(act, l, 3, L)
            head_norm_act(act, l, 4, L)
            meet("act", act)

        def decay_a_pe(pe, l):
            for j in range(4):
                for a, b in PIECES:
                    nc.tensor.matmul(pair(j)[:, a:b], wup[:, l, j, :], pj[0:32, SMALL, a:b], start=True, stop=True)
            meet("pe", pe)
            meet("pe", pe)
            meet("pe", pe)
            meet("pe", pe)

        def decay_a_dve(dve, l):
            meet("dve", dve)
            for j in range(4):
                bup = par[:, l, C_BUP + j:C_BUP + j + 1]
                nc.vector.tensor_scalar(scan[:, j, :], pair(j), bup, 0.0, ALU.add, ALU.min)
                nc.vector.tensor_scalar(tmp(j), pair(j), bup, None, ALU.add)
            dve.drain()
            z = wk[:, 0:4 * T]
            nc.vector.scalar_tensor_tensor(z, scr[:, 0:4 * T], 2.0, z, ALU.mult, ALU.subtract)
            meet("dve", dve)
            meet("dve", dve)
            la = wk[:, 4 * T:8 * T]
            nc.vector.tensor_tensor(la, scr[:, 0:4 * T], wk[:, 0:4 * T], ALU.subtract)
            dve.drain()
            for j in range(4):
                scan_chunks(scan[:, j, :], la[:, j * T:(j + 1) * T], j // 2)
            meet("dve", dve)

        def scan_chunks(out, data, back, p0=0, p1=P):
            m = cmask[p0:p1, back, :]
            if back:
                nc.vector.tensor_tensor_scan(out[p0:p1, ::-1], m[:, ::-1], data[p0:p1, ::-1], 0.0, ALU.mult, ALU.add)
            else:
                nc.vector.tensor_tensor_scan(out[p0:p1, :], m, data[p0:p1, :], 0.0, ALU.mult, ALU.add)

        def decay_a_act(act, l):
            meet("act", act)
            meet("act", act)
            z = wk[:, 0:4 * T]
            nc.scalar.activation(z, z, ACT.Exp, bias=par[:, l, C_ZERO:C_ZERO + 1])
            act.drain()
            nc.scalar.activation(z, z, ACT.Ln, bias=par[:, l, C_ONE:C_ONE + 1], scale=1.0)
            meet("act", act)
            meet("act", act)

        STEPS = ((0, 2), (NP_TOK, 8))

        def chunks(i, s):
            off, n = STEPS[s]
            return (i * L + off, i * (-L) + (off + (n - 1) * L))

        def w4(i):
            return work[:, i, :].rearrange("p (d g c) -> p d g c", d=2, g=2)

        def pb(b, half=0):
            return ps[:, b * 512 + 256 * half:b * 512 + 256 * half + 256].rearrange("p (d g c) -> p d g c", d=2, g=2)

        def units():
            for d in range(2):
                for g in range(2):
                    for p in range(2):
                        yield d, g, slice(64 * p, 64 * p + 64)

        A_E1, A_E2, A_QD, A_KI, A_KE, A_VS, A_AM, A_KES, A_VTOK = range(9)

        def gla_act(act, l, s, it, i):
            act.wait_ge(S["gla_done"], it + 1)
            for d, t in enumerate(chunks(i, s)):
                c = scan[:, 2 * d:2 * d + 2, bass.ds(t, L)]
                nc.scalar.activation(w4(A_E1)[:, d], c, ACT.Exp, bias=par[:, l, C_ZERO:C_ZERO + 1], scale=1.0 / 16)
                a = nc.scalar.activation(w4(A_E2)[:, d], c, ACT.Exp, bias=par[:, l, C_ZERO:C_ZERO + 1],
                                         scale=-1.0 / 16)
            a.then_inc(S["gla_exp"], 1)
            act.wait_ge(S["gla_prod"], it + 1)
            nc.scalar.copy(work[:, A_KES, :], bank(1, 256)).then_inc(S["gla_evac_a"], 1)

        def gla_dve(dve, l, s, it, i):
            ts = chunks(i, s)
            dve.wait_ge(S["gla_exp"], it + 1)
            for d, t in enumerate(ts):
                q, k, v = (pj[:, b:b + 2, bass.ds(t, L)] for b in (AQ, AK, AV))
                nc.vector.scalar_tensor_tensor(w4(A_QD)[:, d], q, L ** -0.5, w4(A_E1)[:, d], ALU.mult, ALU.mult)
                nc.vector.tensor_tensor(w4(A_KI)[:, d], k, w4(A_E2)[:, d], ALU.mult)
                nc.vector.tensor_copy(w4(A_VS)[:, d], v)
                last = L - 1 if d == 0 else 0
                nc.vector.tensor_copy(cols[:, 2 * d:2 * d + 2].unsqueeze(2), w4(A_E1)[:, d, :, last:last + 1])
            dve.drain()
            el = cols[:, 0:4].unsqueeze(2).to_broadcast([P, 4, L])
            nc.vector.tensor_tensor(work[:, A_KE, :].rearrange("p (a c) -> p a c", a=4),
                                    work[:, A_KI, :].rearrange("p (a c) -> p a c", a=4), el,
                                    ALU.mult).then_inc(S["gla_staged"], 1)
            dve.wait_ge(S["gla_prod"], it + 1)
            nc.vector.tensor_tensor(work[:, A_AM, :], bank(0, 256), incl[:].rearrange("p d g c -> p (d g c)"),
                                    ALU.mult)
            nc.vector.tensor_copy(work[:, A_VTOK, :], bank(2, 256)).then_inc(S["gla_evac_v"], 1)
            st = st_a[s][:].rearrange("p d g c -> p (d g) c")
            dve.wait_ge(S["gla_out"], it + 1)
            nc.vector.tensor_tensor(st, st, el, ALU.mult)
            for d, t in enumerate(ts):
                o = hT[:, OA:OA + 2, bass.ds(t, L)]
                nc.vector.tensor_tensor(o, o, pb(3)[:, d], ALU.add)
                dve.drain()
            nc.vector.tensor_tensor(st, st, bank(4, 256).rearrange("p (a c) -> p a c", a=4),
                                    ALU.add).then_inc(S["gla_done"], 1)
            dve.drain()

        def waited(pe):
            nc.tensor.matmul(bank(7, L), incl[:].rearrange("p d g c -> p (d g c)")[:, 0:P], incl[:, 0, 0, :],
                             start=True, stop=True)

        def gla_pe(pe, s, it):
            pe.wait_ge(S["gla_staged"], it + 1)
            waited(pe)
            for d, g, h in units():
                nc.tensor.matmul(pb(0)[h, d, g], w4(A_KI)[h, d, g], w4(A_QD)[h, d, g], start=True, stop=True)
                nc.tensor.matmul(pb(1)[h, d, g], w4(A_KE)[h, d, g], ident[h, h], start=True, stop=True)
                mm = nc.tensor.matmul(pb(2)[h, d, g], w4(A_VS)[h, d, g], ident[h, h], start=True, stop=True)
            mm.then_inc(S["gla_prod"], 1)
            pe.wait_ge(S["gla_evac_v"], it + 1)
            pe.wait_ge(S["gla_evac_a"], it + 1)
            pe.wait_ge(S["gla_done"], it + 1)
            waited(pe)
            for d, g, h in units():
                nc.tensor.matmul(pb(3)[h, d, g], w4(A_VTOK)[h, d, g], w4(A_AM)[h, d, g], start=True, stop=False)
                nc.tensor.matmul(pb(3)[h, d, g], st_a[s][h, d, g], w4(A_QD)[h, d, g], start=False, stop=True)
                mm = nc.tensor.matmul(pb(4)[h, d, g], w4(A_KES)[h, d, g], w4(A_VTOK)[h, d, g], start=True, stop=True)
            mm.then_inc(S["gla_out"], 1)

        def loop_steps(eng, l, body):
            for s, (_, n) in enumerate(STEPS):
                first = l * 10 + (0 if s == 0 else STEPS[0][1])
                with eng.Fori(0, n) as i:
                    body(s, i + first, i)

        def scan_out_dve(dve, l, ob, gate, gain):
            meet("dve", dve)
            x = hT[:, ob:ob + 2, :]
            gt = pj[:, gate:gate + 2, :]
            k = scan_out_n["dve"] = scan_out_n["dve"] + 1
            head_norm_dve(dve, x, 2, gained(x, lambda b: par[:, l, gain:gain + 1]))
            dve.wait_ge(S["gate_exp"], k)
            e = wk[:, 2 * T:4 * T]
            nc.vector.tensor_scalar(e, e, 1.0, None, ALU.add)
            dve.drain()
            nc.vector.reciprocal(e, e)
            nc.vector.tensor_tensor(x, x, gt, ALU.mult)
            dve.drain()
            nc.vector.tensor_tensor(x, x, e.rearrange("p (b t) -> p b t", b=2), ALU.mult)
            meet("dve", dve)

        def scan_out_pe(pe):
            meet("pe", pe)
            head_norm_pe(pe, 2)
            meet("pe", pe)

        def scan_out_act(act, l, gate):
            meet("act", act)
            nc.scalar.activation(wk[:, 2 * T:4 * T].rearrange("p (b t) -> p b t", b=2), pj[:, gate:gate + 2, :],
                                 ACT.Exp, bias=par[:, l, C_ZERO:C_ZERO + 1], scale=-1.0).then_inc(S["gate_exp"], 1)
            head_norm_act(act, l, 2, L)
            meet("act", act)

        scan_out_n = {"dve": 0}

        def conv_dve(dve, l):
            for q in range(2):
                for j in range(3):
                    b = 3 * q + j
                    x, y = pj[:, DQ + b, :], tmp(j)
                    w = [par[:, l, C_CONV + 3 * b + c:C_CONV + 3 * b + c + 1] for c in range(3)]
                    nc.vector.tensor_scalar(y, x, w[1], None, ALU.mult)
                    dve.drain()
                    for a, e in STREAMS:
                        nc.vector.scalar_tensor_tensor(y[:, a + 1:e], x[:, a:e - 1], w[0], y[:, a + 1:e],
                                                       ALU.mult, ALU.add)
                    dve.drain()
                    for a, e in STREAMS:
                        nc.vector.scalar_tensor_tensor(y[:, a:e - 1], x[:, a + 1:e], w[2], y[:, a:e - 1],
                                                       ALU.mult, ALU.add)
                dve.drain().then_inc(S["conv_ready"], 1)
                dve.wait_ge(S["conv_exp"], 2 * l + q + 1)
                y, e = wk[:, 0:3 * T], wk[:, 4 * T:7 * T]
                nc.vector.tensor_scalar(e, e, 1.0, None, ALU.add)
                dve.drain()
                nc.vector.reciprocal(e, e)
                dve.drain()
                nc.vector.tensor_tensor(pj[:, DQ + 3 * q:DQ + 3 * q + 3, :],
                                        y.rearrange("p (b t) -> p b t", b=3),
                                        e.rearrange("p (b t) -> p b t", b=3), ALU.mult)
                dve.drain()
            x = pj[:, DQ:DQ + 4, :]
            head_norm_dve(dve, x, 4, gained(x, lambda b: L ** -0.5 if b < 2 else 1.0))
            z = tmp(0)
            nc.vector.tensor_scalar(z, pj[:, SMALL, :], par[:, l, C_DTB:C_DTB + 1], None, ALU.add)
            dve.drain()
            nc.vector.tensor_scalar(tmp(1), z, 0.0, 2.0, ALU.min, ALU.mult)
            dve.drain()
            nc.vector.tensor_tensor(tmp(1), tmp(1), z, ALU.subtract)
            meet("dve", dve)
            meet("dve", dve)
            nc.vector.scalar_tensor_tensor(z, z, 0.0, tmp(1), ALU.max, ALU.add)
            nc.vector.tensor_scalar(tmp(2), tmp(2), 1.0, None, ALU.add)
            dve.drain()
            nc.vector.tensor_scalar(z, z, tmp(3)[:, 0:1], -1.0, ALU.mult, ALU.mult)
            nc.vector.reciprocal(tmp(2), tmp(2))
            dve.drain()
            scan_chunks(tmp(4), z, 0, 64, 96)
            scan_chunks(tmp(4), z, 1, 96, 128)
            meet("dve", dve)
            meet("dve", dve)
            for j in range(0, 4, 2):
                nc.vector.tensor_copy(scan[:, j, :], pair(j))
            meet("dve", dve)
            meet("dve", dve)
            for j in range(0, 4, 2):
                nc.vector.tensor_copy(scan[:, 4 + j, :], pair(j))
            meet("dve", dve)

        def conv_pe(pe, l):
            head_norm_pe(pe, 4)
            meet("pe", pe)
            meet("pe", pe)
            meet("pe", pe)
            for j in range(4):
                r = R_DEC[j // 2]
                for a, b in PIECES:
                    nc.tensor.matmul(pair(j)[:, a:b], sel[r:r + 4, j, :], tmp(4)[r:r + 4, a:b], start=True, stop=True)
            meet("pe", pe)
            meet("pe", pe)
            for j in range(4):
                r = R_BETA
                for a, b in PIECES:
                    nc.tensor.matmul(pair(j)[:, a:b], sel[r:r + 8, j, :], tmp(2)[r:r + 8, a:b], start=True, stop=True)
            meet("pe", pe)
            meet("pe", pe)

        def conv_act(act, l):
            for q in range(2):
                act.wait_ge(S["conv_ready"], 2 * l + q + 1)
                nc.scalar.activation(wk[:, 4 * T:7 * T], wk[:, 0:3 * T], ACT.Exp, bias=par[:, l, C_ZERO:C_ZERO + 1],
                                     scale=-1.0).then_inc(S["conv_exp"], 1)
            head_norm_act(act, l, 4, 1)
            meet("act", act)
            zero = par[:, l, C_ZERO:C_ZERO + 1]
            nc.scalar.activation(tmp(1), tmp(1), ACT.Exp, bias=zero)
            nc.scalar.activation(tmp(2), pj[:, SMALL, :], ACT.Exp, bias=zero, scale=-1.0)
            nc.scalar.activation(tmp(3)[:, 0:1], par[:, l, C_ALOG:C_ALOG + 1], ACT.Exp, bias=zero, scale=1.0)
            act.drain()
            nc.scalar.activation(tmp(1), tmp(1), ACT.Ln, bias=par[:, l, C_ONE:C_ONE + 1], scale=1.0)
            meet("act", act)
            meet("act", act)
            meet("act", act)
            for j in range(1, 4, 2):
                nc.scalar.copy(scan[:, j, :], pair(j))
            meet("act", act)
            meet("act", act)
            for j in range(1, 4, 2):
                nc.scalar.copy(scan[:, 4 + j, :], pair(j))
            meet("act", act)

        (D_Q, D_K, D_KE, D_VB, D_KB, D_QD, D_GB, D_BB, D_E, D_DF, D_AT, D_QK, D_KES, D_VBS, D_ATL, D_X, D_XT, D_US,
         D_R, D_U) = range(20)

        def gdn_dve(dve, l, s, it, i):
            ts = chunks(i, s)
            dve.wait_ge(S["gdn_done"], it + 1)
            for d, t in enumerate(ts):
                nc.vector.tensor_copy(w4(D_Q)[:, d], pj[:, DQ:DQ + 2, bass.ds(t, L)])
                nc.vector.tensor_copy(w4(D_K)[:, d], pj[:, DK:DK + 2, bass.ds(t, L)])
                nc.vector.tensor_copy(w4(D_GB)[:, d], scan[:, 2 * d:2 * d + 2, bass.ds(t, L)])
                nc.vector.tensor_copy(w4(D_BB)[:, d], scan[:, 4 + 2 * d:6 + 2 * d, bass.ds(t, L)])
                nc.vector.tensor_tensor(w4(D_VB)[:, d], pj[:, DV:DV + 2, bass.ds(t, L)],
                                        scan[:, 4 + 2 * d:6 + 2 * d, bass.ds(t, L)], ALU.mult)
            dve.drain()

            def w3(n):
                return work[:, n, :].rearrange("p (a c) -> p a c", a=4)

            def bc(c):
                return c.unsqueeze(2).to_broadcast([P, 4, L])
            for h in range(2):
                hs = slice(64 * h, 64 * h + 64)
                nc.vector.tensor_tensor(w3(D_DF)[hs], w3(D_GB)[hs],
                                        ident[hs, hs].unsqueeze(1).to_broadcast([64, 4, L]), ALU.mult)
            for d in range(2):
                last = L - 1 if d == 0 else 0
                nc.vector.tensor_copy(cols[:, 4 + 2 * d:6 + 2 * d].unsqueeze(2), w4(D_GB)[:, d, :, last:last + 1])
            dve.drain()
            nc.vector.tensor_reduce(cols[:, 0:4], w3(D_DF), AX.X, ALU.add)
            nc.vector.tensor_tensor(w3(D_E), bc(cols[:, 4:8]), w3(D_GB), ALU.subtract)
            dve.drain()
            nc.vector.tensor_tensor(w3(D_DF), w3(D_GB), bc(cols[:, 0:4]), ALU.subtract)
            dve.drain()
            nc.vector.tensor_tensor(work[:, D_DF, :], work[:, D_DF, :], incl[:].rearrange("p d g c -> p (d g c)"),
                                    ALU.mult).then_inc(S["gdn_dif"], 1)
            dve.wait_ge(S["gdn_staged_a"], it + 1)
            nc.vector.tensor_tensor(work[:, D_KE, :], work[:, D_K, :], work[:, D_E, :], ALU.mult)
            nc.vector.tensor_tensor(work[:, D_KB, :], work[:, D_K, :], work[:, D_QD, :], ALU.mult)
            dve.drain()
            nc.vector.tensor_tensor(work[:, D_KB, :], work[:, D_KB, :], work[:, D_BB, :], ALU.mult)
            nc.vector.tensor_tensor(work[:, D_QD, :], work[:, D_QD, :], work[:, D_Q, :],
                                    ALU.mult).then_inc(S["gdn_staged_v"], 1)
            nc.vector.tensor_tensor(work[:, D_DF, :], work[:, D_DF, :], incl[:].rearrange("p d g c -> p (d g c)"),
                                    ALU.mult)
            dve.drain()
            dve.wait_ge(S["gdn_prod"], it + 1)
            nc.vector.tensor_tensor(work[:, D_AT, :], bank(0, 256), work[:, D_DF, :], ALU.mult)
            nc.vector.tensor_tensor(work[:, D_QK, :], bank(1, 256), work[:, D_DF, :], ALU.mult)
            dve.drain()
            nc.vector.tensor_tensor(work[:, D_AT, :], work[:, D_AT, :], work[:, D_BB, :], ALU.mult)
            dve.drain()
            for h in range(2):
                hs = slice(64 * h, 64 * h + 64)
                nc.vector.tensor_copy(w3(D_X)[hs], ident[hs, hs].unsqueeze(1).to_broadcast([64, 4, L]))
            for v in range(6):
                at = D_ATL
                nc.vector.tensor_tensor(work[:, at, :], work[:, D_AT, :], lvl[:, v].rearrange("p d g c -> p (d g c)"),
                                        ALU.mult).then_inc(S["gdn_at"], 1)
                if v == 0:
                    dve.drain()
                    nc.vector.tensor_tensor(work[:, D_XT, :], work[:, D_X, :], work[:, at, :], ALU.subtract)
                    dve.wait_ge(S["gdn_u"], it * 6 + 1)
                    nc.vector.tensor_tensor(work[:, D_X, :], work[:, D_X, :], bank(4, 256),
                                            ALU.subtract).then_inc(S["gdn_xs"], 1)
                    dve.drain()
                    continue
                dve.wait_ge(S["gdn_u"], it * 6 + (v + 1))
                nc.vector.tensor_copy(work[:, D_US, :], bank(4, 256)).then_inc(S["gdn_us"], 1)
                dve.wait_ge(S["gdn_x"], it * 5 + v)
                if v < 5:
                    nc.vector.tensor_tensor(work[:, D_X, :], work[:, D_X, :], bank(5, 256), ALU.subtract)
                nc.vector.tensor_tensor(work[:, D_XT, :], work[:, D_XT, :], bank(6, 256),
                                        ALU.subtract).then_inc(S["gdn_xs"], 1)
                dve.drain()
            dve.wait_ge(S["gdn_tok"], it + 1)
            dve.wait_ge(S["gdn_r0"], it + 1)
            nc.vector.tensor_tensor(work[:, D_R, :], work[:, D_VBS, :], bank(0, 256),
                                    ALU.subtract).then_inc(S["gdn_rs"], 1)
            dve.wait_ge(S["gdn_u1"], it + 1)
            nc.vector.tensor_copy(work[:, D_U, :], bank(1, 256)).then_inc(S["gdn_us1"], 1)
            dve.wait_ge(S["gdn_o"], it + 1)
            st = st_d[s][:].rearrange("p d g c -> p (d g) c")
            nc.vector.tensor_tensor(st, st, bc(cols[:, 8:12]), ALU.mult)
            for d, t in enumerate(ts):
                o = hT[:, OD:OD + 2, bass.ds(t, L)]
                nc.vector.tensor_tensor(o, o, pb(2)[:, d], ALU.add)
                dve.drain()
            nc.vector.tensor_tensor(st, st, bank(3, 256).rearrange("p (a c) -> p a c", a=4),
                                    ALU.add).then_inc(S["gdn_done"], 1)
            dve.drain()

        def gdn_act(act, l, s, it, i):
            zero = par[:, l, C_ZERO:C_ZERO + 1]
            act.wait_ge(S["gdn_dif"], it + 1)
            nc.scalar.activation(work[:, D_E, :], work[:, D_E, :], ACT.Exp, bias=zero)
            nc.scalar.activation(work[:, D_DF, :], work[:, D_DF, :], ACT.Exp, bias=zero)
            nc.scalar.activation(cols[:, 8:12], cols[:, 4:8], ACT.Exp, bias=zero)
            nc.scalar.activation(work[:, D_QD, :], work[:, D_GB, :], ACT.Exp, bias=zero).then_inc(S["gdn_staged_a"], 1)
            act.wait_ge(S["gdn_prod"], it + 1)
            nc.scalar.copy(work[:, D_KES, :], bank(2, 256))
            nc.scalar.copy(work[:, D_VBS, :], bank(3, 256)).then_inc(S["gdn_tok"], 1)

        def gdn_pe(pe, s, it):
            pe.wait_ge(S["gdn_staged_v"], it + 1)
            waited(pe)
            for d, g, h in units():
                nc.tensor.matmul(pb(0)[h, d, g], w4(D_K)[h, d, g], w4(D_K)[h, d, g], start=True, stop=True)
                nc.tensor.matmul(pb(1)[h, d, g], w4(D_K)[h, d, g], w4(D_Q)[h, d, g], start=True, stop=True)
                nc.tensor.matmul(pb(2)[h, d, g], w4(D_KE)[h, d, g], ident[h, h], start=True, stop=True)
                mm = nc.tensor.matmul(pb(3)[h, d, g], w4(D_VB)[h, d, g], ident[h, h], start=True, stop=True)
            mm.then_inc(S["gdn_prod"], 1)
            for v in range(6):
                pe.wait_ge(S["gdn_at"], it * 6 + (v + 1))
                if v > 0:
                    pe.wait_ge(S["gdn_xs"], it * 6 + v)
                waited(pe)
                for d, g, h in units():
                    mm = nc.tensor.matmul(pb(4)[h, d, g], w4(D_ATL)[h, d, g],
                                          ident[h, h] if v == 0 else w4(D_X)[h, d, g], start=True, stop=True)
                mm.then_inc(S["gdn_u"], 1)
                if v == 0:
                    continue
                pe.wait_ge(S["gdn_us"], it * 5 + v)
                waited(pe)
                for d, g, h in units():
                    if v < 5:
                        nc.tensor.matmul(pb(5)[h, d, g], w4(D_XT)[h, d, g], w4(D_US)[h, d, g], start=True, stop=True)
                    mm = nc.tensor.matmul(pb(6)[h, d, g], w4(D_US)[h, d, g], w4(D_XT)[h, d, g], start=True, stop=True)
                mm.then_inc(S["gdn_x"], 1)
            pe.wait_ge(S["gdn_tok"], it + 1)
            waited(pe)
            for d, g, h in units():
                mm = nc.tensor.matmul(pb(0)[h, d, g], w4(D_KB)[h, d, g], st_d[s][h, d, g], start=True, stop=True)
            mm.then_inc(S["gdn_r0"], 1)
            pe.wait_ge(S["gdn_xs"], it * 6 + 6)
            pe.wait_ge(S["gdn_rs"], it + 1)
            waited(pe)
            for d, g, h in units():
                mm = nc.tensor.matmul(pb(1)[h, d, g], w4(D_XT)[h, d, g], w4(D_R)[h, d, g], start=True, stop=True)
            mm.then_inc(S["gdn_u1"], 1)
            pe.wait_ge(S["gdn_us1"], it + 1)
            waited(pe)
            for d, g, h in units():
                nc.tensor.matmul(pb(2)[h, d, g], st_d[s][h, d, g], w4(D_QD)[h, d, g], start=True, stop=False)
                nc.tensor.matmul(pb(2)[h, d, g], w4(D_U)[h, d, g], w4(D_QK)[h, d, g], start=False, stop=True)
                mm = nc.tensor.matmul(pb(3)[h, d, g], w4(D_KES)[h, d, g], w4(D_U)[h, d, g], start=True, stop=True)
            mm.then_inc(S["gdn_o"], 1)

        def attn_units():
            for t in range(5):
                for kind in "BC":
                    for h in range(4):
                        if kind == "B":
                            p, q, k, o, c, vc = h // 2, SQ + h % 2, SK, OB + h % 2, 0, L * (h // 2)
                            loc = [0] if t == 0 else list(range(max(1, t - 1), min(4, t + 1) + 1))
                        else:
                            p, q, k, o, c, vc = h % 2, NQ + h // 2, NK + h // 2, OC + h // 2, 1 + h // 2, P + L * h
                            loc = [0] if t == 0 else [1, 2, 3, 4]
                        yield dict(t=t, kind=kind, h=h, hs=slice(64 * p, 64 * p + 64), q=q, k=k, o=o, c=c, vc=vc,
                                   loc=loc, ctx=0 if t == 0 else 2, nl=P * len(loc), n=P * len(loc) + (PAST if t else 0))

        UN = list(attn_units())
        NU = len(UN)

        def lbuf(u):
            return wk[:, (u % 2) * 800:(u % 2) * 800 + 800]

        def ptbuf(u):
            return wk[:, 1600 + (u % 2) * 768:1600 + (u % 2) * 768 + 768]

        def attn_scores(pe, u, base):
            x = UN[u]
            if u >= 2:
                pe.wait_ge(S["lg_ready"], base + u - 1)
            q = pj[x["hs"], x["q"], x["t"] * P:(x["t"] + 1) * P]
            b = 2 * (u % 2)
            mm = nc.tensor.matmul(bank(b)[:, 0:x["nl"]], q,
                                  pj[x["hs"], x["k"], x["loc"][0] * P:(x["loc"][-1] + 1) * P], start=True, stop=True)
            if x["ctx"]:
                mm = nc.tensor.matmul(bank(b + 1)[:, 0:PAST], q, ck[x["hs"], x["c"], :], start=True, stop=True)
            mm.then_inc(S["sc_ready"], 1)

        def attn_pv(pe, u, base):
            x = UN[u]
            pe.wait_ge(S["pt_copied"], base + u + 1)
            if u >= 2:
                pe.wait_ge(S["pv_free"], base + u - 1)
            vs = [vtok[:, t, x["vc"]:x["vc"] + L] for t in x["loc"]] + [cv[:, j, x["vc"]:x["vc"] + L]
                                                                       for j in range(x["ctx"])]
            for j, v in enumerate(vs):
                mm = nc.tensor.matmul(bank(6 + u % 2)[x["hs"], 0:P], v, ptbuf(u)[:, j * P:(j + 1) * P],
                                      start=(j == 0), stop=(j == len(vs) - 1))
            mm.then_inc(S["pv_ready"], 1)

        def attn_pe(pe, l):
            base = l * NU
            pe.wait_ge(S["cache_in"], 80 * (l + 1))
            attn_scores(pe, 0, base)
            for u in range(NU):
                if u + 1 < NU:
                    attn_scores(pe, u + 1, base)
                pe.wait_ge(S["pn_ready"], base + u + 1)
                if base + u > 0:
                    pe.wait_ge(S["pt_copied"], base + u)
                for j in range(UN[u]["n"] // P):
                    mm = nc.tensor.transpose(ps[:, 4 * 512 + j * P:4 * 512 + (j + 1) * P],
                                             lbuf(u)[:, j * P:(j + 1) * P], ident[:, :])
                mm.then_inc(S["pt_ready"], 1)
                if u > 0:
                    attn_pv(pe, u - 1, base)
            attn_pv(pe, NU - 1, base)
            meet("pe", pe)

        def attn_dve(dve, l):
            base = l * NU
            dve.wait_ge(S["rpb_loaded"], 16 * (l + 1))
            r3 = rpb.rearrange("p h m c -> p (h m) c")
            nc.vector.tensor_tensor(r3, r3, nmask[:, 0, :].unsqueeze(1).to_broadcast([P, 64, L]), ALU.mult)
            dve.drain()
            nc.vector.tensor_tensor(r3, r3, nmask[:, 1, :].unsqueeze(1).to_broadcast([P, 64, L]), ALU.add)
            dve.drain()

            def logits(u):
                x = UN[u]
                if u >= 2:
                    dve.wait_ge(S["pt_ready"], base + u - 1)
                dve.wait_ge(S["sc_ready"], base + u + 1)
                lg, b, nl, n = lbuf(u), 2 * (u % 2), x["nl"], x["n"]
                if x["t"] == 0:
                    nc.vector.tensor_scalar(lg[:, 0:nl], bank(b)[:, 0:nl], L ** -0.5, None, ALU.mult)
                elif x["kind"] == "B":
                    m0 = (x["loc"][0] - x["t"] + 1) * P
                    nc.vector.scalar_tensor_tensor(lg[:, 0:nl], bank(b)[:, 0:nl], L ** -0.5, swamask[:, m0:m0 + nl],
                                                   ALU.mult, ALU.add)
                else:
                    t = x["t"] - 1
                    bias = rpb[:, x["h"], 7 - 2 * t:15 - 2 * t, :].rearrange("p m c -> p (m c)")
                    nc.vector.scalar_tensor_tensor(lg[:, 0:nl], bank(b)[:, 0:nl], L ** -0.5, bias, ALU.mult, ALU.add)
                if x["ctx"]:
                    nc.vector.tensor_scalar(lg[:, nl:n], bank(b + 1)[:, 0:PAST], L ** -0.5, None, ALU.mult)
                w = n
                if x["kind"] == "B":
                    c = C_SINK + x["h"]
                    nc.vector.tensor_copy(lg[:, n:n + 1], par[:, l, c:c + 1])
                    w = n + 1
                dve.drain()
                a = 4 * (u % 2)
                nc.vector.tensor_reduce(att[:, a + 3:a + 4], lg[:, 0:w], AX.X, ALU.max)
                dve.drain()
                nc.vector.tensor_scalar(att[:, a:a + 1], att[:, a + 3:a + 4], -1.0, None,
                                        ALU.mult).then_inc(S["lg_ready"], 1)

            def normalise(u):
                a = 4 * (u % 2)
                dve.wait_ge(S["p_ready"], base + u + 1)
                nc.vector.reciprocal(att[:, a + 2:a + 3], att[:, a + 1:a + 2])
                dve.drain()
                n = UN[u]["n"]
                nc.vector.tensor_scalar(lbuf(u)[:, 0:n], lbuf(u)[:, 0:n], att[:, a + 2:a + 3], None,
                                        ALU.mult).then_inc(S["pn_ready"], 1)

            def output(u):
                x = UN[u]
                dve.wait_ge(S["pv_ready"], base + u + 1)
                nc.vector.tensor_copy(hT[x["hs"], x["o"], x["t"] * P:(x["t"] + 1) * P],
                                      bank(6 + u % 2)[x["hs"], 0:P]).then_inc(S["pv_free"], 1)

            for u in range(NU + 2):
                if u < NU:
                    logits(u)
                if 0 < u <= NU:
                    normalise(u - 1)
                if u >= 2:
                    output(u - 2)
            dve.drain().then_inc(S["attn_done"], 1)
            meet("dve", dve)

        def attn_act(act, l):
            base = l * NU
            for u in range(NU + 1):
                if u < NU:
                    a = 4 * (u % 2)
                    n = UN[u]["n"] + (UN[u]["kind"] == "B")
                    act.wait_ge(S["lg_ready"], base + u + 1)
                    nc.scalar.activation(lbuf(u)[:, 0:n], lbuf(u)[:, 0:n], ACT.Exp, bias=att[:, a:a + 1],
                                         accum_out=att[:, a + 1:a + 2]).then_inc(S["p_ready"], 1)
                if u > 0:
                    v = u - 1
                    act.wait_ge(S["pt_ready"], base + v + 1)
                    if v >= 2:
                        act.wait_ge(S["pv_ready"], base + v - 1)
                    n = UN[v]["n"]
                    nc.scalar.copy(ptbuf(v)[:, 0:n], ps[:, 4 * 512:4 * 512 + n]).then_inc(S["pt_copied"], 1)
            meet("act", act)

        def out_pe(pe, l):
            for d in range(KT):
                n = base_out[l] + d // 2
                pe.wait_ge(w_loaded[n % NSLOT], 16 * uses(n))
                if d >= 4:
                    pe.wait_ge(S["out_free"], l * KT + d - 3)
                for a, b in PIECES:
                    for k in range(KT):
                        mm = nc.tensor.matmul(pair(d)[:, a:b], slot3(n)[:, k, (d % 2) * P:(d % 2 + 1) * P],
                                              hT[:, k, a:b], start=(k == 0), stop=(k == KT - 1))
                mm.then_inc(S["out_ready"], 1)
                if d % 2:
                    pe.wait_ge(S["out_ready"], l * KT + d + 1)
                    pe.sem_inc(w_used, 1)
            meet("pe", pe)

        def residual(d, src, g):
            for s, (a, b) in enumerate(STREAMS):
                ins = nc.vector.scalar_tensor_tensor(xT[:, d, a:b], src[:, a:b], mod[:, g + d, s:s + 1],
                                                     xT[:, d, a:b], ALU.mult, ALU.add)
            return ins

        def out_dve(dve, l):
            for d in range(KT):
                dve.wait_ge(S["out_ready"], l * KT + d + 1)
                residual(d, pair(d), 16).then_inc(S["out_free"], 1)
            meet("dve", dve)

        gate = pj[:, 0:NE, :]
        lg3 = wk[:, 0:5 * NE].rearrange("p (t e) -> p t e", t=5)
        ge3 = wk[:, 64:64 + 5 * NE].rearrange("p (t e) -> p t e", t=5)
        cmp = wk[:, 256:256 + 5 * 64].rearrange("p (t e f) -> p t e f", t=5, e=NE)
        ceq = wk[:, 640:640 + 5 * 64].rearrange("p (t e f) -> p t e f", t=5, e=NE)
        gT = wk[:, 1024:1024 + T]

        def router_pe(pe):
            for t in range(5):
                for k in range(KT):
                    nc.tensor.matmul(ps[:, t * NE:(t + 1) * NE], hT[:, k, t * P:(t + 1) * P], rt[:, k, :],
                                     start=(k == 0), stop=(k == KT - 1))
            for _ in range(4):
                meet("pe", pe)
            for t in range(5):
                nc.tensor.matmul(ps[0:NE, t * P:(t + 1) * P], ge3[:, t, :], ident[:, :], start=True, stop=True)
            meet("pe", pe)
            meet("pe", pe)
            for half in range(2):
                for j in range(4):
                    e = 4 * half + j
                    for a, b in PIECES:
                        nc.tensor.matmul(pair(j)[:, a:b], ident[0:NE, e:e + 1].to_broadcast([NE, P]), gT[0:NE, a:b],
                                         start=True, stop=True)
                meet("pe", pe)
                meet("pe", pe)

        def router_dve(dve):
            meet("dve", dve)
            nc.vector.tensor_copy(wk[:, 0:5 * NE], ps[:, 0:5 * NE])
            dve.drain()
            nc.vector.tensor_reduce(att[:, 0:5], lg3, AX.X, ALU.max)
            e_ = lg3.unsqueeze(3).to_broadcast([P, 5, NE, NE])
            for t in range(5):
                le = lg3[:, t].unsqueeze(2).to_broadcast([P, NE, NE])
                lf = lg3[:, t].unsqueeze(1).to_broadcast([P, NE, NE])
                nc.vector.tensor_tensor(cmp[:, t], lf, le, ALU.is_gt)
                nc.vector.tensor_tensor(ceq[:, t], lf, le, ALU.is_equal)
            dve.drain()
            nc.vector.tensor_tensor(lg3, lg3, att[:, 0:5].unsqueeze(2).to_broadcast([P, 5, NE]), ALU.subtract)
            for t in range(5):
                nc.vector.tensor_tensor(ceq[:, t], ceq[:, t], tri[:, :, :], ALU.mult)
            meet("dve", dve)
            for t in range(5):
                nc.vector.tensor_tensor(cmp[:, t], cmp[:, t], ceq[:, t], ALU.add)
            dve.drain()
            nc.vector.tensor_reduce(wk[:, 128:128 + 5 * NE], cmp.rearrange("p t e f -> p (t e) f"), AX.X, ALU.add)
            dve.drain()
            nc.vector.tensor_scalar(wk[:, 128:128 + 5 * NE], wk[:, 128:128 + 5 * NE], 2.0, None, ALU.is_lt)
            meet("dve", dve)
            nc.vector.tensor_tensor(wk[:, 64:64 + 5 * NE], wk[:, 64:64 + 5 * NE], wk[:, 128:128 + 5 * NE], ALU.mult)
            dve.drain()
            nc.vector.tensor_reduce(att[:, 5:10], ge3, AX.X, ALU.add)
            dve.drain()
            nc.vector.reciprocal(att[:, 5:10], att[:, 5:10])
            dve.drain()
            nc.vector.tensor_tensor(ge3, ge3, att[:, 5:10].unsqueeze(2).to_broadcast([P, 5, NE]), ALU.mult)
            meet("dve", dve)
            meet("dve", dve)
            nc.vector.tensor_copy(gT[0:NE, :], ps[0:NE, 0:T])
            meet("dve", dve)
            for half in range(2):
                meet("dve", dve)
                for j in range(0, 4, 2):
                    nc.vector.tensor_copy(gate[:, 4 * half + j, :], pair(j))
                meet("dve", dve)

        def router_act(act):
            meet("act", act)
            meet("act", act)
            nc.scalar.activation(wk[:, 64:64 + 5 * NE], wk[:, 0:5 * NE], ACT.Exp, bias=par[:, 1, C_ZERO:C_ZERO + 1])
            meet("act", act)
            meet("act", act)
            meet("act", act)
            meet("act", act)
            for half in range(2):
                meet("act", act)
                for j in range(1, 4, 2):
                    nc.scalar.copy(gate[:, 4 * half + j, :], pair(j))
                meet("act", act)

        def act_buf(i):
            return pj[:, 8 + 2 * (i % 2):10 + 2 * (i % 2), :]

        def up_pe(pe, b, n, item, shift, prod, wshift):
            pe.wait_ge(w_loaded[(b + n) % NSLOT], wshift * 16 + 16 * uses(b + n))
            pe.wait_ge(w_loaded[(b + n + 1) % NSLOT], wshift * 16 + 16 * uses(b + n + 1))
            for c in range(2):
                for w in range(2):
                    q = prod + 2 * c + w
                    ffn_free_pe(pe, q, shift)
                    for a, e in PIECES:
                        for k in range(KT):
                            mm = nc.tensor.matmul(pair(q)[:, a:e], slot3(b + n + w)[:, k, c * P:(c + 1) * P],
                                                  hT[:, k, a:e], start=(k == 0), stop=(k == KT - 1))
                    mm.then_inc(S["f_ready"], 1)
            pe.wait_ge(S["f_ready"], shift + prod + 4)
            pe.sem_inc(w_used, 2)

        def ffn_free_pe(pe, q, shift):
            if q >= 4 or not isinstance(shift, int):
                pe.wait_ge(S["f_free"], shift + q - 3)

        def down_pe(pe, b, n, item, shift, prod, wshift, ishift, aprod):
            pe.wait_ge(w_loaded[(b + n) % NSLOT], wshift * 16 + 16 * uses(b + n))
            pe.wait_ge(S["hid_ready"], 2 * ishift + 2 * aprod + 2)
            for d in range(KT):
                q = prod + d
                ffn_free_pe(pe, q, shift)
                for a, e in PIECES:
                    for c in range(2):
                        mm = nc.tensor.matmul(pair(q)[:, a:e], slot2(b + n)[:, c, d * P:(d + 1) * P],
                                              act_buf(item)[:, c, a:e], start=(c == 0), stop=(c == 1))
                mm.then_inc(S["f_ready"], 1)
            pe.wait_ge(S["f_ready"], shift + prod + 8)
            pe.sem_inc(w_used, 1)

        def up_act(act, l, shift, prod, ishift, aprod):
            for c in range(2):
                q = prod + 2 * c
                act.wait_ge(S["f_ready"], shift + q + 1)
                if 2 * aprod + c - 1 > 0:
                    act.wait_ge(S["hid_ready"], 2 * ishift + 2 * aprod + c - 1)
                nc.scalar.activation(pj[:, 12 + c, :], pair(q), ACT.Exp, bias=par[:, l, C_ZERO:C_ZERO + 1],
                                     scale=-1.0).then_inc(S["f_exp"], 1)

        def up_dve(dve, l, item, shift, prod, ishift, aprod, g):
            for c in range(2):
                e, o = pj[:, 12 + c, :], act_buf(item)[:, c, :]
                q = prod + 2 * c
                dve.wait_ge(S["f_exp"], 2 * ishift + 2 * aprod + c + 1)
                nc.vector.tensor_scalar(e, e, 1.0, None, ALU.add)
                dve.drain()
                nc.vector.reciprocal(e, e)
                dve.drain()
                nc.vector.tensor_tensor(e, e, pair(q), ALU.mult).then_inc(S["f_free"], 1)
                dve.drain()
                dve.wait_ge(S["f_ready"], shift + q + 2)
                if g is None:
                    nc.vector.tensor_tensor(o, e, pair(q + 1), ALU.mult).then_inc(S["f_free"], 1)
                    dve.drain().then_inc(S["hid_ready"], 1)
                else:
                    nc.vector.tensor_tensor(e, e, pair(q + 1), ALU.mult).then_inc(S["f_free"], 1)
                    dve.drain()
                    nc.vector.tensor_tensor(o, e, g, ALU.mult).then_inc(S["hid_ready"], 1)

        def down_dve(dve, shift, prod):
            for d in range(KT):
                dve.wait_ge(S["f_ready"], shift + prod + d + 1)
                residual(d, pair(prod + d), 40).then_inc(S["f_free"], 1)
            dve.drain()

        F_BASE = (0, 12 * DENSE_ITEMS)
        I_BASE = (0, DENSE_ITEMS)

        def ffn(l, up, down):
            items = DENSE_ITEMS if l == 0 else EXPERT_ITEMS * NE
            up(0, 0, F_BASE[l], 0, 0)
            q = F_BASE[l] + 4

            def run(i, e, q, n):
                if i + 1 < items:
                    up(i + 1, e, q, n, i + 1)
                    q, n = q + 4, n + 2
                down(i, e, q, n, i)
                return q + 8, n + 1

            n = 2
            if l == 0:
                for i in range(items):
                    q, n = run(i, 0, q, n)
                return
            with up.eng.Fori(0, NE - 1) as e:
                qq, nn = q, n
                for i in range(EXPERT_ITEMS):
                    qq, nn = run(i, e, qq, nn)
            q, n = q + 48 * (NE - 1), n + 12 * (NE - 1)
            for i in range(EXPERT_ITEMS * (NE - 1), items):
                q, n = run(i, 0, q, n)

        class Part:

            def __init__(self, eng, f):
                self.eng, self.f = eng, f

            def __call__(self, *a):
                self.f(*a)

        def ffn_pe(pe, l):
            b = base_ffn[l]
            ffn(l, Part(pe, lambda i, e, q, n, a: up_pe(pe, b, n, i, e * 48, q, e * 3)),
                Part(pe, lambda i, e, q, n, a: down_pe(pe, b, n, i, e * 48, q, e * 3, e * 4, I_BASE[l] + a)))
            meet("pe", pe)

        def ffn_dve(dve, l):
            def up(i, e, q, n, a):
                if l == 0:
                    g = None
                elif isinstance(e, int):
                    g = gate[:, i // EXPERT_ITEMS, :]
                else:
                    g = gate[:, bass.ds(e + i // EXPERT_ITEMS, 1), :].rearrange("p a t -> p (a t)")
                up_dve(dve, l, i, e * 48, q, e * 4, I_BASE[l] + a, g)
            ffn(l, Part(dve, up), Part(dve, lambda i, e, q, n, a: down_dve(dve, e * 48, q)))
            meet("dve", dve)

        def ffn_act(act, l):
            ffn(l, Part(act, lambda i, e, q, n, a: up_act(act, l, e * 48, q, e * 4, I_BASE[l] + a)), Part(act, lambda *a: None))
            meet("act", act)

        @block.tensor
        def _(pe):
            pe.wait_ge(consts_loaded, 16 * N_CONST)
            meet("pe", pe)
            for l in range(DEPTH):
                mod_pe(pe, l)
                norm_pe(pe, 2 * l)
                in_pe(pe, l)
                qk_pe(pe, l)
                decay_a_pe(pe, l)
                loop_steps(pe, l, lambda s, it, i: gla_pe(pe, s, it))
                scan_out_pe(pe)
                conv_pe(pe, l)
                loop_steps(pe, l, lambda s, it, i: gdn_pe(pe, s, it))
                scan_out_pe(pe)
                attn_pe(pe, l)
                out_pe(pe, l)
                norm_pe(pe, 2 * l + 1)
                if l == 1:
                    router_pe(pe)
                ffn_pe(pe, l)

        @block.scalar
        def _(act):
            act.wait_ge(consts_loaded, 16 * N_CONST)
            nc.scalar.activation(cE[:], cT[:], ACT.Exp, bias=par[:, 0, C_ZERO:C_ZERO + 1], scale=-1.0)
            meet("act", act)
            for l in range(DEPTH):
                mod_act(act, l)
                norm_act(act, 2 * l, l)
                in_evac("act", act, l)
                qk_act(act, l)
                decay_a_act(act, l)
                loop_steps(act, l, lambda s, it, i: gla_act(act, l, s, it, i))
                scan_out_act(act, l, AR)
                conv_act(act, l)
                loop_steps(act, l, lambda s, it, i: gdn_act(act, l, s, it, i))
                scan_out_act(act, l, DR)
                attn_act(act, l)
                meet("act", act)
                norm_act(act, 2 * l + 1, l)
                if l == 1:
                    router_act(act)
                ffn_act(act, l)

        @block.vector
        def _(dve):
            dve.wait_ge(consts_loaded, 16 * N_CONST)
            meet("dve", dve)
            nc.vector.tensor_scalar(cE[:], cE[:], 1.0, None, ALU.add)
            dve.drain()
            nc.vector.reciprocal(cE[:], cE[:])
            dve.drain()
            nc.vector.tensor_tensor(cT[:], cT[:], cE[:], ALU.mult).then_inc(S["silu_c"], 1)
            dve.drain().then_inc(S["gla_done"], 1)
            dve.drain().then_inc(S["gdn_done"], 1)
            for l in range(DEPTH):
                mod_dve(dve, l)
                norm_dve(dve, 2 * l)
                in_evac("dve", dve, l)
                nc.vector.memset(hT[:], 0.0)
                if l > 0:
                    dve.wait_ge(S["states_out"], 80 * l)
                nc.vector.memset(st_a[0][:], 0.0)
                nc.vector.memset(st_d[0][:], 0.0)
                qk_dve(dve, l)
                decay_a_dve(dve, l)
                dve.wait_ge(S["cache_in"], 80 * (l + 1))
                loop_steps(dve, l, lambda s, it, i: gla_dve(dve, l, s, it, i))
                scan_out_dve(dve, l, OA, AR, C_AON)
                dve.drain().then_inc(S["mixer_a_done"], 1)
                conv_dve(dve, l)
                loop_steps(dve, l, lambda s, it, i: gdn_dve(dve, l, s, it, i))
                dve.drain().then_inc(S["mixer_d_done"], 1)
                scan_out_dve(dve, l, OD, DR, C_DON)
                attn_dve(dve, l)
                out_dve(dve, l)
                dve.wait_ge(S["states_out"], 80 * (l + 1))
                norm_dve(dve, 2 * l + 1)
                if l == 1:
                    router_dve(dve)
                ffn_dve(dve, l)
            dve.drain().then_inc(S["final_x"], 1)


N_CONST = 16


def constants():
    def bits(m):
        return (m * 0x3F80).astype(np.uint16)
    i = np.arange(P)
    f, j = i % L, i // L
    c = {"ident": np.eye(P), "ones": np.ones((P, P)), "blk": (j[:, None] == j[None, :]) * 1.0}
    sel = np.zeros((P, 4, P))
    for d in range(2):
        for h in range(4):
            for r in (R_BETA + 4 * d + h, R_DEC[d] + h):
                sel[r, 2 * d + h // 2, L * (h % 2):L * (h % 2) + L] = 1.0
    c["sel"] = sel
    src = np.where(f % 32 < 16, i + 16, i - 16)
    rot = np.zeros((P, P))
    rot[src, i] = np.where(f % 32 < 16, -1.0, 1.0)
    c["rot"] = rot
    tok = np.arange(NS_TOK)
    pos = np.where((f < 32)[:, None], (tok // L)[None, :], (tok % L)[None, :]).astype(np.float32)
    inv = (1.0 / (np.float32(10000.0) ** (np.arange(16, dtype=np.float32) / np.float32(16))))[f % 16]
    ang = pos * inv[:, None].astype(np.float32)
    c["cossin"] = np.stack([np.cos(ang), np.sin(ang)], 1)
    t = np.arange(T)
    c["cmask"] = np.broadcast_to(np.stack([t % L != 0, t % L != L - 1])[None], (P, 2, T))
    a, b = f[:, None], np.arange(L)[None, :]
    inc = np.stack([a <= b, a >= b], 1)
    c["incl"] = np.broadcast_to(inc[:, :, None, :], (P, 2, 2, L))
    lv = []
    for s in (1, 2, 4, 8, 16, 32):
        fwd = ((b // s) % 2 == 1) & (a // s == b // s - 1)
        bwd = ((a // s) % 2 == 1) & (b // s == a // s - 1)
        lv.append(np.stack([fwd, bwd], 1))
    c["lvl"] = np.broadcast_to(np.stack(lv, 1)[:, :, :, None, :], (P, 6, 2, 2, L))
    q, k = i[:, None], np.arange(3 * P)[None, :] - P
    c["swamask"] = np.where(abs(q - k) <= P, 0.0, NEG)
    col = np.arange(L)
    cs = np.clip(col - 8, 0, L - 16)
    m = ((col[None, :] >= cs[:, None]) & (col[None, :] < cs[:, None] + 16))[f]
    c["nmask"] = np.stack([m * 1.0, np.where(m, 0.0, NEG)], 1)
    c["tri"] = np.broadcast_to((np.arange(NE)[None, :] < np.arange(NE)[:, None])[None], (P, NE, NE))
    return {n: np.ascontiguousarray(bits(v) if n in BITS else v.astype(np.float32)) for n, v in c.items()}


def layouts(x):
    f32 = np.float32

    def feat(a):
        return np.moveaxis(a.reshape(a.shape[:-1] + (KT, P)), (-1, -2), (0, 1))

    def rows(w, width):
        s = w.shape[:-2]
        w = w.reshape(s + (KT, P, w.shape[-1] // width, width))
        k = len(s)
        return np.moveaxis(w, (k + 2, k + 1, k, k + 3), (k, k + 1, k + 2, k + 3)).reshape(s + (-1, P, KT * width))

    def down(w):
        s = w.shape[:-2]
        w = w.reshape(s + (w.shape[-2] // WCOL, 2, P, D))
        return np.swapaxes(w, -3, -2).reshape(s + (-1, P, 2 * D))

    o = constants()
    o["xT"] = feat(np.concatenate([x["x_prompt"][0], x["x_sample"][0]]))
    o["cT"] = feat(np.stack([x["c_ctx"], x["c"][0]]))
    o["wmod"] = rows(x["w_mod"], WCOL)
    w = x["w_in"]
    cut = [0] + list(np.cumsum([256] * 4 + [16] * 2 + [256, 128, 128] + [256] * 3 + [256] * 4 + [4] * 4))
    part = [w[:, :, a:b] for a, b in zip(cut[:-1], cut[1:])]
    aq, ak, av, ar, alf, alb, sq, sk, sv, nq, nk, nv, dq, dk, dv, dr, daf, dab, dbf, dbb = part

    def z(n):
        return np.zeros((DEPTH, D, n), f32)
    sq = sq.reshape(DEPTH, D, 2, 2, L).transpose(0, 1, 3, 2, 4).reshape(DEPTH, D, 256)
    small = np.concatenate([alf, alb, dbf, dbb, z(24), daf, z(28), dab, z(28)], -1)
    o["win"] = rows(np.concatenate([aq, ak, av, ar, sq, sk, nq, nk, dq, dk, dv, dr, small], -1), WCOL)
    o["wv"] = np.concatenate([sv, nv], -1).reshape(DEPTH, KT, P, V_COLS).transpose(0, 2, 1, 3)
    wo = x["w_out"].reshape(DEPTH, 4, 256, D).copy()
    wo[:, 1] = wo[:, 1].reshape(DEPTH, 2, 2, L, D).transpose(0, 2, 1, 3, 4).reshape(DEPTH, 256, D)
    o["wout"] = rows(wo.reshape(DEPTH, D, D), WCOL)
    o["d1"], o["d3"], o["d2"] = rows(x["ffn_w1"][0], WCOL), rows(x["ffn_w3"][0], WCOL), down(x["ffn_w2"][0])
    o["e1"] = rows(x["moe_w1"][0], WCOL).reshape(-1, P, SLOT)
    o["e3"] = rows(x["moe_w3"][0], WCOL).reshape(-1, P, SLOT)
    o["e2"] = down(x["moe_w2"][0]).reshape(-1, P, SLOT)
    o["router"] = x["moe_router"][0].reshape(KT, P, NE).transpose(1, 0, 2)

    par = np.zeros((P, DEPTH, NPAR), f32)
    for l in range(DEPTH):
        def put(c, a):
            par[:, l, c:c + a.shape[1]] = a
        put(C_N1, x["norm1_g"][l].reshape(KT, P).T)
        put(C_N2, x["norm2_g"][l].reshape(KT, P).T)
        put(C_BMOD, x["b_mod"][l].reshape(48, P).T)
        put(C_BUP, x["gla_bup"][l].reshape(4, P).T)
        for c, n in ((C_AON, "gla_onorm"), (C_SQN, "swa_qnorm"), (C_SKN, "swa_knorm"), (C_NQN, "na_qnorm"),
                     (C_NKN, "na_knorm"), (C_DON, "gdn_onorm")):
            put(c, np.tile(x[n][l], 2)[:, None])
        put(C_SINK, np.broadcast_to(x["swa_sink"][l][None], (P, 4)))
        put(C_CONV, x["gdn_conv"][l].reshape(3, 6, P).transpose(2, 1, 0).reshape(P, 18))
        for d in range(2):
            par[R_DEC[d]:R_DEC[d] + 4, l, C_ALOG] = x["gdn_alog"][l, d]
            par[R_DEC[d]:R_DEC[d] + 4, l, C_DTB] = x["gdn_dtbias"][l, d]
        par[:, l, C_EPS], par[:, l, C_ONE] = EPS, 1.0
    o["par"] = par
    wup = np.zeros((32, DEPTH, 4, P), f32)
    for d in range(2):
        wup[16 * d:16 * d + 16, :, 2 * d:2 * d + 2] = x["gla_wup"][:, d].reshape(DEPTH, 16, 2, P).transpose(1, 0, 2, 3)
    o["wup"] = wup
    sk_, nk_ = x["cache_swa_k"][0], x["cache_na_k"][0]
    o["ck"] = np.concatenate([sk_.transpose(0, 1, 3, 2).reshape(DEPTH, 1, P, PAST),
                              nk_.transpose(0, 1, 3, 2).reshape(DEPTH, 2, P, PAST)], 1).transpose(0, 2, 1, 3)
    v = np.concatenate([x["cache_swa_v"][0], x["cache_na_v"][0]], 1)
    o["cv"] = v.reshape(DEPTH, 6, 2, P, L).transpose(0, 3, 2, 1, 4).reshape(DEPTH, P, 2, V_COLS)
    for n, s in (("sta", "state_gla"), ("std", "state_gdn")):
        o[n] = x[s][0].reshape(DEPTH, 2, 2, P, L).transpose(0, 3, 1, 2, 4)
    r = np.pad(x["na_rpb"], ((0, 0), (0, 0), (1, 1), (48, 48)))
    q, k, m = np.arange(L)[:, None], np.arange(L)[None, :], np.arange(16)
    win = r[:, :, :, k - q + 63]
    o["rpb"] = np.stack([win[:, :, m + 1 - rr].transpose(0, 3, 1, 2, 4) for rr in range(2)], 1).reshape(DEPTH, P, 4096)
    return {n: np.ascontiguousarray(a) for n, a in o.items()}


BITS = ("cmask", "incl", "lvl", "tri")


OUTS = {"yT": (P, KT, T), "new_k": (DEPTH, P, NP_TOK), "new_nk": (DEPTH, P, 2, NP_TOK), "new_v": (DEPTH, P, V_COLS),
        "new_sta": (DEPTH, P, 2, 2, L), "new_std": (DEPTH, P, 2, 2, L)}


def declare(nc, arrays):
    A = {n: nc.dram_tensor(f"in_{n}", a.shape, mybir.dt.from_np(a.dtype), kind="ExternalInput").ap()
         for n, a in arrays.items()}
    for n in BITS:
        A[n] = A[n].bitcast(BF16)
    A |= {n: nc.dram_tensor(n, s, F32, kind="ExternalOutput").ap() for n, s in OUTS.items()}
    build(nc, A)


def kernel(**inputs):
    import concourse.bacc as bacc
    from concourse.bass_utils import run_bass_kernel_spmd
    arrays = layouts({n: np.asarray(a) for n, a in inputs.items()})
    nc = bacc.Bacc("TRN2", target_bir_lowering=False, num_devices=1)
    declare(nc, arrays)
    r = run_bass_kernel_spmd(nc, [{f"in_{n}": a for n, a in arrays.items()}], core_ids=[0]).results[0]
    return results(r)


def results(r):
    y = np.moveaxis(r["yT"], (1, 0), (1, 2)).reshape(T, D)
    k = r["new_k"].reshape(DEPTH, 2, L, NP_TOK).transpose(0, 1, 3, 2)[None]
    nk = r["new_nk"].reshape(DEPTH, 2, L, 2, NP_TOK).transpose(0, 3, 1, 4, 2).reshape(1, DEPTH, 4, NP_TOK, L)
    v = r["new_v"].reshape(DEPTH, P, 6, L).transpose(0, 2, 1, 3)
    sta, std = (r[n].transpose(0, 2, 3, 1, 4).reshape(1, DEPTH, 2, 4, L, L) for n in ("new_sta", "new_std"))
    out = (y[None, :NP_TOK], y[None, NP_TOK:], k, v[None, :, 0:2], nk, v[None, :, 2:6], sta, std)
    return tuple(np.ascontiguousarray(a) for a in out)
```

```python
from contextlib import ExitStack

import numpy as np

import concourse.bass as bass
from concourse import mybir

F32 = mybir.dt.float32
BF16 = mybir.dt.bfloat16
F16 = mybir.dt.float16
ALU = mybir.AluOpType
ACT = mybir.ActivationFunctionType
AX = mybir.AxisListType

P = 128
D = 1024
KT = D // P
NP_TOK, NS_TOK = 128, 512
T = NP_TOK + NS_TOK
STREAMS = ((0, NP_TOK), (NP_TOK, T))
PIECES = ((0, 512), (512, T))
DEPTH = 2
L = 64
PAST = 256
EPS = 1e-6
NEG = -1e30
FF = 2816
NE = 8
WCOL = 256
SLOT = KT * WCOL
NSLOT = 4
W_SCALE = 512.0
N_MOD, N_IN, N_OUT = 6 * D // WCOL, 12, D // WCOL
DENSE_ITEMS = FF // WCOL
EXPERT_ITEMS = 4
V_COLS = 384

AQ, AK, AV, AR, SQ, SK, NQ, NK, DQ, DK, DV, DR, SMALL = 0, 2, 4, 6, 8, 10, 11, 13, 15, 17, 19, 21, 23
NBLK = 24
R_BETA, R_DEC = 32, (64, 96)

C_N1, C_N2, C_BMOD, C_BUP, C_AON, C_SQN, C_SKN, C_SINK, C_NQN, C_NKN, C_CONV, C_ALOG, C_DTB, C_DON, C_EPS, C_ONE, \
    C_ZERO = 0, 8, 16, 64, 68, 69, 70, 71, 75, 76, 77, 95, 96, 97, 98, 99, 100
NPAR = 101
OA, OB, OC, OD = 0, 2, 4, 6


def build(nc, A):
    with ExitStack() as ctx:
        def sb(name, shape, dt=F32):
            return ctx.enter_context(nc.sbuf_tensor(name, shape, dt))

        def sem(name):
            return ctx.enter_context(nc.semaphore(name))

        xT = sb("xT", [P, KT, T])
        hT = sb("hT", [P, KT, T])
        pj = sb("pj", [P, NBLK, T])
        vtok = sb("vtok", [P, 5, V_COLS])
        scan = sb("scan", [P, 8, T])
        ring = sb("ring", [P, NSLOT, SLOT])
        work = sb("work", [P, 20, 256])
        ident = sb("ident", [P, P])
        ones = sb("ones", [P, P])
        blk = sb("blk", [P, P])
        sel = sb("sel", [P, 4, P])
        rot = sb("rot", [P, P])
        cmask = sb("cmask", [P, 2, T], BF16)
        incl = sb("incl", [P, 2, 2, L], BF16)
        lvl = sb("lvl", [P, 6, 2, 2, L], BF16)
        swamask = sb("swamask", [P, 3 * P])
        nmask = sb("nmask", [P, 2, L])
        ck = sb("ck", [P, 3, PAST])
        cv = sb("cv", [P, 2, V_COLS])
        st_a = [sb(f"st_a{s}", [P, 2, 2, L]) for s in range(2)]
        st_d = [sb(f"st_d{s}", [P, 2, 2, L]) for s in range(2)]
        par = sb("par", [P, DEPTH, NPAR])
        wup = sb("wup", [32, DEPTH, 4, P])
        cT = sb("cT", [P, KT, 2])
        cE = sb("cE", [P, KT, 2])
        mod = sb("mod", [P, 48, 2])
        s1 = sb("s1", [P, 2, KT, 2])
        cols = sb("cols", [P, 32])
        att = sb("att", [P, 16])
        rt = sb("rt", [P, KT, NE])
        tri = sb("tri", [P, NE, NE], BF16)
        ps = ctx.enter_context(nc.psum_tensor("ps", [P, 8 * 512], F32))

        cossin = scan[:, 6:8, 0:NS_TOK]
        wk = work[:, :, :].rearrange("p a b -> p (a b)")
        scr = scan[:, :, :].rearrange("p a b -> p (a b)")
        rpb = pj[:, 0:8, :].rearrange("p a b -> p (a b)")[:, 0:4 * 16 * L].rearrange(
            "p (h m c) -> p h m c", h=4, m=16)

        def tmp(n):
            return wk[:, n * T:(n + 1) * T]

        def pair(n):
            return ps[:, (n % 4) * 1024:(n % 4) * 1024 + T]

        def bank(n, w=512):
            return ps[:, n * 512:n * 512 + w]

        def halves(region, n):
            return region.bitcast(F16)[:, 0:n], region.bitcast(F16)[:, n:2 * n]

        def split_slot(phase, n):
            at = (wk[:, 0:SLOT], wk[:, SLOT:2 * SLOT], scr[:, 0:SLOT], scr[:, SLOT:2 * SLOT])
            return halves(at[n % (4 if phase == "ffn" else 2)], SLOT)

        def split_h(phase):
            region = pj[:, 16:24, :].rearrange("p a b -> p (a b)") if phase == "ffn" else scr
            return [x.rearrange("p (k t) -> p k t", k=KT) for x in halves(region, KT * T)]

        def w3k(parts, k=KT):
            return [x.rearrange("p (k c) -> p k c", k=k) for x in parts]

        def mm3(out, w, x, start, stop):
            nc.tensor.matmul(out, w[0], x[0], start=start, stop=False)
            nc.tensor.matmul(out, w[0], x[1], start=False, stop=False)
            return nc.tensor.matmul(out, w[1], x[0], start=False, stop=stop)

        def slot3(n):
            return ring[:, n % NSLOT, :].rearrange("p (k c) -> p k c", k=KT)

        def slot2(n):
            return ring[:, n % NSLOT, :].rearrange("p (c n) -> p c n", c=2)

        consts_loaded = sem("consts_loaded")
        w_loaded = [sem(f"w_loaded{i}") for i in range(NSLOT)]
        w_used = sem("w_used")
        meeting = sem("meeting")
        names = """c_padded row_in row_exp row_scanned spread_ready spread_free_v spread_free_a conv_sq conv_sum conv_r
            ssq_in ssq_out rstd_ready normed_v prod_ready prod_free_v prod_free_a
            hn_sq hn_sum hn_r w_high h_high proj_done conv_ready conv_exp gate_exp rope_ready rope_out
            sc_ready lg_ready p_ready pn_ready pt_ready pt_copied pv_ready pv_free mixer_a_done mixer_d_done
            rpb_loaded out_ready out_free f_ready f_free f_exp hid_ready out_stored states_out new_kv final_x
            cache_in attn_done""".split()
        S = {n: sem(n) for n in names}
        by_direction = """gla_exp gla_staged gla_prod gla_evac_v gla_evac_a gla_out gla_done gdn_staged_v gdn_staged_a
            gdn_dif gdn_prod gdn_at gdn_u gdn_us gdn_x gdn_xs gdn_r0 gdn_tok gdn_rs gdn_u1 gdn_us1 gdn_o
            gdn_done""".split()
        S |= {n: [sem(f"{n}{d}") for d in range(2)] for n in by_direction}

        block = ctx.enter_context(nc.Block())
        met = {"pe": 0, "dve": 0, "act": 0}

        def meet(who, eng):
            met[who] += 1
            eng.drain().then_inc(meeting, 1)
            eng.wait_ge(meeting, 3 * met[who])

        base_mod = [0, 0]
        base_in, base_out, base_ffn = [0, 0], [0, 0], [0, 0]
        n = 0
        for l in range(DEPTH):
            base_mod[l] = n
            n += N_MOD
            base_in[l] = n
            n += N_IN + 2
            base_out[l] = n
            n += N_OUT
            base_ffn[l] = n
            n += 3 * (DENSE_ITEMS if l == 0 else EXPERT_ITEMS * NE)

        def uses(n):
            return n // NSLOT + 1

        @block.sync
        def _(sp):
            def load(n, src, width=None, shift=0):
                if isinstance(shift, int) and shift == 0 and n < NSLOT:
                    pass
                else:
                    sp.wait_ge(w_used, shift + (n - NSLOT + 1))
                dst = ring[:, n % NSLOT, :] if width is None else slot3(n)[:, :, 0:width]
                sp.dma_start(dst, src).then_inc(w_loaded[n % NSLOT], 16)

            consts = [(ident, "ident"), (ones, "ones"), (blk, "blk"), (rot, "rot"), (sel, "sel"),
                      (cmask, "cmask"), (incl, "incl"), (lvl, "lvl"), (swamask, "swamask"), (nmask, "nmask"),
                      (par, "par"), (wup, "wup"), (cT, "cT"), (rt, "router"), (tri, "tri"), (xT, "xT")]
            for dst, name in consts:
                sp.dma_start(dst[:], A[name]).then_inc(consts_loaded, 16)
            for l in range(DEPTH):
                for j in range(N_MOD):
                    load(base_mod[l] + j, A["wmod"][l, j])
                for j in range(N_IN):
                    load(base_in[l] + j, A["win"][l, j])
                for j in range(2):
                    load(base_in[l] + N_IN + j, A["wv"][l, j])
                for j in range(N_OUT):
                    load(base_out[l] + j, A["wout"][l, j])
                b = base_ffn[l]
                if l == 0:
                    load(b, A["d1"][0])
                    load(b + 1, A["d3"][0])
                    b += 2
                    for i in range(DENSE_ITEMS):
                        if i + 1 < DENSE_ITEMS:
                            load(b, A["d1"][i + 1])
                            load(b + 1, A["d3"][i + 1])
                            b += 2
                        load(b, A["d2"][i])
                        b += 1
                else:
                    load(b, A["e1"][0])
                    load(b + 1, A["e3"][0])
                    b += 2

                    def iteration(b, it, e):
                        def item(name, i):
                            if isinstance(e, int):
                                return A[name][i]
                            return A[name][bass.ds(e * EXPERT_ITEMS + i, 1)].rearrange("a p n -> p (a n)")
                        if it + 1 < EXPERT_ITEMS * NE:
                            load(b, item("e1", it + 1), None, e * 12)
                            load(b + 1, item("e3", it + 1), None, e * 12)
                            b += 2
                        load(b, item("e2", it), None, e * 12)
                        return b + 1
                    for it in range(EXPERT_ITEMS):
                        b = iteration(b, it, 0)
                    with sp.Fori(0, NE - 2) as e:
                        for j in range(EXPERT_ITEMS):
                            iteration(b + 3 * j, EXPERT_ITEMS + j, e)
                    b += 12 * (NE - 2)
                    for it in range(EXPERT_ITEMS * (NE - 1), EXPERT_ITEMS * NE):
                        b = iteration(b, it, 0)

        @block.gpsimd
        def _(pool):
            for l in range(DEPTH):
                if l > 0:
                    pool.wait_ge(S["attn_done"], l)
                for dst, name in ((ck, "ck"), (cv, "cv"), (st_a[1], "sta"), (st_d[1], "std")):
                    pool.dma_start(dst[:], A[name][l]).then_inc(S["cache_in"], 16)
                pool.wait_ge(S["proj_done"], l + 1)
                pool.dma_start(cossin, A["cossin"]).then_inc(S["cache_in"], 16)
                pool.wait_ge(S["mixer_a_done"], l + 1)
                pool.dma_start(rpb.rearrange("p h m c -> p (h m c)"), A["rpb"][l]).then_inc(S["rpb_loaded"], 16)
                pool.dma_start(A["new_sta"][l], st_a[0][:]).then_inc(S["states_out"], 16)
                pool.wait_ge(S["new_kv"], l + 1)
                pool.dma_start(A["new_k"][l], pj[:, SK, 0:NP_TOK]).then_inc(S["states_out"], 16)
                pool.dma_start(A["new_nk"][l], pj[:, NK:NK + 2, 0:NP_TOK]).then_inc(S["states_out"], 16)
                pool.dma_start(A["new_v"][l], vtok[:, 0, :]).then_inc(S["states_out"], 16)
                pool.wait_ge(S["mixer_d_done"], l + 1)
                pool.dma_start(A["new_std"][l], st_d[0][:]).then_inc(S["states_out"], 16)
            pool.wait_ge(S["final_x"], 1)
            pool.dma_start(A["yT"], xT[:]).then_inc(S["out_stored"], 16)
            pool.wait_ge(S["out_stored"], 16)
            pool.wait_ge(S["states_out"], 80 * DEPTH)

        n_hi = {"act": 0, "dve": 0}

        def split_hi(act, phase, n, shift=0, hshift=0):
            act.wait_ge(w_loaded[n % NSLOT], shift * 16 + 16 * uses(n))
            nc.scalar.mul(split_slot(phase, n)[0], ring[:, n % NSLOT, :], W_SCALE).then_inc(S["w_high"], 1)
            n_hi["act"] += 1

        def split_lo(dve, phase, n, shift=0, hshift=0):
            n_hi["dve"] += 1
            dve.wait_ge(S["w_high"], hshift + n_hi["dve"])
            nc.vector.scalar_tensor_tensor(split_slot(phase, n)[1], ring[:, n % NSLOT, :], W_SCALE,
                                           split_slot(phase, n)[0], ALU.mult, ALU.subtract).then_inc(w_used, 1)

        def split_act(act, phase):
            hi, lo = split_h(phase)
            for a in range(0, KT, 4):
                nc.scalar.copy(hi[:, a:a + 4, :], hT[:, a:a + 4, :]).then_inc(S["h_high"], 1)
            meet("act", act)

        def split_dve(dve, phase):
            hi, lo = split_h(phase)
            for a in range(0, KT, 4):
                n_h["dve"] += 1
                dve.wait_ge(S["h_high"], n_h["dve"])
                nc.vector.tensor_tensor(lo[:, a:a + 4, :], hT[:, a:a + 4, :], hi[:, a:a + 4, :], ALU.subtract)
            meet("dve", dve)

        n_h = {"dve": 0}
        def sigmoid(act, l, out, x, scale=1.0):
            zero, one = par[:, l, C_ZERO:C_ZERO + 1], par[:, l, C_ONE:C_ONE + 1]
            nc.scalar.activation(out, x, ACT.Exp, bias=zero, scale=-scale)
            act.drain()
            nc.scalar.activation(out, out, ACT.Ln, bias=one, scale=1.0)
            act.drain()
            return nc.scalar.activation(out, out, ACT.Exp, bias=zero, scale=-1.0)

        MROW = 2 * N_MOD
        PAD = MROW - 2
        padded = wk[:, 0:KT * (MROW + PAD)].rearrange("p (k c) -> p k c", k=KT)
        mrows = wk[0:MROW, 1024:1024 + WCOL]

        def mod_pe(pe, l):
            pe.wait_ge(S["c_padded"], l + 1)
            for j in range(N_MOD):
                pe.wait_ge(w_loaded[(base_mod[l] + j) % NSLOT], 16 * uses(base_mod[l] + j))
                w = slot3(base_mod[l] + j)
                for k in range(KT):
                    mm = nc.tensor.matmul(ps[0:MROW, 0:WCOL], padded[:, k, PAD - 2 * j:PAD - 2 * j + MROW], w[:, k, :],
                                          start=(j == 0 and k == 0), stop=(j == N_MOD - 1 and k == KT - 1))
                mm.then_inc(w_used, 1)
            meet("pe", pe)
            meet("pe", pe)
            for m in range(2):
                nc.tensor.matmul(ps[:, 512 + MROW * m:512 + MROW * (m + 1)], mrows[:, m * P:(m + 1) * P],
                                 ident[0:MROW, 0:MROW], start=True, stop=True)
            meet("pe", pe)
            meet("pe", pe)

        def mod_dve(dve, l):
            nc.vector.memset(padded, 0.0)
            dve.drain()
            nc.vector.tensor_copy(padded[:, :, PAD:MROW], cT[:, :, :])
            dve.drain().then_inc(S["c_padded"], 1)
            meet("dve", dve)
            nc.vector.tensor_copy(mrows, ps[0:MROW, 0:WCOL])
            meet("dve", dve)
            meet("dve", dve)
            for m in range(2):
                nc.vector.tensor_tensor(mod[:, m::2, :],
                                        ps[:, 512 + MROW * m:512 + MROW * (m + 1)].rearrange("p (j s) -> p j s", s=2),
                                        par[:, l, C_BMOD + m:C_BMOD + 48:2].unsqueeze(2).to_broadcast([P, N_MOD, 2]),
                                        ALU.add)
            dve.drain()
            for g in (16, 40):
                nc.vector.tensor_scalar(mod[:, g:g + 8, :], mod[:, g:g + 8, :], 1.0 / W_SCALE, None, ALU.mult)
            for w, c in ((0, C_N1), (1, C_N2)):
                nc.vector.scalar_tensor_tensor(s1[:, w], mod[:, 24 * w + 8:24 * w + 16, :], 1.0,
                                               par[:, l, c:c + 8].unsqueeze(2).to_broadcast([P, 8, 2]),
                                               ALU.add, ALU.mult)
            meet("dve", dve)

        def mod_act(act, l):
            for _ in range(4):
                meet("act", act)

        def norm_dve(dve, call):
            w = call % 2
            nc.vector.tensor_tensor(hT[:, :, :], xT[:, :, :], xT[:, :, :], ALU.mult).then_inc(S["ssq_in"], 1)
            dve.wait_ge(S["rstd_ready"], call + 1)
            nc.vector.tensor_tensor(hT[:, :, :], xT[:, :, :], tmp(0).unsqueeze(1).to_broadcast([P, KT, T]),
                                    ALU.mult).then_inc(S["normed_v"], 1)
            dve.wait_ge(S["normed_v"], call + 1)
            for k in range(0, KT, 2):
                for s, (a, b) in enumerate(STREAMS):
                    nc.vector.tensor_scalar(hT[:, k, a:b], hT[:, k, a:b], s1[:, w, k, s:s + 1],
                                            mod[:, 24 * w + k, s:s + 1], ALU.mult, ALU.add)
            meet("dve", dve)

        def norm_pe(pe, call):
            pe.wait_ge(S["ssq_in"], call + 1)
            for a, b in PIECES:
                for k in range(KT):
                    mm = nc.tensor.matmul(pair(0)[:, a:b], ones[:, :], hT[:, k, a:b],
                                          start=(k == 0), stop=(k == KT - 1))
            mm.then_inc(S["ssq_out"], 1)
            meet("pe", pe)

        def norm_act(act, call, l):
            w = call % 2
            act.wait_ge(S["ssq_out"], call + 1)
            nc.scalar.activation(tmp(1), pair(0), ACT.Ln, bias=par[:, l, C_EPS:C_EPS + 1], scale=1.0 / D)
            act.drain()
            nc.scalar.activation(tmp(0), tmp(1), ACT.Exp, bias=par[:, l, C_ZERO:C_ZERO + 1],
                                 scale=-0.5).then_inc(S["rstd_ready"], 1)
            act.wait_ge(S["normed_v"], call + 1)
            for k in range(1, KT, 2):
                for s, (a, b) in enumerate(STREAMS):
                    nc.scalar.activation(hT[:, k, a:b], hT[:, k, a:b], ACT.Identity,
                                         bias=mod[:, 24 * w + k, s:s + 1], scale=s1[:, w, k, s:s + 1])
            meet("act", act)

        N_PROD = NBLK + 5

        def in_pe(pe, l):
            hp = split_h("mix")
            for j in range(N_PROD):
                if j >= 4:
                    free = S["prod_free_v"] if j % 2 == 0 else S["prod_free_a"]
                    per = (N_PROD + 1) // 2 if j % 2 == 0 else N_PROD // 2
                    pe.wait_ge(free, l * per + (j - 4) // 2 + 1)
                if j < NBLK:
                    n, m = base_in[l] + j // 2, slice(j % 2 * P, j % 2 * P + P)
                    pe.wait_ge(w_used, n + 1)
                    w = w3k(split_slot("mix", n))
                    for a, b in PIECES:
                        for k in range(KT):
                            mm = mm3(pair(j)[:, a:b], [x[:, k, m] for x in w], [x[:, k, a:b] for x in hp],
                                     k == 0, k == KT - 1)
                    mm.then_inc(S["prod_ready"], 1)
                else:
                    t = slice((j - NBLK) * P, (j - NBLK + 1) * P)
                    for h, (c0, c1) in enumerate(((0, WCOL), (WCOL, V_COLS))):
                        n = base_in[l] + N_IN + h
                        pe.wait_ge(w_used, n + 1)
                        w = w3k(split_slot("mix", n))
                        for k in range(KT):
                            mm = mm3(pair(j)[:, c0:c1], [x[:, k, t] for x in hp], [x[:, k, 0:c1 - c0] for x in w],
                                     k == 0, k == KT - 1)
                    mm.then_inc(S["prod_ready"], 1)
            meet("pe", pe)

        def in_evac(who, eng, l):
            def split(i):
                if i >= N_IN + 2:
                    return
                if who == "act":
                    if i >= 2:
                        act_wait = l * N_PROD + 2 * (i - 1)
                        eng.wait_ge(S["prod_ready"], act_wait)
                    split_hi(eng, "mix", base_in[l] + i)
                else:
                    split_lo(eng, "mix", base_in[l] + i)
            split(0)
            split(1)
            for j in range(0 if who == "dve" else 1, N_PROD, 2):
                eng.wait_ge(S["prod_ready"], l * N_PROD + j + 1)
                src = pair(j) if j < NBLK else pair(j)[:, 0:V_COLS]
                dst = pj[:, j, :] if j < NBLK else vtok[:, j - NBLK, :]
                if who == "dve":
                    nc.vector.tensor_scalar(dst, src, 1.0 / W_SCALE, None, ALU.mult).then_inc(S["prod_free_v"], 1)
                else:
                    nc.scalar.mul(dst, src, 1.0 / W_SCALE).then_inc(S["prod_free_a"], 1)
                if j < NBLK:
                    split(j // 2 + 2)
            meet(who, eng)

        hn = {"pe": 0, "dve": 0, "act": 0}

        def head_norm_dve(dve, x, nb, finish):
            hn["dve"] += 1
            nc.vector.tensor_tensor(wk[:, 0:nb * T].rearrange("p (b t) -> p b t", b=nb), x, x,
                                    ALU.mult).then_inc(S["hn_sq"], 1)
            dve.wait_ge(S["hn_r"], hn["dve"])
            for b in range(nb):
                finish(b, tmp(4 + b))
            dve.drain()

        def head_norm_pe(pe, nb):
            hn["pe"] += 1
            pe.wait_ge(S["hn_sq"], hn["pe"])
            for b in range(nb):
                for p0, p1 in PIECES:
                    mm = nc.tensor.matmul(pair(b)[:, p0:p1], blk[:, :], tmp(b)[:, p0:p1], start=True, stop=True)
            mm.then_inc(S["hn_sum"], 1)

        def head_norm_act(act, l, nb, div):
            hn["act"] += 1
            act.wait_ge(S["hn_sum"], hn["act"])
            for b in range(nb):
                nc.scalar.activation(tmp(4 + b), pair(b), ACT.Ln, bias=par[:, l, C_EPS:C_EPS + 1], scale=1.0 / div)
            act.drain()
            r = wk[:, 4 * T:(4 + nb) * T]
            nc.scalar.activation(r, r, ACT.Exp, bias=par[:, l, C_ZERO:C_ZERO + 1], scale=-0.5).then_inc(S["hn_r"], 1)

        def gained(x, col):
            def f(b, r):
                g = col(b)
                nc.vector.scalar_tensor_tensor(x[:, b, :], x[:, b, :], g, r, ALU.mult, ALU.mult)
            return f

        QKN = [(SQ, 3), (NQ, 4)]

        def qk_dve(dve, l):
            def pc(c):
                return par[:, l, c:c + 1]
            head_norm_dve(dve, pj[:, SQ:SQ + 3, :], 3, gained(pj[:, SQ:SQ + 3, :],
                                                              lambda b: pc(C_SQN if b < 2 else C_SKN)))
            head_norm_dve(dve, pj[:, NQ:NQ + 4, :], 4, gained(pj[:, NQ:NQ + 4, :],
                                                              lambda b: pc(C_NQN if b < 2 else C_NKN)))
            dve.drain().then_inc(S["new_kv"], 1)
            dve.drain().then_inc(S["rope_ready"], 1)
            dve.wait_ge(S["rope_out"], l + 1)
            dve.wait_ge(S["cache_in"], 80 * (l + 1))
            x = pj[:, SQ:SQ + 3, NP_TOK:T]
            r = wk[:, 0:3 * NS_TOK].rearrange("p (b t) -> p b t", b=3)
            nc.vector.tensor_tensor(r, ps[:, 0:3 * 512].rearrange("p (b t) -> p b t", b=3),
                                    cossin[:, 1, :].unsqueeze(1).to_broadcast([P, 3, NS_TOK]), ALU.mult)
            nc.vector.tensor_tensor(x, x, cossin[:, 0, :].unsqueeze(1).to_broadcast([P, 3, NS_TOK]), ALU.mult)
            dve.drain()
            nc.vector.tensor_tensor(x, x, r, ALU.add)
            meet("dve", dve)

        def qk_pe(pe, l):
            head_norm_pe(pe, 3)
            head_norm_pe(pe, 4)
            pe.wait_ge(S["rope_ready"], l + 1)
            for b in range(3):
                mm = nc.tensor.matmul(bank(b), rot[:, :], pj[:, SQ + b, NP_TOK:T], start=True, stop=True)
            mm.then_inc(S["rope_out"], 1)
            meet("pe", pe)

        def qk_act(act, l):
            head_norm_act(act, l, 3, L)
            head_norm_act(act, l, 4, L)
            meet("act", act)

        def decay_a_pe(pe, l):
            for j in range(4):
                for a, b in PIECES:
                    nc.tensor.matmul(pair(j)[:, a:b], wup[:, l, j, :], pj[0:32, SMALL, a:b], start=True, stop=True)
            meet("pe", pe)
            meet("pe", pe)
            meet("pe", pe)
            meet("pe", pe)

        def decay_a_dve(dve, l):
            meet("dve", dve)
            for j in range(4):
                bup = par[:, l, C_BUP + j:C_BUP + j + 1]
                nc.vector.tensor_scalar(scan[:, j, :], pair(j), bup, 0.0, ALU.add, ALU.min)
                nc.vector.tensor_scalar(tmp(j), pair(j), bup, None, ALU.add)
            dve.drain()
            z = wk[:, 0:4 * T]
            nc.vector.scalar_tensor_tensor(z, scr[:, 0:4 * T], 2.0, z, ALU.mult, ALU.subtract)
            meet("dve", dve)
            meet("dve", dve)
            la = wk[:, 4 * T:8 * T]
            nc.vector.tensor_tensor(la, scr[:, 0:4 * T], wk[:, 0:4 * T], ALU.subtract)
            dve.drain()
            for j in range(4):
                scan_chunks(scan[:, j, :], la[:, j * T:(j + 1) * T], j // 2)
            meet("dve", dve)

        def scan_chunks(out, data, back, p0=0, p1=P):
            m = cmask[p0:p1, back, :]
            if back:
                nc.vector.tensor_tensor_scan(out[p0:p1, ::-1], m[:, ::-1], data[p0:p1, ::-1], 0.0, ALU.mult, ALU.add)
            else:
                nc.vector.tensor_tensor_scan(out[p0:p1, :], m, data[p0:p1, :], 0.0, ALU.mult, ALU.add)

        def decay_a_act(act, l):
            meet("act", act)
            meet("act", act)
            z = wk[:, 0:4 * T]
            nc.scalar.activation(z, z, ACT.Exp, bias=par[:, l, C_ZERO:C_ZERO + 1])
            act.drain()
            nc.scalar.activation(z, z, ACT.Ln, bias=par[:, l, C_ONE:C_ONE + 1], scale=1.0)
            meet("act", act)
            meet("act", act)

        STEPS = ((0, 2), (NP_TOK, 8))

        def chunks(i, s, ahead=0):
            off, n = STEPS[s]
            return (i * L + (off + ahead * L), i * (-L) + (off + (n - 1 - ahead) * L))

        spare = pj[:, 0:8, :].rearrange("p a b -> p (a b)")[:, 4 * 16 * L:4 * 16 * L + 2 * 256].rearrange(
            "p (n c) -> p n c", n=2)

        def buf(i):
            return work[:, i, :] if i < 20 else spare[:, i - 20, :]

        def w4(i):
            return buf(i).rearrange("p (d g c) -> p d g c", d=2, g=2)

        def pd(d, b, j=0):
            o = (4 * d + b) * 512 + P * j
            return ps[:, o:o + P].rearrange("p (g c) -> p g c", g=2)

        def wd(i, d):
            return buf(i)[:, P * d:P * d + P]

        def fd(d, b, j=0, n=1):
            o = (4 * d + b) * 512 + P * j
            return ps[:, o:o + P * n]

        def units(d):
            for g in range(2):
                for p in range(2):
                    yield g, slice(64 * p, 64 * p + 64)

        A_E1, A_E2, A_QD, A_KI, A_KE, A_VS, A_AM, A_KES, A_VTOK = range(9)

        def gla_act(act, l, s, it, i):
            zero = par[:, l, C_ZERO:C_ZERO + 1]
            for d, t in enumerate(chunks(i, s)):
                act.wait_ge(S["gla_done"][d], it + 1)
                c = scan[:, 2 * d:2 * d + 2, bass.ds(t, L)]
                nc.scalar.activation(w4(A_E1)[:, d], c, ACT.Exp, bias=zero, scale=1.0 / 16)
                nc.scalar.activation(w4(A_E2)[:, d], c, ACT.Exp, bias=zero, scale=-1.0 / 16).then_inc(S["gla_exp"][d], 1)
            for d in range(2):
                act.wait_ge(S["gla_prod"][d], it + 1)
                nc.scalar.copy(wd(A_KES, d), fd(d, 1)).then_inc(S["gla_evac_a"][d], 1)

        def gla_dve(dve, l, s, it, i):
            ts = chunks(i, s)
            el = [cols[:, 2 * d:2 * d + 2].unsqueeze(2).to_broadcast([P, 2, L]) for d in range(2)]
            for d, t in enumerate(ts):
                q, k, v = (pj[:, b:b + 2, bass.ds(t, L)] for b in (AQ, AK, AV))
                dve.wait_ge(S["gla_exp"][d], it + 1)
                last = L - 1 if d == 0 else 0
                nc.vector.tensor_copy(cols[:, 2 * d:2 * d + 2].unsqueeze(2), w4(A_E1)[:, d, :, last:last + 1])
                nc.vector.tensor_tensor(w4(A_KI)[:, d], k, w4(A_E2)[:, d], ALU.mult)
                nc.vector.scalar_tensor_tensor(w4(A_QD)[:, d], q, L ** -0.5, w4(A_E1)[:, d], ALU.mult, ALU.mult)
                nc.vector.tensor_copy(w4(A_VS)[:, d], v)
                dve.drain()
                nc.vector.tensor_tensor(w4(A_KE)[:, d], w4(A_KI)[:, d], el[d], ALU.mult).then_inc(S["gla_staged"][d], 1)
            for d in range(2):
                dve.wait_ge(S["gla_prod"][d], it + 1)
                nc.vector.tensor_tensor(w4(A_AM)[:, d], pd(d, 0), incl[:, d], ALU.mult)
                nc.vector.tensor_copy(wd(A_VTOK, d), fd(d, 0, 1)).then_inc(S["gla_evac_v"][d], 1)
            for d, t in enumerate(ts):
                st = st_a[s][:, d]
                o = hT[:, OA:OA + 2, bass.ds(t, L)]
                dve.wait_ge(S["gla_out"][d], it + 1)
                nc.vector.tensor_tensor(st, st, el[d], ALU.mult)
                nc.vector.tensor_tensor(o, o, pd(d, 2), ALU.add)
                dve.drain()
                nc.vector.tensor_tensor(st, st, pd(d, 2, 1), ALU.add).then_inc(S["gla_done"][d], 1)

        def waited(pe, out):
            nc.tensor.matmul(out, incl[:].rearrange("p d g c -> p (d g c)")[:, 0:P], incl[:, 0, 0, :],
                             start=True, stop=True)

        def corner(d, b):
            o = (4 * d + b) * 512 + 448
            return ps[:, o:o + L]

        def gla_pe(pe, s, it):
            for d in range(2):
                pe.wait_ge(S["gla_staged"][d], it + 1)
                waited(pe, corner(d, 0))
                for g, h in units(d):
                    nc.tensor.matmul(pd(d, 0)[h, g], w4(A_KI)[h, d, g], w4(A_QD)[h, d, g], start=True, stop=True)
                    nc.tensor.matmul(pd(d, 0, 1)[h, g], w4(A_VS)[h, d, g], ident[h, h], start=True, stop=True)
                    mm = nc.tensor.matmul(pd(d, 1)[h, g], w4(A_KE)[h, d, g], ident[h, h], start=True, stop=True)
                mm.then_inc(S["gla_prod"][d], 1)
            for d in range(2):
                pe.wait_ge(S["gla_evac_v"][d], it + 1)
                pe.wait_ge(S["gla_evac_a"][d], it + 1)
                pe.wait_ge(S["gla_done"][d], it + 1)
                waited(pe, corner(d, 2))
                for g, h in units(d):
                    nc.tensor.matmul(pd(d, 2)[h, g], w4(A_VTOK)[h, d, g], w4(A_AM)[h, d, g], start=True, stop=False)
                    nc.tensor.matmul(pd(d, 2)[h, g], st_a[s][h, d, g], w4(A_QD)[h, d, g], start=False, stop=True)
                    mm = nc.tensor.matmul(pd(d, 2, 1)[h, g], w4(A_KES)[h, d, g], w4(A_VTOK)[h, d, g],
                                          start=True, stop=True)
                mm.then_inc(S["gla_out"][d], 1)

        def loop_steps(eng, l, body):
            for s, (_, n) in enumerate(STEPS):
                first = l * 10 + (0 if s == 0 else STEPS[0][1])
                with eng.Fori(0, n) as i:
                    body(s, i + first, i)

        def scan_out_dve(dve, l, ob, gate, gain):
            meet("dve", dve)
            x = hT[:, ob:ob + 2, :]
            gt = pj[:, gate:gate + 2, :]
            k = scan_out_n["dve"] = scan_out_n["dve"] + 1
            head_norm_dve(dve, x, 2, gained(x, lambda b: par[:, l, gain:gain + 1]))
            dve.wait_ge(S["gate_exp"], k)
            e = wk[:, 2 * T:4 * T]
            nc.vector.tensor_tensor(x, x, gt, ALU.mult)
            dve.drain()
            nc.vector.tensor_tensor(x, x, e.rearrange("p (b t) -> p b t", b=2), ALU.mult)
            meet("dve", dve)

        def scan_out_pe(pe):
            meet("pe", pe)
            head_norm_pe(pe, 2)
            meet("pe", pe)

        def scan_out_act(act, l, gate):
            meet("act", act)
            sigmoid(act, l, wk[:, 2 * T:4 * T], pj[:, gate:gate + 2, :].rearrange("p b t -> p (b t)")).then_inc(
                S["gate_exp"], 1)
            head_norm_act(act, l, 2, L)
            meet("act", act)

        scan_out_n = {"dve": 0}

        CONV_E = ((wk[:, 6 * T:8 * T], pj[:, 5:7, :].rearrange("p b t -> p (b t)")) * 2)[0:3]

        def row(n):
            return pj[:, n, :]

        def conv_dve(dve, l):
            z = row(0)
            nc.vector.tensor_scalar(z, pj[:, SMALL, :], par[:, l, C_DTB:C_DTB + 1], None, ALU.add)
            dve.drain()
            nc.vector.tensor_scalar(row(1), z, 0.0, 2.0, ALU.min, ALU.mult)
            dve.drain()
            nc.vector.tensor_tensor(row(1), row(1), z, ALU.subtract).then_inc(S["row_in"], 1)

            def conv(q):
                for b in (2 * q, 2 * q + 1):
                    nc.vector.tensor_scalar(tmp(b), pj[:, DQ + b, :], tap(b, 1), None, ALU.mult)
                dve.drain()
                for b in (2 * q, 2 * q + 1):
                    for a, e in STREAMS:
                        nc.vector.scalar_tensor_tensor(tmp(b)[:, a + 1:e], pj[:, DQ + b, a:e - 1], tap(b, 0),
                                                       tmp(b)[:, a + 1:e], ALU.mult, ALU.add)
                dve.drain()
                for b in (2 * q, 2 * q + 1):
                    for a, e in STREAMS:
                        nc.vector.scalar_tensor_tensor(tmp(b)[:, a:e - 1], pj[:, DQ + b, a + 1:e], tap(b, 2),
                                                       tmp(b)[:, a:e - 1], ALU.mult, ALU.add)
                dve.drain().then_inc(S["conv_ready"], 1)

            def tap(b, c):
                return par[:, l, C_CONV + 3 * b + c:C_CONV + 3 * b + c + 1]

            def silu(q):
                dve.wait_ge(S["conv_exp"], 3 * l + q + 1)
                x, y = pj[:, DQ + 2 * q:DQ + 2 * q + 2, :], wk[:, 2 * q * T:(2 * q + 2) * T]
                nc.vector.tensor_tensor(x, y.rearrange("p (b t) -> p b t", b=2),
                                        CONV_E[q].rearrange("p (b t) -> p b t", b=2), ALU.mult)
                dve.drain()
                if q < 2:
                    nc.vector.tensor_tensor(y.rearrange("p (b t) -> p b t", b=2), x, x,
                                            ALU.mult).then_inc(S["conv_sq"], 1)

            def spread(n):
                dve.wait_ge(S["spread_ready"], 2 * l + n + 1)
                for j in range(0, 4, 2):
                    nc.vector.tensor_copy(scan[:, 4 - 4 * n + j, :], pair(j)).then_inc(S["spread_free_v"], 1)

            conv(0)
            conv(1)
            dve.wait_ge(S["row_exp"], l + 1)
            nc.vector.scalar_tensor_tensor(z, z, 0.0, row(1), ALU.max, ALU.add)
            dve.drain()
            nc.vector.tensor_scalar(z, z, row(3)[:, 0:1], -1.0, ALU.mult, ALU.mult)
            dve.drain()
            scan_chunks(row(4), z, 0, 64, 96)
            scan_chunks(row(4), z, 1, 96, 128)
            dve.drain().then_inc(S["row_scanned"], 1)
            silu(0)
            spread(0)
            conv(2)
            silu(1)
            spread(1)
            for q in range(2):
                dve.wait_ge(S["conv_r"], 2 * l + q + 1)
                for b in (2 * q, 2 * q + 1):
                    x = pj[:, DQ + b, :]
                    nc.vector.scalar_tensor_tensor(x, x, L ** -0.5 if q == 0 else 1.0, tmp(b), ALU.mult, ALU.mult)
                if q == 0:
                    silu(2)
            meet("dve", dve)

        def conv_pe(pe, l):
            for n, (r, rows_, src) in enumerate(((R_BETA, 8, row(2)), (None, 4, row(4)))):
                pe.wait_ge(S["row_exp" if n == 0 else "row_scanned"], l + 1)
                if n:
                    pe.wait_ge(S["spread_free_v"], 4 * l + 2)
                    pe.wait_ge(S["spread_free_a"], 4 * l + 2)
                for j in range(4):
                    r0 = R_DEC[j // 2] if r is None else r
                    for a, b in PIECES:
                        mm = nc.tensor.matmul(pair(j)[:, a:b], sel[r0:r0 + rows_, j, :], src[r0:r0 + rows_, a:b],
                                              start=True, stop=True)
                mm.then_inc(S["spread_ready"], 1)
            pe.wait_ge(S["spread_free_v"], 4 * l + 4)
            pe.wait_ge(S["spread_free_a"], 4 * l + 4)
            for q in range(2):
                pe.wait_ge(S["conv_sq"], 2 * l + q + 1)
                for b in (2 * q, 2 * q + 1):
                    for p0, p1 in PIECES:
                        mm = nc.tensor.matmul(pair(b)[:, p0:p1], blk[:, :], tmp(b)[:, p0:p1], start=True, stop=True)
                mm.then_inc(S["conv_sum"], 1)
            meet("pe", pe)

        def conv_act(act, l):
            zero, one = par[:, l, C_ZERO:C_ZERO + 1], par[:, l, C_ONE:C_ONE + 1]

            def spread(n):
                act.wait_ge(S["spread_ready"], 2 * l + n + 1)
                for j in range(1, 4, 2):
                    nc.scalar.copy(scan[:, 4 - 4 * n + j, :], pair(j)).then_inc(S["spread_free_a"], 1)

            act.wait_ge(S["row_in"], l + 1)
            nc.scalar.activation(row(1), row(1), ACT.Exp, bias=zero)
            nc.scalar.activation(row(3)[:, 0:1], par[:, l, C_ALOG:C_ALOG + 1], ACT.Exp, bias=zero, scale=1.0)
            sigmoid(act, l, row(2), pj[:, SMALL, :])
            nc.scalar.activation(row(1), row(1), ACT.Ln, bias=one, scale=1.0)
            act.drain().then_inc(S["row_exp"], 1)
            for q in range(3):
                act.wait_ge(S["conv_ready"], 3 * l + q + 1)
                if q == 2:
                    act.wait_ge(S["conv_sq"], 2 * l + 1)
                sigmoid(act, l, CONV_E[q], wk[:, 2 * q * T:(2 * q + 2) * T]).then_inc(S["conv_exp"], 1)
                if q == 1:
                    spread(0)
            spread(1)
            for q in range(2):
                act.wait_ge(S["conv_sum"], 2 * l + q + 1)
                for b in (2 * q, 2 * q + 1):
                    nc.scalar.activation(tmp(b), pair(b), ACT.Ln, bias=par[:, l, C_EPS:C_EPS + 1], scale=1.0)
                act.drain()
                r = wk[:, 2 * q * T:(2 * q + 2) * T]
                nc.scalar.activation(r, r, ACT.Exp, bias=zero, scale=-0.5).then_inc(S["conv_r"], 1)
            meet("act", act)

        (D_Q, D_K, D_KE, D_VB, D_KB, D_QD, D_GB, D_BB, D_E, D_DF, D_AT, D_QK, D_KES, D_VBS, D_ATL, D_X, D_XT, D_US,
         D_R, D_U, D_EG, D_LV1) = range(22)

        def w3(n, d):
            return buf(n)[:, P * d:P * d + P].rearrange("p (g c) -> p g c", g=2)

        def bc(c):
            return c.unsqueeze(2).to_broadcast([P, 2, L])

        D_LV = (D_ATL, D_LV1)

        def alternate(x, v, which):
            return x.rearrange("p (n two s) -> p n two s", two=2, s=2 ** v)[:, :, which, :]

        def gdn_front_dve(dve, l, s, it, i, ahead, part):
            ts = chunks(i, s, ahead)
            tt = nc.vector.tensor_tensor
            if part == 0:
                for d, t in enumerate(ts):
                    at = bass.ds(t, L)
                    nc.vector.tensor_copy(w3(D_GB, d), scan[:, 2 * d:2 * d + 2, at])
                    nc.vector.tensor_copy(w3(D_K, d), pj[:, DK:DK + 2, at])
                    nc.vector.tensor_copy(w3(D_BB, d), scan[:, 4 + 2 * d:6 + 2 * d, at])
                    tt(w3(D_VB, d), pj[:, DV:DV + 2, at], scan[:, 4 + 2 * d:6 + 2 * d, at], ALU.mult)
            elif part == 1:
                for d, t in enumerate(ts):
                    for h in range(2):
                        hs = slice(64 * h, 64 * h + 64)
                        tt(w3(D_DF, d)[hs], w3(D_GB, d)[hs], ident[hs, hs].unsqueeze(1).to_broadcast([64, 2, L]),
                           ALU.mult)
                    last = L - 1 if d == 0 else 0
                    nc.vector.tensor_copy(cols[:, 4 + 2 * d:6 + 2 * d].unsqueeze(2), w3(D_GB, d)[:, :, last:last + 1])
                    nc.vector.tensor_copy(w3(D_Q, d), pj[:, DQ:DQ + 2, bass.ds(t, L)])
                dve.drain()
                for d in range(2):
                    nc.vector.tensor_reduce(cols[:, 2 * d:2 * d + 2], w3(D_DF, d), AX.X, ALU.add)
                    tt(w3(D_E, d), bc(cols[:, 4 + 2 * d:6 + 2 * d]), w3(D_GB, d), ALU.subtract)
            elif part == 2:
                for d in range(2):
                    tt(w3(D_DF, d), w3(D_GB, d), bc(cols[:, 2 * d:2 * d + 2]), ALU.subtract)
                dve.drain()
                for d in range(2):
                    tt(w3(D_DF, d), w3(D_DF, d), incl[:, d], ALU.mult).then_inc(S["gdn_dif"][d], 1)
            elif part == 3:
                for d in range(2):
                    dve.wait_ge(S["gdn_staged_a"][d], it + 1)
                    tt(wd(D_KE, d), wd(D_K, d), wd(D_E, d), ALU.mult).then_inc(S["gdn_staged_v"][d], 1)
            else:
                for d in range(2):
                    tt(wd(D_KB, d), wd(D_K, d), wd(D_EG, d), ALU.mult)
                    tt(w3(D_DF, d), w3(D_DF, d), incl[:, d], ALU.mult)
                    for h in range(2):
                        hs = slice(64 * h, 64 * h + 64)
                        nc.vector.tensor_copy(w3(D_X, d)[hs], ident[hs, hs].unsqueeze(1).to_broadcast([64, 2, L]))
                dve.drain()
                for d in range(2):
                    tt(wd(D_KB, d), wd(D_KB, d), wd(D_BB, d), ALU.mult)
                    tt(wd(D_BB, d), wd(D_BB, d), wd(D_DF, d), ALU.mult)

        def gdn_dve(dve, l, s, it, i, front):
            ts = chunks(i, s)
            tt = nc.vector.tensor_tensor
            for d in range(2):
                dve.wait_ge(S["gdn_prod"][d], it + 1)
                tt(wd(D_AT, d), fd(d, 0), wd(D_BB, d), ALU.mult)
                tt(wd(D_QK, d), fd(d, 0, 1), wd(D_DF, d), ALU.mult)
                dve.drain()
                tt(w3(D_LV[0], d), w3(D_AT, d), lvl[:, 0, d], ALU.mult).then_inc(S["gdn_at"][d], 1)
            for d in range(2):
                tt(wd(D_QD, d), wd(D_EG, d), wd(D_Q, d), ALU.mult)
                nc.vector.tensor_copy(cols[:, 8 + 2 * d:10 + 2 * d], cols[:, 12 + 2 * d:14 + 2 * d])
            dve.drain()
            for d in range(2):
                tt(wd(D_XT, d), wd(D_X, d), wd(D_LV[0], d), ALU.subtract)
            for v in range(6):
                for d in range(2):
                    if v < 5:
                        tt(w3(D_LV[(v + 1) % 2], d), w3(D_AT, d), lvl[:, v + 1, d], ALU.mult)
                    if v == 0:
                        dve.wait_ge(S["gdn_u"][d], it * 6 + 1)
                        tt(wd(D_X, d), wd(D_X, d), fd(d, 2), ALU.subtract).then_inc(S["gdn_xs"][d], 1)
                        continue
                    dve.wait_ge(S["gdn_x"][d], it * 5 + v)
                    if v < 5:
                        x = alternate(wd(D_X, d), v, d)
                        tt(x, x, alternate(fd(d, 3), v, d), ALU.subtract)
                    x = alternate(wd(D_XT, d), v, 1 - d)
                    tt(x, x, alternate(fd(d, 3, 1), v, 1 - d), ALU.subtract).then_inc(S["gdn_xs"][d], 1)
                if v < 4:
                    front(v)
                dve.drain()
            for d in range(2):
                dve.wait_ge(S["gdn_tok"][d], it + 1)
                dve.wait_ge(S["gdn_r0"][d], it + 1)
                tt(wd(D_R, d), wd(D_VBS, d), fd(d, 0, 2), ALU.subtract).then_inc(S["gdn_rs"][d], 1)
            front(4)
            for d, t in enumerate(ts):
                st = st_d[s][:, d]
                o = hT[:, OD:OD + 2, bass.ds(t, L)]
                dve.wait_ge(S["gdn_o"][d], it + 1)
                tt(st, st, bc(cols[:, 8 + 2 * d:10 + 2 * d]), ALU.mult)
                tt(o, o, pd(d, 2), ALU.add)
                dve.drain()
                tt(st, st, pd(d, 2, 1), ALU.add).then_inc(S["gdn_done"][d], 1)

        def gdn_front_act(act, l, it):
            zero = par[:, l, C_ZERO:C_ZERO + 1]
            for d in range(2):
                act.wait_ge(S["gdn_dif"][d], it + 1)
                nc.scalar.activation(wd(D_E, d), wd(D_E, d), ACT.Exp, bias=zero)
                nc.scalar.activation(wd(D_DF, d), wd(D_DF, d), ACT.Exp, bias=zero)
                nc.scalar.activation(cols[:, 12 + 2 * d:14 + 2 * d], cols[:, 4 + 2 * d:6 + 2 * d], ACT.Exp, bias=zero)
                nc.scalar.activation(wd(D_EG, d), wd(D_GB, d), ACT.Exp, bias=zero).then_inc(S["gdn_staged_a"][d], 1)

        def gdn_act(act, l, s, it, i, front):
            for d in range(2):
                act.wait_ge(S["gdn_prod"][d], it + 1)
                nc.scalar.copy(wd(D_KES, d), fd(d, 1))
                nc.scalar.copy(wd(D_VBS, d), fd(d, 1, 1)).then_inc(S["gdn_tok"][d], 1)
            for v in range(1, 6):
                for d in range(2):
                    act.wait_ge(S["gdn_u"][d], it * 6 + (v + 1))
                    nc.scalar.copy(wd(D_US, d), fd(d, 2)).then_inc(S["gdn_us"][d], 1)
                if v == 3:
                    front()
            for d in range(2):
                act.wait_ge(S["gdn_u1"][d], it + 1)
                nc.scalar.copy(wd(D_U, d), fd(d, 1, 2)).then_inc(S["gdn_us1"][d], 1)

        def gdn_front_pe(pe, it):
            for d in range(2):
                pe.wait_ge(S["gdn_staged_v"][d], it + 1)
                waited(pe, corner(d, 0))
                for g, h in units(d):
                    nc.tensor.matmul(pd(d, 0)[h, g], w4(D_K)[h, d, g], w4(D_K)[h, d, g], start=True, stop=True)
                    nc.tensor.matmul(pd(d, 0, 1)[h, g], w4(D_K)[h, d, g], w4(D_Q)[h, d, g], start=True, stop=True)
                    nc.tensor.matmul(pd(d, 1)[h, g], w4(D_KE)[h, d, g], ident[h, h], start=True, stop=True)
                    mm = nc.tensor.matmul(pd(d, 1, 1)[h, g], w4(D_VB)[h, d, g], ident[h, h], start=True, stop=True)
                mm.then_inc(S["gdn_prod"][d], 1)

        def gdn_pe(pe, s, it, front):
            for v in range(6):
                for d in range(2):
                    if v == 0:
                        pe.wait_ge(S["gdn_at"][d], it + 1)
                    else:
                        pe.wait_ge(S["gdn_xs"][d], it * 6 + v)
                    waited(pe, corner(d, 2))
                    for g, h in units(d):
                        mm = nc.tensor.matmul(pd(d, 2)[h, g], w4(D_LV[v % 2])[h, d, g],
                                              ident[h, h] if v == 0 else w4(D_X)[h, d, g], start=True, stop=True)
                    mm.then_inc(S["gdn_u"][d], 1)
                for d in range(2):
                    if v == 0:
                        continue
                    pe.wait_ge(S["gdn_us"][d], it * 5 + v)
                    waited(pe, corner(d, 3))
                    for g, h in units(d):
                        if v < 5:
                            nc.tensor.matmul(alternate(pd(d, 3)[h, g], v, d), w4(D_XT)[h, d, g],
                                             alternate(w4(D_US)[h, d, g], v, d), start=True, stop=True)
                        mm = nc.tensor.matmul(alternate(pd(d, 3, 1)[h, g], v, 1 - d), w4(D_US)[h, d, g],
                                              alternate(w4(D_XT)[h, d, g], v, 1 - d), start=True, stop=True)
                    mm.then_inc(S["gdn_x"][d], 1)
                if v == 0:
                    for d in range(2):
                        pe.wait_ge(S["gdn_at"][d], it + 1)
                        pe.wait_ge(S["gdn_done"][d], it + 1)
                        waited(pe, corner(d, 0))
                        for g, h in units(d):
                            mm = nc.tensor.matmul(pd(d, 0, 2)[h, g], w4(D_KB)[h, d, g], st_d[s][h, d, g],
                                                  start=True, stop=True)
                        mm.then_inc(S["gdn_r0"][d], 1)
            for d in range(2):
                pe.wait_ge(S["gdn_tok"][d], it + 1)
                pe.wait_ge(S["gdn_xs"][d], it * 6 + 6)
                pe.wait_ge(S["gdn_rs"][d], it + 1)
                waited(pe, corner(d, 1))
                for g, h in units(d):
                    mm = nc.tensor.matmul(pd(d, 1, 2)[h, g], w4(D_XT)[h, d, g], w4(D_R)[h, d, g],
                                          start=True, stop=True)
                mm.then_inc(S["gdn_u1"][d], 1)
            for d in range(2):
                pe.wait_ge(S["gdn_us1"][d], it + 1)
                waited(pe, corner(d, 2))
                for g, h in units(d):
                    nc.tensor.matmul(pd(d, 2)[h, g], st_d[s][h, d, g], w4(D_QD)[h, d, g], start=True, stop=False)
                    nc.tensor.matmul(pd(d, 2)[h, g], w4(D_U)[h, d, g], w4(D_QK)[h, d, g], start=False, stop=True)
                    mm = nc.tensor.matmul(pd(d, 2, 1)[h, g], w4(D_KES)[h, d, g], w4(D_U)[h, d, g],
                                          start=True, stop=True)
                mm.then_inc(S["gdn_o"][d], 1)
            front()

        def loop_pipelined(eng, l, front, step):
            for s, (_, n) in enumerate(STEPS):
                first = l * 10 + (0 if s == 0 else STEPS[0][1])
                front(s, first, 0, 0)
                with eng.Fori(0, n - 1) as i:
                    step(s, i + first, i, True)
                step(s, first + n - 1, n - 1, False)

        def gdn_all_dve(dve, l):
            def front(s, it, i, ahead):
                for part in range(5):
                    gdn_front_dve(dve, l, s, it, i, ahead, part)
                    dve.drain()
            loop_pipelined(dve, l, front, lambda s, it, i, more: gdn_dve(
                dve, l, s, it, i, lambda part: gdn_front_dve(dve, l, s, it + 1, i, 1, part) if more else None))

        def gdn_all_act(act, l):
            loop_pipelined(act, l, lambda s, it, i, ahead: gdn_front_act(act, l, it),
                           lambda s, it, i, more: gdn_act(
                               act, l, s, it, i, lambda: gdn_front_act(act, l, it + 1) if more else None))

        def gdn_all_pe(pe, l):
            loop_pipelined(pe, l, lambda s, it, i, ahead: gdn_front_pe(pe, it),
                           lambda s, it, i, more: gdn_pe(
                               pe, s, it, lambda: gdn_front_pe(pe, it + 1) if more else None))

        def attn_units():
            for t in range(5):
                for kind in "BC":
                    for h in range(4):
                        if kind == "B":
                            p, q, k, o, c, vc = h // 2, SQ + h % 2, SK, OB + h % 2, 0, L * (h // 2)
                            loc = [0] if t == 0 else list(range(max(1, t - 1), min(4, t + 1) + 1))
                        else:
                            p, q, k, o, c, vc = h % 2, NQ + h // 2, NK + h // 2, OC + h // 2, 1 + h // 2, P + L * h
                            loc = [0] if t == 0 else [1, 2, 3, 4]
                        yield dict(t=t, kind=kind, h=h, hs=slice(64 * p, 64 * p + 64), q=q, k=k, o=o, c=c, vc=vc,
                                   loc=loc, ctx=0 if t == 0 else 2, nl=P * len(loc), n=P * len(loc) + (PAST if t else 0))

        UN = list(attn_units())
        NU = len(UN)

        def lbuf(u):
            return wk[:, (u % 2) * 800:(u % 2) * 800 + 800]

        def ptbuf(u):
            return wk[:, 1600 + (u % 2) * 768:1600 + (u % 2) * 768 + 768]

        def attn_scores(pe, u, base):
            x = UN[u]
            if u >= 2:
                pe.wait_ge(S["lg_ready"], base + u - 1)
            q = pj[x["hs"], x["q"], x["t"] * P:(x["t"] + 1) * P]
            b = 2 * (u % 2)
            mm = nc.tensor.matmul(bank(b)[:, 0:x["nl"]], q,
                                  pj[x["hs"], x["k"], x["loc"][0] * P:(x["loc"][-1] + 1) * P], start=True, stop=True)
            if x["ctx"]:
                mm = nc.tensor.matmul(bank(b + 1)[:, 0:PAST], q, ck[x["hs"], x["c"], :], start=True, stop=True)
            mm.then_inc(S["sc_ready"], 1)

        def attn_pv(pe, u, base):
            x = UN[u]
            pe.wait_ge(S["pt_copied"], base + u + 1)
            if u >= 2:
                pe.wait_ge(S["pv_free"], base + u - 1)
            vs = [vtok[:, t, x["vc"]:x["vc"] + L] for t in x["loc"]] + [cv[:, j, x["vc"]:x["vc"] + L]
                                                                       for j in range(x["ctx"])]
            for j, v in enumerate(vs):
                mm = nc.tensor.matmul(bank(6 + u % 2)[x["hs"], 0:P], v, ptbuf(u)[:, j * P:(j + 1) * P],
                                      start=(j == 0), stop=(j == len(vs) - 1))
            mm.then_inc(S["pv_ready"], 1)

        def attn_pe(pe, l):
            base = l * NU
            pe.wait_ge(S["cache_in"], 80 * (l + 1))
            attn_scores(pe, 0, base)
            for u in range(NU):
                if u + 1 < NU:
                    attn_scores(pe, u + 1, base)
                pe.wait_ge(S["pn_ready"], base + u + 1)
                if base + u > 0:
                    pe.wait_ge(S["pt_copied"], base + u)
                for j in range(UN[u]["n"] // P):
                    mm = nc.tensor.transpose(ps[:, 4 * 512 + j * P:4 * 512 + (j + 1) * P],
                                             lbuf(u)[:, j * P:(j + 1) * P], ident[:, :])
                mm.then_inc(S["pt_ready"], 1)
                if u > 0:
                    attn_pv(pe, u - 1, base)
            attn_pv(pe, NU - 1, base)
            meet("pe", pe)

        def attn_dve(dve, l):
            base = l * NU
            dve.wait_ge(S["rpb_loaded"], 16 * (l + 1))
            r3 = rpb.rearrange("p h m c -> p (h m) c")
            nc.vector.tensor_tensor(r3, r3, nmask[:, 0, :].unsqueeze(1).to_broadcast([P, 64, L]), ALU.mult)
            dve.drain()
            nc.vector.tensor_tensor(r3, r3, nmask[:, 1, :].unsqueeze(1).to_broadcast([P, 64, L]), ALU.add)
            dve.drain()

            def logits(u):
                x = UN[u]
                if u >= 2:
                    dve.wait_ge(S["pt_ready"], base + u - 1)
                dve.wait_ge(S["sc_ready"], base + u + 1)
                lg, b, nl, n = lbuf(u), 2 * (u % 2), x["nl"], x["n"]
                if x["t"] == 0:
                    nc.vector.tensor_scalar(lg[:, 0:nl], bank(b)[:, 0:nl], L ** -0.5, None, ALU.mult)
                elif x["kind"] == "B":
                    m0 = (x["loc"][0] - x["t"] + 1) * P
                    nc.vector.scalar_tensor_tensor(lg[:, 0:nl], bank(b)[:, 0:nl], L ** -0.5, swamask[:, m0:m0 + nl],
                                                   ALU.mult, ALU.add)
                else:
                    t = x["t"] - 1
                    bias = rpb[:, x["h"], 7 - 2 * t:15 - 2 * t, :].rearrange("p m c -> p (m c)")
                    nc.vector.scalar_tensor_tensor(lg[:, 0:nl], bank(b)[:, 0:nl], L ** -0.5, bias, ALU.mult, ALU.add)
                if x["ctx"]:
                    nc.vector.tensor_scalar(lg[:, nl:n], bank(b + 1)[:, 0:PAST], L ** -0.5, None, ALU.mult)
                w = n
                if x["kind"] == "B":
                    c = C_SINK + x["h"]
                    nc.vector.tensor_copy(lg[:, n:n + 1], par[:, l, c:c + 1])
                    w = n + 1
                dve.drain()
                a = 4 * (u % 2)
                nc.vector.tensor_reduce(att[:, a + 3:a + 4], lg[:, 0:w], AX.X, ALU.max)
                dve.drain()
                nc.vector.tensor_scalar(att[:, a:a + 1], att[:, a + 3:a + 4], -1.0, None,
                                        ALU.mult).then_inc(S["lg_ready"], 1)

            def normalise(u):
                a = 4 * (u % 2)
                dve.wait_ge(S["p_ready"], base + u + 1)
                nc.vector.reciprocal(att[:, a + 2:a + 3], att[:, a + 1:a + 2])
                dve.drain()
                n = UN[u]["n"]
                nc.vector.tensor_scalar(lbuf(u)[:, 0:n], lbuf(u)[:, 0:n], att[:, a + 2:a + 3], None,
                                        ALU.mult).then_inc(S["pn_ready"], 1)

            def output(u):
                x = UN[u]
                dve.wait_ge(S["pv_ready"], base + u + 1)
                nc.vector.tensor_copy(hT[x["hs"], x["o"], x["t"] * P:(x["t"] + 1) * P],
                                      bank(6 + u % 2)[x["hs"], 0:P]).then_inc(S["pv_free"], 1)

            for u in range(NU + 2):
                if 0 < u <= NU:
                    normalise(u - 1)
                if u < NU:
                    logits(u)
                if u >= 2:
                    output(u - 2)
            dve.drain().then_inc(S["attn_done"], 1)
            meet("dve", dve)

        def attn_act(act, l):
            base = l * NU
            for u in range(NU + 1):
                if u < NU:
                    a = 4 * (u % 2)
                    n = UN[u]["n"] + (UN[u]["kind"] == "B")
                    act.wait_ge(S["lg_ready"], base + u + 1)
                    nc.scalar.activation(lbuf(u)[:, 0:n], lbuf(u)[:, 0:n], ACT.Exp, bias=att[:, a:a + 1],
                                         accum_out=att[:, a + 1:a + 2]).then_inc(S["p_ready"], 1)
                if u > 0:
                    v = u - 1
                    act.wait_ge(S["pt_ready"], base + v + 1)
                    if v >= 2:
                        act.wait_ge(S["pv_ready"], base + v - 1)
                    n = UN[v]["n"]
                    nc.scalar.copy(ptbuf(v)[:, 0:n], ps[:, 4 * 512:4 * 512 + n]).then_inc(S["pt_copied"], 1)
            meet("act", act)

        def out_pe(pe, l):
            hp = split_h("mix")
            for d in range(KT):
                n = base_out[l] + d // 2
                pe.wait_ge(w_used, n + 1)
                if d >= 4:
                    pe.wait_ge(S["out_free"], l * KT + d - 3)
                w = w3k(split_slot("mix", n))
                m = slice(d % 2 * P, d % 2 * P + P)
                for a, b in PIECES:
                    for k in range(KT):
                        mm = mm3(pair(d)[:, a:b], [x[:, k, m] for x in w], [x[:, k, a:b] for x in hp],
                                 k == 0, k == KT - 1)
                mm.then_inc(S["out_ready"], 1)
            meet("pe", pe)

        def out_act(act, l):
            for i in range(N_OUT):
                if i >= 2:
                    act.wait_ge(S["out_ready"], l * KT + 2 * (i - 1))
                split_hi(act, "mix", base_out[l] + i)
            meet("act", act)

        def residual(d, src, g):
            for s, (a, b) in enumerate(STREAMS):
                ins = nc.vector.scalar_tensor_tensor(xT[:, d, a:b], src[:, a:b], mod[:, g + d, s:s + 1],
                                                     xT[:, d, a:b], ALU.mult, ALU.add)
            return ins

        def out_dve(dve, l):
            split_lo(dve, "mix", base_out[l])
            split_lo(dve, "mix", base_out[l] + 1)
            for d in range(KT):
                dve.wait_ge(S["out_ready"], l * KT + d + 1)
                residual(d, pair(d), 16).then_inc(S["out_free"], 1)
                if d % 2 and d // 2 + 2 < N_OUT:
                    split_lo(dve, "mix", base_out[l] + d // 2 + 2)
            meet("dve", dve)

        gate = pj[:, 0:NE, :]
        lg3 = wk[:, 0:5 * NE].rearrange("p (t e) -> p t e", t=5)
        ge3 = wk[:, 64:64 + 5 * NE].rearrange("p (t e) -> p t e", t=5)
        cmp = wk[:, 256:256 + 5 * 64].rearrange("p (t e f) -> p t e f", t=5, e=NE)
        ceq = wk[:, 640:640 + 5 * 64].rearrange("p (t e f) -> p t e f", t=5, e=NE)
        gT = wk[:, 1024:1024 + T]

        def router_pe(pe):
            for t in range(5):
                for k in range(KT):
                    nc.tensor.matmul(ps[:, t * NE:(t + 1) * NE], hT[:, k, t * P:(t + 1) * P], rt[:, k, :],
                                     start=(k == 0), stop=(k == KT - 1))
            for _ in range(4):
                meet("pe", pe)
            for t in range(5):
                nc.tensor.matmul(ps[0:NE, t * P:(t + 1) * P], ge3[:, t, :], ident[:, :], start=True, stop=True)
            meet("pe", pe)
            meet("pe", pe)
            for half in range(2):
                for j in range(4):
                    e = 4 * half + j
                    for a, b in PIECES:
                        nc.tensor.matmul(pair(j)[:, a:b], ident[0:NE, e:e + 1].to_broadcast([NE, P]), gT[0:NE, a:b],
                                         start=True, stop=True)
                meet("pe", pe)
                meet("pe", pe)

        def router_dve(dve):
            meet("dve", dve)
            nc.vector.tensor_copy(wk[:, 0:5 * NE], ps[:, 0:5 * NE])
            dve.drain()
            nc.vector.tensor_reduce(att[:, 0:5], lg3, AX.X, ALU.max)
            e_ = lg3.unsqueeze(3).to_broadcast([P, 5, NE, NE])
            for t in range(5):
                le = lg3[:, t].unsqueeze(2).to_broadcast([P, NE, NE])
                lf = lg3[:, t].unsqueeze(1).to_broadcast([P, NE, NE])
                nc.vector.tensor_tensor(cmp[:, t], lf, le, ALU.is_gt)
                nc.vector.tensor_tensor(ceq[:, t], lf, le, ALU.is_equal)
            dve.drain()
            nc.vector.tensor_tensor(lg3, lg3, att[:, 0:5].unsqueeze(2).to_broadcast([P, 5, NE]), ALU.subtract)
            for t in range(5):
                nc.vector.tensor_tensor(ceq[:, t], ceq[:, t], tri[:, :, :], ALU.mult)
            meet("dve", dve)
            for t in range(5):
                nc.vector.tensor_tensor(cmp[:, t], cmp[:, t], ceq[:, t], ALU.add)
            dve.drain()
            nc.vector.tensor_reduce(wk[:, 128:128 + 5 * NE], cmp.rearrange("p t e f -> p (t e) f"), AX.X, ALU.add)
            dve.drain()
            nc.vector.tensor_scalar(wk[:, 128:128 + 5 * NE], wk[:, 128:128 + 5 * NE], 2.0, None, ALU.is_lt)
            meet("dve", dve)
            nc.vector.tensor_tensor(wk[:, 64:64 + 5 * NE], wk[:, 64:64 + 5 * NE], wk[:, 128:128 + 5 * NE], ALU.mult)
            dve.drain()
            nc.vector.tensor_reduce(att[:, 5:10], ge3, AX.X, ALU.add)
            dve.drain()
            nc.vector.reciprocal(att[:, 5:10], att[:, 5:10])
            dve.drain()
            nc.vector.tensor_tensor(ge3, ge3, att[:, 5:10].unsqueeze(2).to_broadcast([P, 5, NE]), ALU.mult)
            meet("dve", dve)
            meet("dve", dve)
            nc.vector.tensor_copy(gT[0:NE, :], ps[0:NE, 0:T])
            meet("dve", dve)
            for half in range(2):
                meet("dve", dve)
                for j in range(0, 4, 2):
                    nc.vector.tensor_copy(gate[:, 4 * half + j, :], pair(j))
                meet("dve", dve)

        def router_act(act):
            meet("act", act)
            meet("act", act)
            nc.scalar.activation(wk[:, 64:64 + 5 * NE], wk[:, 0:5 * NE], ACT.Exp, bias=par[:, 1, C_ZERO:C_ZERO + 1])
            meet("act", act)
            meet("act", act)
            meet("act", act)
            meet("act", act)
            for half in range(2):
                meet("act", act)
                for j in range(1, 4, 2):
                    nc.scalar.copy(gate[:, 4 * half + j, :], pair(j))
                meet("act", act)

        def act_buf(i):
            return w3k(halves(pj[:, 8 + 2 * (i % 2):10 + 2 * (i % 2), :].rearrange("p a b -> p (a b)"), 2 * T), 2)

        def up_pe(pe, b, n, shift, prod, wshift):
            hp = split_h("ffn")
            pe.wait_ge(w_used, wshift + b + n + 2)
            w = [w3k(split_slot("ffn", b + n + i)) for i in range(2)]
            for c in range(2):
                for i in range(2):
                    q = prod + 2 * c + i
                    ffn_free_pe(pe, q, shift)
                    for a, e in PIECES:
                        for k in range(KT):
                            mm = mm3(pair(q)[:, a:e], [x[:, k, c * P:(c + 1) * P] for x in w[i]],
                                     [x[:, k, a:e] for x in hp], k == 0, k == KT - 1)
                    mm.then_inc(S["f_ready"], 1)

        def ffn_free_pe(pe, q, shift):
            if q >= 4 or not isinstance(shift, int):
                pe.wait_ge(S["f_free"], shift + q - 3)

        def down_pe(pe, b, n, item, shift, prod, wshift, ishift, aprod):
            pe.wait_ge(w_used, wshift + b + n + 1)
            pe.wait_ge(S["hid_ready"], 2 * ishift + 2 * aprod + 2)
            w = w3k(split_slot("ffn", b + n), 2)
            hid = act_buf(item)
            for d in range(KT):
                q = prod + d
                ffn_free_pe(pe, q, shift)
                for a, e in PIECES:
                    for c in range(2):
                        mm = mm3(pair(q)[:, a:e], [x[:, c, d * P:(d + 1) * P] for x in w],
                                 [x[:, c, a:e] for x in hid], c == 0, c == 1)
                mm.then_inc(S["f_ready"], 1)

        def up_act(act, l, shift, prod, ishift, aprod):
            for c in range(2):
                q = prod + 2 * c
                act.wait_ge(S["f_ready"], shift + q + 1)
                if 2 * aprod + c - 1 > 0:
                    act.wait_ge(S["hid_ready"], 2 * ishift + 2 * aprod + c - 1)
                sigmoid(act, l, pj[:, 12 + c, :], pair(q), 1.0 / W_SCALE).then_inc(S["f_exp"], 1)

        def up_dve(dve, item, shift, prod, ishift, aprod, g):
            hi, lo = act_buf(item)
            for c in range(2):
                e = pj[:, 12 + c, :]
                q = prod + 2 * c
                dve.wait_ge(S["f_exp"], 2 * ishift + 2 * aprod + c + 1)
                nc.vector.scalar_tensor_tensor(e, pair(q), 1.0 / W_SCALE, e, ALU.mult,
                                               ALU.mult).then_inc(S["f_free"], 1)
                dve.drain()
                dve.wait_ge(S["f_ready"], shift + q + 2)
                nc.vector.scalar_tensor_tensor(e, pair(q + 1), 1.0 / W_SCALE, e, ALU.mult,
                                               ALU.mult).then_inc(S["f_free"], 1)
                dve.drain()
                if g is not None:
                    nc.vector.tensor_tensor(e, e, g, ALU.mult)
                    dve.drain()
                nc.vector.tensor_copy(hi[:, c, :], e)
                dve.drain()
                nc.vector.tensor_tensor(lo[:, c, :], e, hi[:, c, :], ALU.subtract).then_inc(S["hid_ready"], 1)

        def down_dve(dve, shift, prod):
            for d in range(KT):
                dve.wait_ge(S["f_ready"], shift + prod + d + 1)
                residual(d, pair(prod + d), 40).then_inc(S["f_free"], 1)
            dve.drain()

        F_BASE = (0, 12 * DENSE_ITEMS)
        I_BASE = (0, DENSE_ITEMS)

        def ffn(l, eng, up, down, ahead):
            items = DENSE_ITEMS if l == 0 else EXPERT_ITEMS * NE
            ahead(0, 0, "first")
            up(0, 0, F_BASE[l], 0)
            ahead(0, 0, "load 4")

            def run(i, e):
                q = F_BASE[l] + 4 + 12 * i
                ahead(i + 1, e, "w1")
                if i + 1 < items:
                    up(i + 1, e, q, 2 + 3 * i)
                    ahead(i + 1, e, "rest")
                    down(i, e, q + 4, 4 + 3 * i)
                else:
                    down(i, e, q, 2 + 3 * i)

            if l == 0:
                for i in range(items):
                    run(i, 0)
                return
            for i in range(EXPERT_ITEMS):
                run(i, 0)
            with eng.Fori(0, NE - 2) as e:
                for i in range(EXPERT_ITEMS):
                    run(EXPERT_ITEMS + i, e)
            for i in range(EXPERT_ITEMS * (NE - 1), items):
                run(i, 0)

        def ffn_ahead(l, f):
            items = DENSE_ITEMS if l == 0 else EXPERT_ITEMS * NE

            def ahead(i, e, what):
                if what == "first":
                    for n in range(4):
                        f(n, e, None)
                elif what == "load 4":
                    f(4, e, 4)
                elif what == "w1":
                    if i + 1 < items:
                        f(2 + 3 * i, e, 12 * i - 8)
                elif i + 1 < items:
                    f(3 + 3 * i, e, 12 * i - 4)
                    f(4 + 3 * i, e, 12 * i - 4)
                elif i < items:
                    f(2 + 3 * i, e, 12 * i - 4)
            return ahead

        def ffn_pe(pe, l):
            b = base_ffn[l]
            ffn(l, pe, lambda i, e, q, n: up_pe(pe, b, n, e * 48, q, e * 12),
                lambda i, e, q, n: down_pe(pe, b, n, i, e * 48, q, e * 12, e * 4, I_BASE[l] + i), lambda *a: None)
            meet("pe", pe)

        def ffn_dve(dve, l):
            b = base_ffn[l]
            count = n_hi["dve"]

            def up(i, e, q, n):
                if l == 0:
                    g = None
                elif isinstance(e, int):
                    g = gate[:, i // EXPERT_ITEMS, :]
                else:
                    g = gate[:, bass.ds(e + i // EXPERT_ITEMS, 1), :].rearrange("p a t -> p (a t)")
                up_dve(dve, i, e * 48, q, e * 4, I_BASE[l] + i, g)

            def lo(n, e, after):
                n_hi["dve"] = count + n
                split_lo(dve, "ffn", b + n, 0, e * 12)
            ffn(l, dve, up, lambda i, e, q, n: down_dve(dve, e * 48, q), ffn_ahead(l, lo))
            n_hi["dve"] = count + 3 * (DENSE_ITEMS if l == 0 else EXPERT_ITEMS * NE)
            meet("dve", dve)

        def ffn_act(act, l):
            b = base_ffn[l]

            def hi(n, e, after):
                if after is not None and after + F_BASE[l] > 0 and (after > 0 or not isinstance(e, int)):
                    act.wait_ge(S["f_ready"], e * 48 + F_BASE[l] + after)
                split_hi(act, "ffn", b + n, e * 3)
            ffn(l, act, lambda i, e, q, n: up_act(act, l, e * 48, q, e * 4, I_BASE[l] + i), lambda *a: None,
                ffn_ahead(l, hi))
            meet("act", act)

        @block.tensor
        def _(pe):
            pe.wait_ge(consts_loaded, 16 * N_CONST)
            meet("pe", pe)
            for l in range(DEPTH):
                mod_pe(pe, l)
                norm_pe(pe, 2 * l)
                meet("pe", pe)
                in_pe(pe, l)
                qk_pe(pe, l)
                decay_a_pe(pe, l)
                loop_steps(pe, l, lambda s, it, i: gla_pe(pe, s, it))
                scan_out_pe(pe)
                conv_pe(pe, l)
                gdn_all_pe(pe, l)
                scan_out_pe(pe)
                attn_pe(pe, l)
                meet("pe", pe)
                out_pe(pe, l)
                norm_pe(pe, 2 * l + 1)
                if l == 1:
                    router_pe(pe)
                meet("pe", pe)
                ffn_pe(pe, l)

        @block.scalar
        def _(act):
            act.wait_ge(consts_loaded, 16 * N_CONST)
            nc.scalar.preload_act_table_set("natural_log_exp_and_others")
            nc.scalar.activation(cE[:], cT[:], ACT.Exp, bias=par[:, 0, C_ZERO:C_ZERO + 1], scale=-1.0)
            meet("act", act)
            for l in range(DEPTH):
                mod_act(act, l)
                norm_act(act, 2 * l, l)
                split_act(act, "mix")
                in_evac("act", act, l)
                qk_act(act, l)
                decay_a_act(act, l)
                loop_steps(act, l, lambda s, it, i: gla_act(act, l, s, it, i))
                scan_out_act(act, l, AR)
                conv_act(act, l)
                gdn_all_act(act, l)
                scan_out_act(act, l, DR)
                attn_act(act, l)
                split_act(act, "mix")
                out_act(act, l)
                norm_act(act, 2 * l + 1, l)
                if l == 1:
                    router_act(act)
                split_act(act, "ffn")
                ffn_act(act, l)

        @block.vector
        def _(dve):
            dve.wait_ge(consts_loaded, 16 * N_CONST)
            meet("dve", dve)
            nc.vector.tensor_scalar(cE[:], cE[:], 1.0, None, ALU.add)
            dve.drain()
            nc.vector.reciprocal(cE[:], cE[:])
            dve.drain()
            nc.vector.tensor_tensor(cT[:], cT[:], cE[:], ALU.mult)
            dve.drain()
            for d in range(2):
                dve.drain().then_inc(S["gla_done"][d], 1)
                dve.drain().then_inc(S["gdn_done"][d], 1)
            for l in range(DEPTH):
                mod_dve(dve, l)
                norm_dve(dve, 2 * l)
                split_dve(dve, "mix")
                in_evac("dve", dve, l)
                dve.drain().then_inc(S["proj_done"], 1)
                nc.vector.memset(hT[:], 0.0)
                if l > 0:
                    dve.wait_ge(S["states_out"], 80 * l)
                nc.vector.memset(st_a[0][:], 0.0)
                nc.vector.memset(st_d[0][:], 0.0)
                qk_dve(dve, l)
                decay_a_dve(dve, l)
                dve.wait_ge(S["cache_in"], 80 * (l + 1))
                loop_steps(dve, l, lambda s, it, i: gla_dve(dve, l, s, it, i))
                scan_out_dve(dve, l, OA, AR, C_AON)
                conv_dve(dve, l)
                dve.drain().then_inc(S["mixer_a_done"], 1)
                gdn_all_dve(dve, l)
                dve.drain().then_inc(S["mixer_d_done"], 1)
                scan_out_dve(dve, l, OD, DR, C_DON)
                attn_dve(dve, l)
                split_dve(dve, "mix")
                out_dve(dve, l)
                dve.wait_ge(S["states_out"], 80 * (l + 1))
                norm_dve(dve, 2 * l + 1)
                if l == 1:
                    router_dve(dve)
                split_dve(dve, "ffn")
                ffn_dve(dve, l)
            dve.drain().then_inc(S["final_x"], 1)


N_CONST = 16


def constants():
    def bits(m):
        return (m * 0x3F80).astype(np.uint16)
    i = np.arange(P)
    f, j = i % L, i // L
    c = {"ident": np.eye(P), "ones": np.ones((P, P)), "blk": (j[:, None] == j[None, :]) * 1.0}
    sel = np.zeros((P, 4, P))
    for d in range(2):
        for h in range(4):
            for r in (R_BETA + 4 * d + h, R_DEC[d] + h):
                sel[r, 2 * d + h // 2, L * (h % 2):L * (h % 2) + L] = 1.0
    c["sel"] = sel
    src = np.where(f % 32 < 16, i + 16, i - 16)
    rot = np.zeros((P, P))
    rot[src, i] = np.where(f % 32 < 16, -1.0, 1.0)
    c["rot"] = rot
    tok = np.arange(NS_TOK)
    pos = np.where((f < 32)[:, None], (tok // L)[None, :], (tok % L)[None, :]).astype(np.float32)
    inv = (1.0 / (np.float32(10000.0) ** (np.arange(16, dtype=np.float32) / np.float32(16))))[f % 16]
    ang = pos * inv[:, None].astype(np.float32)
    c["cossin"] = np.stack([np.cos(ang), np.sin(ang)], 1)
    t = np.arange(T)
    c["cmask"] = np.broadcast_to(np.stack([t % L != 0, t % L != L - 1])[None], (P, 2, T))
    a, b = f[:, None], np.arange(L)[None, :]
    inc = np.stack([a <= b, a >= b], 1)
    c["incl"] = np.broadcast_to(inc[:, :, None, :], (P, 2, 2, L))
    lv = []
    for s in (1, 2, 4, 8, 16, 32):
        fwd = ((b // s) % 2 == 1) & (a // s == b // s - 1)
        bwd = ((a // s) % 2 == 1) & (b // s == a // s - 1)
        lv.append(np.stack([fwd, bwd], 1))
    c["lvl"] = np.broadcast_to(np.stack(lv, 1)[:, :, :, None, :], (P, 6, 2, 2, L))
    q, k = i[:, None], np.arange(3 * P)[None, :] - P
    c["swamask"] = np.where(abs(q - k) <= P, 0.0, NEG)
    col = np.arange(L)
    cs = np.clip(col - 8, 0, L - 16)
    m = ((col[None, :] >= cs[:, None]) & (col[None, :] < cs[:, None] + 16))[f]
    c["nmask"] = np.stack([m * 1.0, np.where(m, 0.0, NEG)], 1)
    c["tri"] = np.broadcast_to((np.arange(NE)[None, :] < np.arange(NE)[:, None])[None], (P, NE, NE))
    return {n: np.ascontiguousarray(bits(v) if n in BITS else v.astype(np.float32)) for n, v in c.items()}


def layouts(x):
    f32 = np.float32

    def feat(a):
        return np.moveaxis(a.reshape(a.shape[:-1] + (KT, P)), (-1, -2), (0, 1))

    def rows(w, width):
        s = w.shape[:-2]
        w = w.reshape(s + (KT, P, w.shape[-1] // width, width))
        k = len(s)
        return np.moveaxis(w, (k + 2, k + 1, k, k + 3), (k, k + 1, k + 2, k + 3)).reshape(s + (-1, P, KT * width))

    def down(w):
        s = w.shape[:-2]
        w = w.reshape(s + (w.shape[-2] // WCOL, 2, P, D))
        return np.swapaxes(w, -3, -2).reshape(s + (-1, P, 2 * D))

    o = constants()
    o["xT"] = feat(np.concatenate([x["x_prompt"][0], x["x_sample"][0]]))
    o["cT"] = feat(np.stack([x["c_ctx"], x["c"][0]]))
    o["wmod"] = rows(x["w_mod"], WCOL)
    w = x["w_in"]
    cut = [0] + list(np.cumsum([256] * 4 + [16] * 2 + [256, 128, 128] + [256] * 3 + [256] * 4 + [4] * 4))
    part = [w[:, :, a:b] for a, b in zip(cut[:-1], cut[1:])]
    aq, ak, av, ar, alf, alb, sq, sk, sv, nq, nk, nv, dq, dk, dv, dr, daf, dab, dbf, dbb = part

    def z(n):
        return np.zeros((DEPTH, D, n), f32)
    sq = sq.reshape(DEPTH, D, 2, 2, L).transpose(0, 1, 3, 2, 4).reshape(DEPTH, D, 256)
    small = np.concatenate([alf, alb, dbf, dbb, z(24), daf, z(28), dab, z(28)], -1)
    o["win"] = rows(np.concatenate([aq, ak, av, ar, sq, sk, nq, nk, dq, dk, dv, dr, small], -1), WCOL)
    o["wv"] = rows(np.concatenate([sv, nv, z(2 * WCOL - V_COLS)], -1), WCOL)
    wo = x["w_out"].reshape(DEPTH, 4, 256, D).copy()
    wo[:, 1] = wo[:, 1].reshape(DEPTH, 2, 2, L, D).transpose(0, 2, 1, 3, 4).reshape(DEPTH, 256, D)
    o["wout"] = rows(wo.reshape(DEPTH, D, D), WCOL)
    o["d1"], o["d3"], o["d2"] = rows(x["ffn_w1"][0], WCOL), rows(x["ffn_w3"][0], WCOL), down(x["ffn_w2"][0])
    o["e1"] = rows(x["moe_w1"][0], WCOL).reshape(-1, P, SLOT)
    o["e3"] = rows(x["moe_w3"][0], WCOL).reshape(-1, P, SLOT)
    o["e2"] = down(x["moe_w2"][0]).reshape(-1, P, SLOT)
    o["router"] = x["moe_router"][0].reshape(KT, P, NE).transpose(1, 0, 2)

    par = np.zeros((P, DEPTH, NPAR), f32)
    for l in range(DEPTH):
        def put(c, a):
            par[:, l, c:c + a.shape[1]] = a
        put(C_N1, x["norm1_g"][l].reshape(KT, P).T)
        put(C_N2, x["norm2_g"][l].reshape(KT, P).T)
        put(C_BMOD, x["b_mod"][l].reshape(48, P).T)
        put(C_BUP, x["gla_bup"][l].reshape(4, P).T)
        for c, n in ((C_AON, "gla_onorm"), (C_SQN, "swa_qnorm"), (C_SKN, "swa_knorm"), (C_NQN, "na_qnorm"),
                     (C_NKN, "na_knorm"), (C_DON, "gdn_onorm")):
            put(c, np.tile(x[n][l], 2)[:, None])
        put(C_SINK, np.broadcast_to(x["swa_sink"][l][None], (P, 4)))
        put(C_CONV, x["gdn_conv"][l].reshape(3, 6, P).transpose(2, 1, 0).reshape(P, 18))
        for d in range(2):
            par[R_DEC[d]:R_DEC[d] + 4, l, C_ALOG] = x["gdn_alog"][l, d]
            par[R_DEC[d]:R_DEC[d] + 4, l, C_DTB] = x["gdn_dtbias"][l, d]
        par[:, l, C_EPS], par[:, l, C_ONE] = EPS, 1.0
    o["par"] = par
    wup = np.zeros((32, DEPTH, 4, P), f32)
    for d in range(2):
        wup[16 * d:16 * d + 16, :, 2 * d:2 * d + 2] = x["gla_wup"][:, d].reshape(DEPTH, 16, 2, P).transpose(1, 0, 2, 3)
    o["wup"] = wup
    sk_, nk_ = x["cache_swa_k"][0], x["cache_na_k"][0]
    o["ck"] = np.concatenate([sk_.transpose(0, 1, 3, 2).reshape(DEPTH, 1, P, PAST),
                              nk_.transpose(0, 1, 3, 2).reshape(DEPTH, 2, P, PAST)], 1).transpose(0, 2, 1, 3)
    v = np.concatenate([x["cache_swa_v"][0], x["cache_na_v"][0]], 1)
    o["cv"] = v.reshape(DEPTH, 6, 2, P, L).transpose(0, 3, 2, 1, 4).reshape(DEPTH, P, 2, V_COLS)
    for n, s in (("sta", "state_gla"), ("std", "state_gdn")):
        o[n] = x[s][0].reshape(DEPTH, 2, 2, P, L).transpose(0, 3, 1, 2, 4)
    r = np.pad(x["na_rpb"], ((0, 0), (0, 0), (1, 1), (48, 48)))
    q, k, m = np.arange(L)[:, None], np.arange(L)[None, :], np.arange(16)
    win = r[:, :, :, k - q + 63]
    o["rpb"] = np.stack([win[:, :, m + 1 - rr].transpose(0, 3, 1, 2, 4) for rr in range(2)], 1).reshape(DEPTH, P, 4096)
    return {n: np.ascontiguousarray(a) for n, a in o.items()}


BITS = ("cmask", "incl", "lvl", "tri")


OUTS = {"yT": (P, KT, T), "new_k": (DEPTH, P, NP_TOK), "new_nk": (DEPTH, P, 2, NP_TOK), "new_v": (DEPTH, P, V_COLS),
        "new_sta": (DEPTH, P, 2, 2, L), "new_std": (DEPTH, P, 2, 2, L)}


def declare(nc, arrays):
    A = {n: nc.dram_tensor(f"in_{n}", a.shape, mybir.dt.from_np(a.dtype), kind="ExternalInput").ap()
         for n, a in arrays.items()}
    for n in BITS:
        A[n] = A[n].bitcast(BF16)
    A |= {n: nc.dram_tensor(n, s, F32, kind="ExternalOutput").ap() for n, s in OUTS.items()}
    build(nc, A)


def kernel(**inputs):
    import concourse.bacc as bacc
    from concourse.bass_utils import run_bass_kernel_spmd
    arrays = layouts({n: np.asarray(a) for n, a in inputs.items()})
    nc = bacc.Bacc("TRN2", target_bir_lowering=False, num_devices=1)
    declare(nc, arrays)
    r = run_bass_kernel_spmd(nc, [{f"in_{n}": a for n, a in arrays.items()}], core_ids=[0]).results[0]
    return results(r)


def results(r):
    y = np.moveaxis(r["yT"], (1, 0), (1, 2)).reshape(T, D)
    k = r["new_k"].reshape(DEPTH, 2, L, NP_TOK).transpose(0, 1, 3, 2)[None]
    nk = r["new_nk"].reshape(DEPTH, 2, L, 2, NP_TOK).transpose(0, 3, 1, 4, 2).reshape(1, DEPTH, 4, NP_TOK, L)
    v = r["new_v"].reshape(DEPTH, P, 6, L).transpose(0, 2, 1, 3)
    sta, std = (r[n].transpose(0, 2, 3, 1, 4).reshape(1, DEPTH, 2, 4, L, L) for n in ("new_sta", "new_std"))
    out = (y[None, :NP_TOK], y[None, NP_TOK:], k, v[None, :, 0:2], nk, v[None, :, 2:6], sta, std)
    return tuple(np.ascontiguousarray(a) for a in out)
```

```python
from contextlib import ExitStack

import numpy as np

import concourse.bass as bass
from concourse import mybir

F32 = mybir.dt.float32
BF16 = mybir.dt.bfloat16
F16 = mybir.dt.float16
ALU = mybir.AluOpType
ACT = mybir.ActivationFunctionType
AX = mybir.AxisListType

P = 128
D = 1024
KT = D // P
NP_TOK, NS_TOK = 128, 512
T = NP_TOK + NS_TOK
STREAMS = ((0, NP_TOK), (NP_TOK, T))
PIECES = ((0, 512), (512, T))
DEPTH = 2
L = 64
PAST = 256
EPS = 1e-6
NEG = -1e30
FF = 2816
NE = 8
WCOL = 256
SLOT = KT * WCOL
NSLOT = 4
W_SCALE = 512.0
N_MOD, N_IN, N_OUT = 6 * D // WCOL, 12, D // WCOL
DENSE_ITEMS = FF // WCOL
EXPERT_ITEMS = 4
CAP = 256
TOP = 2
BLOCKS = (TOP * T - NE) // CAP + NE
Y_SCALE = 16.0
V_COLS = 384

AQ, AK, AV, AR, SQ, SK, NQ, NK, DQ, DK, DV, DR, SMALL = 0, 2, 4, 6, 8, 10, 11, 13, 15, 17, 19, 21, 23
NBLK = 24
R_BETA, R_DEC = 32, (64, 96)

C_N1, C_N2, C_BMOD, C_BUP, C_AON, C_SQN, C_SKN, C_SINK, C_NQN, C_NKN, C_CONV, C_ALOG, C_DTB, C_DON, C_EPS, C_ONE, \
    C_ZERO = 0, 8, 16, 64, 68, 69, 70, 71, 75, 76, 77, 95, 96, 97, 98, 99, 100
NPAR = 101
OA, OB, OC, OD = 0, 2, 4, 6


def build(nc, A):
    with ExitStack() as ctx:
        def sb(name, shape, dt=F32):
            return ctx.enter_context(nc.sbuf_tensor(name, shape, dt))

        def sem(name):
            return ctx.enter_context(nc.semaphore(name))

        xT = sb("xT", [P, KT, T])
        hT = sb("hT", [P, KT, T])
        pj = sb("pj", [P, NBLK, T])
        vtok = sb("vtok", [P, 5, V_COLS])
        scan = sb("scan", [P, 8, T])
        ring = sb("ring", [P, NSLOT, SLOT])
        work = sb("work", [P, 20, 256])
        ident = sb("ident", [P, P])
        ones = sb("ones", [P, P])
        blk = sb("blk", [P, P])
        sel = sb("sel", [P, 4, P])
        rot = sb("rot", [P, P])
        cmask = sb("cmask", [P, 2, T], BF16)
        incl = sb("incl", [P, 2, 2, L], BF16)
        lvl = sb("lvl", [P, 6, 2, 2, L], BF16)
        swamask = sb("swamask", [P, 3 * P])
        nmask = sb("nmask", [P, 2, L])
        ck = sb("ck", [P, 3, PAST])
        cv = sb("cv", [P, 2, V_COLS])
        st_a = [sb(f"st_a{s}", [P, 2, 2, L]) for s in range(2)]
        st_d = [sb(f"st_d{s}", [P, 2, 2, L]) for s in range(2)]
        par = sb("par", [P, DEPTH, NPAR])
        wup = sb("wup", [32, DEPTH, 4, P])
        cT = sb("cT", [P, KT, 2])
        cE = sb("cE", [P, KT, 2])
        mod = sb("mod", [P, 48, 2])
        s1 = sb("s1", [P, 2, KT, 2])
        cols = sb("cols", [P, 32])
        att = sb("att", [P, 16])
        rt = sb("rt", [P, KT, NE])
        tri = sb("tri", [P, NE, NE], BF16)
        before = sb("before", [P, P], BF16)
        block_expert = sb("block_expert", [P, BLOCKS], mybir.dt.int32)
        ps = ctx.enter_context(nc.psum_tensor("ps", [P, 8 * 512], F32))

        cossin = scan[:, 6:8, 0:NS_TOK]
        wk = work[:, :, :].rearrange("p a b -> p (a b)")
        scr = scan[:, :, :].rearrange("p a b -> p (a b)")
        rpb = pj[:, 0:8, :].rearrange("p a b -> p (a b)")[:, 0:4 * 16 * L].rearrange(
            "p (h m c) -> p h m c", h=4, m=16)

        def tmp(n):
            return wk[:, n * T:(n + 1) * T]

        def pair(n):
            return ps[:, (n % 4) * 1024:(n % 4) * 1024 + T]

        def bank(n, w=512):
            return ps[:, n * 512:n * 512 + w]

        def halves(region, n):
            return region.bitcast(F16)[:, 0:n], region.bitcast(F16)[:, n:2 * n]

        def split_slot(phase, n):
            at = (wk[:, 0:SLOT], wk[:, SLOT:2 * SLOT], scr[:, 0:SLOT], scr[:, SLOT:2 * SLOT])
            return halves(at[n % (4 if phase == "ffn" else 2)], SLOT)

        def split_h(phase):
            region = pj[:, 16:24, :].rearrange("p a b -> p (a b)") if phase == "ffn" else scr
            return [x.rearrange("p (k t) -> p k t", k=KT) for x in halves(region, KT * T)]

        def w3k(parts, k=KT):
            return [x.rearrange("p (k c) -> p k c", k=k) for x in parts]

        def mm3(out, w, x, start, stop):
            nc.tensor.matmul(out, w[0], x[0], start=start, stop=False)
            nc.tensor.matmul(out, w[0], x[1], start=False, stop=False)
            return nc.tensor.matmul(out, w[1], x[0], start=False, stop=stop)

        def slot3(n):
            return ring[:, n % NSLOT, :].rearrange("p (k c) -> p k c", k=KT)

        def slot2(n):
            return ring[:, n % NSLOT, :].rearrange("p (c n) -> p c n", c=2)

        c_loaded = sem("c_loaded")
        consts_loaded = sem("consts_loaded")
        w_loaded = [sem(f"w_loaded{i}") for i in range(NSLOT)]
        w_used = sem("w_used")
        meeting = sem("meeting")
        names = """front_sq front_sum front_r decay_ready decay_read decay_in decay_ln blocks_ready ht_ready ht_hi
            ht_lo moe_prod up_free e_ready moe_hid onehot_ready gathered gath_free_a gath_free_v spread_t
            gt_copied slot_gate y_high y_low scat_ready scat_free c_padded row_in row_exp row_scanned
            spread_ready spread_free_v spread_free_a conv_sq conv_sum conv_r ssq_in ssq_out rstd_ready
            normed_v prod_ready prod_free_v prod_free_a hn_sq hn_sum hn_r w_high h_high h_low proj_done
            conv_ready conv_exp gate_exp rope_ready rope_out sc_ready lg_ready p_ready pn_ready pt_ready
            pt_copied pv_ready pv_free mixer_a_done mixer_d_done rpb_loaded out_ready out_free f_ready
            f_free f_exp hid_ready out_stored states_out new_kv final_x cache_in attn_done""".split()
        S = {n: sem(n) for n in names}
        by_direction = """gla_staging gla_exp gla_staged gla_prod gla_evac_v gla_evac_a gla_out gla_done gdn_staged_v gdn_staged_a
            gdn_dif gdn_prod gdn_at gdn_u gdn_us gdn_x gdn_xs gdn_r0 gdn_tok gdn_rs gdn_u1 gdn_us1 gdn_o
            gdn_done""".split()
        S |= {n: [sem(f"{n}{d}") for d in range(2)] for n in by_direction}

        block = ctx.enter_context(nc.Block())
        met = {"pe": 0, "dve": 0, "act": 0}

        def meet(who, eng):
            met[who] += 1
            eng.drain().then_inc(meeting, 1)
            eng.wait_ge(meeting, 3 * met[who])

        base_mod = [0, 0]
        base_in, base_out, base_ffn = [0, 0], [0, 0], [0, 0]
        n = 0
        for l in range(DEPTH):
            base_mod[l] = n
            n += N_MOD
            base_in[l] = n
            n += N_IN + 2
            base_out[l] = n
            n += N_OUT
            base_ffn[l] = n
            n += 3 * (DENSE_ITEMS if l == 0 else EXPERT_ITEMS * BLOCKS)

        def uses(n):
            return n // NSLOT + 1

        MOE_LOADS = (("e1", 0), ("e3", 0), ("e1", 1), ("e3", 1), ("e2", 0), ("e1", 2), ("e3", 2), ("e2", 1),
                     ("e1", 3), ("e3", 3), ("e2", 2), ("e2", 3))

        @block.sync
        def _(sp):
            def load(n, src, width=None, shift=0):
                if isinstance(shift, int) and shift == 0 and n < NSLOT:
                    pass
                else:
                    sp.wait_ge(w_used, shift + (n - NSLOT + 1))
                dst = ring[:, n % NSLOT, :] if width is None else slot3(n)[:, :, 0:width]
                sp.dma_start(dst, src).then_inc(w_loaded[n % NSLOT], 16)

            for dst, name in ((par, "par"), (cT, "cT")):
                sp.dma_start(dst[:], A[name]).then_inc(c_loaded, 16)
            for j in range(NSLOT):
                load(base_mod[0] + j, A["wmod"][0, j])
            consts = [(ident, "ident"), (ones, "ones"), (blk, "blk"), (rot, "rot"), (sel, "sel"),
                      (cmask, "cmask"), (incl, "incl"), (lvl, "lvl"), (swamask, "swamask"), (nmask, "nmask"),
                      (wup, "wup"), (rt, "router"), (tri, "tri"), (before, "before"), (xT, "xT")]
            for dst, name in consts:
                sp.dma_start(dst[:], A[name]).then_inc(consts_loaded, 16)
            for l in range(DEPTH):
                for j in range(NSLOT if l == 0 else 0, N_MOD):
                    load(base_mod[l] + j, A["wmod"][l, j])
                for j in range(N_IN):
                    load(base_in[l] + j, A["win"][l, j])
                for j in range(2):
                    load(base_in[l] + N_IN + j, A["wv"][l, j])
                for j in range(N_OUT):
                    load(base_out[l] + j, A["wout"][l, j])
                b = base_ffn[l]
                if l == 0:
                    load(b, A["d1"][0])
                    load(b + 1, A["d3"][0])
                    b += 2
                    for i in range(DENSE_ITEMS):
                        if i + 1 < DENSE_ITEMS:
                            load(b, A["d1"][i + 1])
                            load(b + 1, A["d3"][i + 1])
                            b += 2
                        load(b, A["d2"][i])
                        b += 1
                else:
                    sp.wait_ge(S["blocks_ready"], 1)
                    with sp.Fori(0, BLOCKS) as block_no:
                        e = sp.value_load(block_expert[0:1, bass.ds(block_no, 1)], min_val=0, max_val=NE - 1)
                        for n, (name, i) in enumerate(MOE_LOADS):
                            src = A[name][bass.ds(e * EXPERT_ITEMS + i, 1)].rearrange("a p n -> p (a n)")
                            load(b + n, src, None, block_no * len(MOE_LOADS))

        @block.gpsimd
        def _(pool):
            for l in range(DEPTH):
                if l > 0:
                    pool.wait_ge(S["attn_done"], l)
                for dst, name in ((ck, "ck"), (cv, "cv"), (st_a[1], "sta"), (st_d[1], "std")):
                    pool.dma_start(dst[:], A[name][l]).then_inc(S["cache_in"], 16)
                pool.wait_ge(S["proj_done"], l + 1)
                pool.dma_start(cossin, A["cossin"]).then_inc(S["cache_in"], 16)
                pool.wait_ge(S["mixer_a_done"], l + 1)
                pool.dma_start(rpb.rearrange("p h m c -> p (h m c)"), A["rpb"][l]).then_inc(S["rpb_loaded"], 16)
                pool.dma_start(A["new_sta"][l], st_a[0][:]).then_inc(S["states_out"], 16)
                pool.wait_ge(S["new_kv"], l + 1)
                pool.dma_start(A["new_k"][l], pj[:, SK, 0:NP_TOK]).then_inc(S["states_out"], 16)
                pool.dma_start(A["new_nk"][l], pj[:, NK:NK + 2, 0:NP_TOK]).then_inc(S["states_out"], 16)
                pool.dma_start(A["new_v"][l], vtok[:, 0, :]).then_inc(S["states_out"], 16)
                pool.wait_ge(S["mixer_d_done"], l + 1)
                pool.dma_start(A["new_std"][l], st_d[0][:]).then_inc(S["states_out"], 16)
            pool.wait_ge(S["final_x"], 1)
            pool.dma_start(A["yT"], xT[:]).then_inc(S["out_stored"], 16)
            pool.wait_ge(S["out_stored"], 16)
            pool.wait_ge(S["states_out"], 80 * DEPTH)

        n_hi = {"act": 0, "dve": 0}

        def split_hi(act, phase, n, shift=0, hshift=0):
            act.wait_ge(w_loaded[n % NSLOT], shift * 16 + 16 * uses(n))
            nc.scalar.mul(split_slot(phase, n)[0], ring[:, n % NSLOT, :], W_SCALE).then_inc(S["w_high"], 1)
            n_hi["act"] += 1

        def split_lo(dve, phase, n, shift=0, hshift=0):
            n_hi["dve"] += 1
            dve.wait_ge(S["w_high"], hshift + n_hi["dve"])
            nc.vector.scalar_tensor_tensor(split_slot(phase, n)[1], ring[:, n % NSLOT, :], W_SCALE,
                                           split_slot(phase, n)[0], ALU.mult, ALU.subtract).then_inc(w_used, 1)

        def split_act(act, phase):
            hi, lo = split_h(phase)
            for a in range(0, KT, 4):
                nc.scalar.copy(hi[:, a:a + 4, :], hT[:, a:a + 4, :]).then_inc(S["h_high"], 1)

        def split_dve(dve, phase):
            hi, lo = split_h(phase)
            for a in range(0, KT, 4):
                n_h["dve"] += 1
                dve.wait_ge(S["h_high"], n_h["dve"])
                nc.vector.tensor_tensor(lo[:, a:a + 4, :], hT[:, a:a + 4, :], hi[:, a:a + 4, :], ALU.subtract)
            dve.drain().then_inc(S["h_low"], 1)

        def split_pe(pe):
            n_h["pe"] += 1
            pe.wait_ge(S["h_low"], n_h["pe"])

        n_h = {"dve": 0, "pe": 0}

        def sigmoid(act, l, out, x, scale=1.0):
            zero, one = par[:, l, C_ZERO:C_ZERO + 1], par[:, l, C_ONE:C_ONE + 1]
            nc.scalar.activation(out, x, ACT.Exp, bias=zero, scale=-scale)
            act.drain()
            nc.scalar.activation(out, out, ACT.Ln, bias=one, scale=1.0)
            act.drain()
            return nc.scalar.activation(out, out, ACT.Exp, bias=zero, scale=-1.0)

        MROW = 2 * N_MOD
        PAD = MROW - 2
        padded = wk[:, 0:KT * (MROW + PAD)].rearrange("p (k c) -> p k c", k=KT)
        mrows = wk[0:MROW, 1024:1024 + WCOL]

        def mod_pe(pe, l):
            pe.wait_ge(S["c_padded"], l + 1)
            for j in range(N_MOD):
                pe.wait_ge(w_loaded[(base_mod[l] + j) % NSLOT], 16 * uses(base_mod[l] + j))
                w = slot3(base_mod[l] + j)
                for k in range(KT):
                    mm = nc.tensor.matmul(ps[0:MROW, 0:WCOL], padded[:, k, PAD - 2 * j:PAD - 2 * j + MROW], w[:, k, :],
                                          start=(j == 0 and k == 0), stop=(j == N_MOD - 1 and k == KT - 1))
                mm.then_inc(w_used, 1)
            meet("pe", pe)
            meet("pe", pe)
            if l == 0:
                pe.wait_ge(consts_loaded, 16 * N_CONST)
            for m in range(2):
                nc.tensor.matmul(ps[:, 512 + MROW * m:512 + MROW * (m + 1)], mrows[:, m * P:(m + 1) * P],
                                 ident[0:MROW, 0:MROW], start=True, stop=True)
            meet("pe", pe)
            meet("pe", pe)

        def mod_dve(dve, l):
            nc.vector.memset(padded, 0.0)
            dve.drain()
            nc.vector.tensor_copy(padded[:, :, PAD:MROW], cT[:, :, :])
            dve.drain().then_inc(S["c_padded"], 1)
            meet("dve", dve)
            nc.vector.tensor_copy(mrows, ps[0:MROW, 0:WCOL])
            meet("dve", dve)
            meet("dve", dve)
            for m in range(2):
                nc.vector.tensor_tensor(mod[:, m::2, :],
                                        ps[:, 512 + MROW * m:512 + MROW * (m + 1)].rearrange("p (j s) -> p j s", s=2),
                                        par[:, l, C_BMOD + m:C_BMOD + 48:2].unsqueeze(2).to_broadcast([P, N_MOD, 2]),
                                        ALU.add)
            dve.drain()
            for g in (16, 40):
                scale = Y_SCALE if l == 1 and g == 40 else W_SCALE
                nc.vector.tensor_scalar(mod[:, g:g + 8, :], mod[:, g:g + 8, :], 1.0 / scale, None, ALU.mult)
            for w, c in ((0, C_N1), (1, C_N2)):
                nc.vector.scalar_tensor_tensor(s1[:, w], mod[:, 24 * w + 8:24 * w + 16, :], 1.0,
                                               par[:, l, c:c + 8].unsqueeze(2).to_broadcast([P, 8, 2]),
                                               ALU.add, ALU.mult)
            meet("dve", dve)

        def mod_act(act, l):
            for _ in range(4):
                meet("act", act)

        rstd = wk[:, 2 * SLOT:2 * SLOT + T]

        def norm_dve(dve, call, early):
            w = call % 2
            for k in range(0, KT, 2):
                nc.vector.tensor_tensor(hT[:, k:k + 2, :], xT[:, k:k + 2, :], xT[:, k:k + 2, :],
                                        ALU.mult).then_inc(S["ssq_in"], 1)
            for phase, n in early:
                split_lo(dve, phase, n)
            dve.wait_ge(S["rstd_ready"], call + 1)
            for k in range(0, KT + 2, 2):
                if k < KT:
                    nc.vector.tensor_tensor(hT[:, k:k + 2, :], xT[:, k:k + 2, :],
                                            rstd.unsqueeze(1).to_broadcast([P, 2, T]), ALU.mult).then_inc(S["normed_v"], 1)
                if k > 0:
                    dve.wait_ge(S["normed_v"], call * (KT // 2) + k // 2)
                    for s, (a, b) in enumerate(STREAMS):
                        nc.vector.tensor_scalar(hT[:, k - 2, a:b], hT[:, k - 2, a:b], s1[:, w, k - 2, s:s + 1],
                                                mod[:, 24 * w + k - 2, s:s + 1], ALU.mult, ALU.add)
            meet("dve", dve)

        def norm_pe(pe, call):
            for k in range(KT):
                if k % 2 == 0:
                    pe.wait_ge(S["ssq_in"], call * (KT // 2) + k // 2 + 1)
                for a, b in PIECES:
                    mm = nc.tensor.matmul(pair(0)[:, a:b], ones[:, :], hT[:, k, a:b],
                                          start=(k == 0), stop=(k == KT - 1))
            mm.then_inc(S["ssq_out"], 1)
            meet("pe", pe)

        def norm_act(act, call, l, early):
            w = call % 2
            for phase, n in early:
                split_hi(act, phase, n)
            act.wait_ge(S["ssq_out"], call + 1)
            nc.scalar.activation(rstd, pair(0), ACT.Ln, bias=par[:, l, C_EPS:C_EPS + 1], scale=1.0 / D)
            act.drain()
            nc.scalar.activation(rstd, rstd, ACT.Exp, bias=par[:, l, C_ZERO:C_ZERO + 1],
                                 scale=-0.5).then_inc(S["rstd_ready"], 1)
            for k in range(1, KT, 2):
                act.wait_ge(S["normed_v"], call * (KT // 2) + k // 2 + 1)
                for s, (a, b) in enumerate(STREAMS):
                    nc.scalar.activation(hT[:, k, a:b], hT[:, k, a:b], ACT.Identity,
                                         bias=mod[:, 24 * w + k, s:s + 1], scale=s1[:, w, k, s:s + 1])
            meet("act", act)

        N_PROD = NBLK + 5

        def in_pe(pe, l):
            hp = split_h("mix")
            for j in range(N_PROD):
                if j >= 4:
                    free = S["prod_free_v"] if j % 2 == 0 else S["prod_free_a"]
                    per = (N_PROD + 1) // 2 if j % 2 == 0 else N_PROD // 2
                    pe.wait_ge(free, l * per + (j - 4) // 2 + 1)
                if j < NBLK:
                    n, m = base_in[l] + j // 2, slice(j % 2 * P, j % 2 * P + P)
                    pe.wait_ge(w_used, n + 1)
                    w = w3k(split_slot("mix", n))
                    for a, b in PIECES:
                        for k in range(KT):
                            mm = mm3(pair(j)[:, a:b], [x[:, k, m] for x in w], [x[:, k, a:b] for x in hp],
                                     k == 0, k == KT - 1)
                    mm.then_inc(S["prod_ready"], 1)
                else:
                    t = slice((j - NBLK) * P, (j - NBLK + 1) * P)
                    for h, (c0, c1) in enumerate(((0, WCOL), (WCOL, V_COLS))):
                        n = base_in[l] + N_IN + h
                        pe.wait_ge(w_used, n + 1)
                        w = w3k(split_slot("mix", n))
                        for k in range(KT):
                            mm = mm3(pair(j)[:, c0:c1], [x[:, k, t] for x in hp], [x[:, k, 0:c1 - c0] for x in w],
                                     k == 0, k == KT - 1)
                    mm.then_inc(S["prod_ready"], 1)
            meet("pe", pe)

        def in_evac(who, eng, l):
            def split(i):
                if i >= N_IN + 2:
                    return
                if who == "act":
                    if i >= 2:
                        act_wait = l * N_PROD + 2 * (i - 1)
                        eng.wait_ge(S["prod_ready"], act_wait)
                    split_hi(eng, "mix", base_in[l] + i)
                else:
                    split_lo(eng, "mix", base_in[l] + i)
            for j in range(0 if who == "dve" else 1, N_PROD, 2):
                eng.wait_ge(S["prod_ready"], l * N_PROD + j + 1)
                src = pair(j) if j < NBLK else pair(j)[:, 0:V_COLS]
                dst = pj[:, j, :] if j < NBLK else vtok[:, j - NBLK, :]
                if who == "dve":
                    nc.vector.tensor_scalar(dst, src, 1.0 / W_SCALE, None, ALU.mult).then_inc(S["prod_free_v"], 1)
                else:
                    nc.scalar.mul(dst, src, 1.0 / W_SCALE).then_inc(S["prod_free_a"], 1)
                if j < NBLK:
                    split(j // 2 + 2)
            meet(who, eng)

        hn = {"pe": 0, "dve": 0, "act": 0}

        def head_norm_dve(dve, x, nb, finish):
            hn["dve"] += 1
            nc.vector.tensor_tensor(wk[:, 0:nb * T].rearrange("p (b t) -> p b t", b=nb), x, x,
                                    ALU.mult).then_inc(S["hn_sq"], 1)
            dve.wait_ge(S["hn_r"], hn["dve"])
            for b in range(nb):
                finish(b, tmp(4 + b))
            dve.drain()

        def head_norm_pe(pe, nb):
            hn["pe"] += 1
            pe.wait_ge(S["hn_sq"], hn["pe"])
            for b in range(nb):
                for p0, p1 in PIECES:
                    mm = nc.tensor.matmul(pair(b)[:, p0:p1], blk[:, :], tmp(b)[:, p0:p1], start=True, stop=True)
            mm.then_inc(S["hn_sum"], 1)

        def head_norm_act(act, l, nb, div):
            hn["act"] += 1
            act.wait_ge(S["hn_sum"], hn["act"])
            for b in range(nb):
                nc.scalar.activation(tmp(4 + b), pair(b), ACT.Ln, bias=par[:, l, C_EPS:C_EPS + 1], scale=1.0 / div)
            act.drain()
            r = wk[:, 4 * T:(4 + nb) * T]
            nc.scalar.activation(r, r, ACT.Exp, bias=par[:, l, C_ZERO:C_ZERO + 1], scale=-0.5).then_inc(S["hn_r"], 1)

        def gained(x, col):
            def f(b, r):
                g = col(b)
                nc.vector.scalar_tensor_tensor(x[:, b, :], x[:, b, :], g, r, ALU.mult, ALU.mult)
            return f

        decay_z = hT[:, OB:OB + 4, :].rearrange("p b t -> p (b t)")

        def front_dve(dve, l):
            nc.vector.memset(hT[:, OA:OA + 2, :], 0.0)
            nc.vector.memset(hT[:, OD:OD + 2, :], 0.0)
            for n, (x, nb) in enumerate(((SQ, 3), (NQ, 4))):
                at = 3 * n * T
                nc.vector.tensor_tensor(wk[:, at:at + nb * T].rearrange("p (b t) -> p b t", b=nb), pj[:, x:x + nb, :],
                                        pj[:, x:x + nb, :], ALU.mult).then_inc(S["front_sq"], 1)
            dve.wait_ge(S["decay_ready"], l + 1)
            for j in range(4):
                bup = par[:, l, C_BUP + j:C_BUP + j + 1]
                nc.vector.tensor_scalar(scan[:, j, :], pair(j), bup, 0.0, ALU.add, ALU.min)
                nc.vector.tensor_scalar(decay_z[:, j * T:(j + 1) * T], pair(j), bup, None, ALU.add)
            dve.drain().then_inc(S["decay_read"], 1)
            nc.vector.scalar_tensor_tensor(decay_z, scr[:, 0:4 * T], 2.0, decay_z, ALU.mult,
                                           ALU.subtract).then_inc(S["decay_in"], 1)
            dve.wait_ge(S["front_r"], 2 * l + 1)
            for b in range(3):
                g = par[:, l, C_SQN:C_SQN + 1] if b < 2 else par[:, l, C_SKN:C_SKN + 1]
                x = pj[:, SQ + b, :]
                nc.vector.scalar_tensor_tensor(x, x, g, tmp(b), ALU.mult, ALU.mult)
            dve.drain().then_inc(S["rope_ready"], 1)
            dve.wait_ge(S["decay_ln"], l + 1)
            nc.vector.tensor_tensor(decay_z, scr[:, 0:4 * T], decay_z, ALU.subtract)
            dve.drain()
            for j in range(4):
                scan_chunks(scan[:, j, :], decay_z[:, j * T:(j + 1) * T], j // 2)
            dve.wait_ge(S["front_r"], 2 * l + 2)
            for b in range(4):
                g = par[:, l, C_NQN:C_NQN + 1] if b < 2 else par[:, l, C_NKN:C_NKN + 1]
                x = pj[:, NQ + b, :]
                nc.vector.scalar_tensor_tensor(x, x, g, tmp(3 + b), ALU.mult, ALU.mult)
            dve.drain().then_inc(S["new_kv"], 1)
            dve.wait_ge(S["rope_out"], l + 1)
            dve.wait_ge(S["cache_in"], 80 * (l + 1))
            x = pj[:, SQ:SQ + 3, NP_TOK:T]
            r = wk[:, 0:3 * NS_TOK].rearrange("p (b t) -> p b t", b=3)
            nc.vector.tensor_tensor(r, ps[:, 0:3 * 512].rearrange("p (b t) -> p b t", b=3),
                                    cossin[:, 1, :].unsqueeze(1).to_broadcast([P, 3, NS_TOK]), ALU.mult)
            nc.vector.tensor_tensor(x, x, cossin[:, 0, :].unsqueeze(1).to_broadcast([P, 3, NS_TOK]), ALU.mult)
            dve.drain()
            nc.vector.tensor_tensor(x, x, r, ALU.add)
            meet("dve", dve)

        def front_pe(pe, l):
            for j in range(4):
                for a, b in PIECES:
                    mm = nc.tensor.matmul(pair(j)[:, a:b], wup[:, l, j, :], pj[0:32, SMALL, a:b], start=True, stop=True)
            mm.then_inc(S["decay_ready"], 1)
            pe.wait_ge(S["decay_read"], l + 1)
            for n, nb in enumerate((3, 4)):
                pe.wait_ge(S["front_sq"], 2 * l + n + 1)
                if n:
                    pe.wait_ge(S["front_r"], 2 * l + 1)
                for b in range(nb):
                    for p0, p1 in PIECES:
                        mm = nc.tensor.matmul(pair(b)[:, p0:p1], blk[:, :], tmp(3 * n + b)[:, p0:p1],
                                              start=True, stop=True)
                mm.then_inc(S["front_sum"], 1)
            pe.wait_ge(S["rope_ready"], l + 1)
            pe.wait_ge(S["front_r"], 2 * l + 2)
            for b in range(3):
                mm = nc.tensor.matmul(bank(b), rot[:, :], pj[:, SQ + b, NP_TOK:T], start=True, stop=True)
            mm.then_inc(S["rope_out"], 1)
            meet("pe", pe)

        def front_act(act, l):
            def norm(n, nb):
                act.wait_ge(S["front_sum"], 2 * l + n + 1)
                for b in range(nb):
                    nc.scalar.activation(tmp(3 * n + b), pair(b), ACT.Ln, bias=par[:, l, C_EPS:C_EPS + 1],
                                         scale=1.0 / L)
                act.drain()
                r = wk[:, 3 * n * T:(3 * n + nb) * T]
                nc.scalar.activation(r, r, ACT.Exp, bias=par[:, l, C_ZERO:C_ZERO + 1],
                                     scale=-0.5).then_inc(S["front_r"], 1)
            norm(0, 3)
            act.wait_ge(S["decay_in"], l + 1)
            nc.scalar.activation(decay_z, decay_z, ACT.Exp, bias=par[:, l, C_ZERO:C_ZERO + 1])
            act.drain()
            nc.scalar.activation(decay_z, decay_z, ACT.Ln, bias=par[:, l, C_ONE:C_ONE + 1],
                                 scale=1.0).then_inc(S["decay_ln"], 1)
            norm(1, 4)
            meet("act", act)

        def scan_chunks(out, data, back, p0=0, p1=P):
            m = cmask[p0:p1, back, :]
            if back:
                nc.vector.tensor_tensor_scan(out[p0:p1, ::-1], m[:, ::-1], data[p0:p1, ::-1], 0.0, ALU.mult, ALU.add)
            else:
                nc.vector.tensor_tensor_scan(out[p0:p1, :], m, data[p0:p1, :], 0.0, ALU.mult, ALU.add)

        STEPS = ((0, 2), (NP_TOK, 8))

        def chunks(i, s, ahead=0):
            off, n = STEPS[s]
            return (i * L + (off + ahead * L), i * (-L) + (off + (n - 1 - ahead) * L))

        spare = pj[:, 0:8, :].rearrange("p a b -> p (a b)")[:, 4 * 16 * L:4 * 16 * L + 2 * 256].rearrange(
            "p (n c) -> p n c", n=2)

        def buf(i):
            return work[:, i, :] if i < 20 else spare[:, i - 20, :]

        def w4(i):
            return buf(i).rearrange("p (d g c) -> p d g c", d=2, g=2)

        def pd(d, b, j=0):
            o = (4 * d + b) * 512 + P * j
            return ps[:, o:o + P].rearrange("p (g c) -> p g c", g=2)

        def wd(i, d):
            return buf(i)[:, P * d:P * d + P]

        def fd(d, b, j=0, n=1):
            o = (4 * d + b) * 512 + P * j
            return ps[:, o:o + P * n]

        def units(d):
            for g in range(2):
                for p in range(2):
                    yield g, slice(64 * p, 64 * p + 64)

        A_E1, A_E2, A_QD, A_KI, A_KE, A_VS, A_AM, A_KES, A_VTOK, A_QN = range(10)

        def gla_front_act(act, l, s, it, i, ahead):
            zero = par[:, l, C_ZERO:C_ZERO + 1]
            for d, t in enumerate(chunks(i, s, ahead)):
                act.wait_ge(S["gla_staging"][d], it + 1)
                c = scan[:, 2 * d:2 * d + 2, bass.ds(t, L)]
                nc.scalar.activation(w4(A_E1)[:, d], c, ACT.Exp, bias=zero, scale=1.0 / 16)
                nc.scalar.activation(w4(A_E2)[:, d], c, ACT.Exp, bias=zero, scale=-1.0 / 16).then_inc(S["gla_exp"][d], 1)

        def gla_front_dve(dve, l, s, it, i, ahead):
            for d, t in enumerate(chunks(i, s, ahead)):
                q, k, v = (pj[:, b:b + 2, bass.ds(t, L)] for b in (AQ, AK, AV))
                last = L - 1 if d == 0 else 0
                decay = cols[:, 4 + 2 * d:6 + 2 * d].unsqueeze(2)
                dve.wait_ge(S["gla_exp"][d], it + 1)
                nc.vector.tensor_copy(decay, w4(A_E1)[:, d, :, last:last + 1])
                nc.vector.tensor_tensor(w4(A_KI)[:, d], k, w4(A_E2)[:, d], ALU.mult)
                nc.vector.scalar_tensor_tensor(w4(A_QN)[:, d], q, L ** -0.5, w4(A_E1)[:, d], ALU.mult, ALU.mult)
                nc.vector.tensor_copy(w4(A_VS)[:, d], v)
                dve.drain().then_inc(S["gla_staging"][d], 1)
                nc.vector.tensor_tensor(w4(A_KE)[:, d], w4(A_KI)[:, d], decay.to_broadcast([P, 2, L]),
                                        ALU.mult).then_inc(S["gla_staged"][d], 1)

        def gla_act(act, l, s, it, i, front):
            for d in range(2):
                act.wait_ge(S["gla_prod"][d], it + 1)
                nc.scalar.copy(wd(A_KES, d), fd(d, 1)).then_inc(S["gla_evac_a"][d], 1)
            front()

        def gla_dve(dve, l, s, it, i, front):
            ts = chunks(i, s)
            for d in range(2):
                dve.wait_ge(S["gla_prod"][d], it + 1)
                nc.vector.tensor_tensor(w4(A_AM)[:, d], pd(d, 0), incl[:, d], ALU.mult)
                nc.vector.tensor_copy(wd(A_QD, d), wd(A_QN, d))
                nc.vector.tensor_copy(cols[:, 2 * d:2 * d + 2], cols[:, 4 + 2 * d:6 + 2 * d])
                nc.vector.tensor_copy(wd(A_VTOK, d), fd(d, 0, 1)).then_inc(S["gla_evac_v"][d], 1)
            dve.drain()
            front()
            for d, t in enumerate(ts):
                st = st_a[s][:, d]
                o = hT[:, OA:OA + 2, bass.ds(t, L)]
                dve.wait_ge(S["gla_out"][d], it + 1)
                nc.vector.tensor_tensor(st, st, cols[:, 2 * d:2 * d + 2].unsqueeze(2).to_broadcast([P, 2, L]), ALU.mult)
                nc.vector.tensor_tensor(o, o, pd(d, 2), ALU.add)
                dve.drain()
                nc.vector.tensor_tensor(st, st, pd(d, 2, 1), ALU.add).then_inc(S["gla_done"][d], 1)

        def waited(pe, out):
            nc.tensor.matmul(out, incl[:].rearrange("p d g c -> p (d g c)")[:, 0:P], incl[:, 0, 0, :],
                             start=True, stop=True)

        def corner(d, b):
            o = (4 * d + b) * 512 + 448
            return ps[:, o:o + L]

        def gla_front_pe(pe, it):
            for d in range(2):
                pe.wait_ge(S["gla_staged"][d], it + 1)
                waited(pe, corner(d, 0))
                for g, h in units(d):
                    nc.tensor.matmul(pd(d, 0)[h, g], w4(A_KI)[h, d, g], w4(A_QN)[h, d, g], start=True, stop=True)
                    nc.tensor.matmul(pd(d, 0, 1)[h, g], w4(A_VS)[h, d, g], ident[h, h], start=True, stop=True)
                    mm = nc.tensor.matmul(pd(d, 1)[h, g], w4(A_KE)[h, d, g], ident[h, h], start=True, stop=True)
                mm.then_inc(S["gla_prod"][d], 1)

        def gla_pe(pe, s, it, front):
            for d in range(2):
                pe.wait_ge(S["gla_evac_v"][d], it + 1)
                pe.wait_ge(S["gla_evac_a"][d], it + 1)
                pe.wait_ge(S["gla_done"][d], it + 1)
                waited(pe, corner(d, 2))
                for g, h in units(d):
                    nc.tensor.matmul(pd(d, 2)[h, g], w4(A_VTOK)[h, d, g], w4(A_AM)[h, d, g], start=True, stop=False)
                    nc.tensor.matmul(pd(d, 2)[h, g], st_a[s][h, d, g], w4(A_QD)[h, d, g], start=False, stop=True)
                    mm = nc.tensor.matmul(pd(d, 2, 1)[h, g], w4(A_KES)[h, d, g], w4(A_VTOK)[h, d, g],
                                          start=True, stop=True)
                mm.then_inc(S["gla_out"][d], 1)
            front()

        def loop_pipelined(eng, l, front, step):
            for s, (_, n) in enumerate(STEPS):
                first = l * 10 + (0 if s == 0 else STEPS[0][1])
                front(s, first, 0, 0)
                with eng.Fori(0, n - 1) as i:
                    step(s, i + first, i, True)
                step(s, first + n - 1, n - 1, False)

        def gla_all_dve(dve, l):
            loop_pipelined(dve, l, lambda s, it, i, ahead: gla_front_dve(dve, l, s, it, i, ahead),
                           lambda s, it, i, more: gla_dve(
                               dve, l, s, it, i, lambda: gla_front_dve(dve, l, s, it + 1, i, 1) if more else None))

        def gla_all_act(act, l):
            loop_pipelined(act, l, lambda s, it, i, ahead: gla_front_act(act, l, s, it, i, ahead),
                           lambda s, it, i, more: gla_act(
                               act, l, s, it, i, lambda: gla_front_act(act, l, s, it + 1, i, 1) if more else None))

        def gla_all_pe(pe, l):
            loop_pipelined(pe, l, lambda s, it, i, ahead: gla_front_pe(pe, it),
                           lambda s, it, i, more: gla_pe(
                               pe, s, it, lambda: gla_front_pe(pe, it + 1) if more else None))

        def scan_out_dve(dve, l, ob, gate, gain):
            meet("dve", dve)
            x = hT[:, ob:ob + 2, :]
            gt = pj[:, gate:gate + 2, :]
            k = scan_out_n["dve"] = scan_out_n["dve"] + 1
            head_norm_dve(dve, x, 2, gained(x, lambda b: par[:, l, gain:gain + 1]))
            dve.wait_ge(S["gate_exp"], k)
            e = wk[:, 2 * T:4 * T]
            nc.vector.tensor_tensor(x, x, gt, ALU.mult)
            dve.drain()
            nc.vector.tensor_tensor(x, x, e.rearrange("p (b t) -> p b t", b=2), ALU.mult)
            meet("dve", dve)

        def scan_out_pe(pe):
            meet("pe", pe)
            head_norm_pe(pe, 2)
            meet("pe", pe)

        def scan_out_act(act, l, gate):
            meet("act", act)
            sigmoid(act, l, wk[:, 2 * T:4 * T], pj[:, gate:gate + 2, :].rearrange("p b t -> p (b t)")).then_inc(
                S["gate_exp"], 1)
            head_norm_act(act, l, 2, L)
            meet("act", act)

        scan_out_n = {"dve": 0}

        CONV_E = ((wk[:, 6 * T:8 * T], pj[:, 5:7, :].rearrange("p b t -> p (b t)")) * 2)[0:3]

        def row(n):
            return pj[:, n, :]

        def conv_dve(dve, l):
            z = row(0)
            nc.vector.tensor_scalar(z, pj[:, SMALL, :], par[:, l, C_DTB:C_DTB + 1], None, ALU.add)
            dve.drain()
            nc.vector.tensor_scalar(row(1), z, 0.0, 2.0, ALU.min, ALU.mult)
            dve.drain()
            nc.vector.tensor_tensor(row(1), row(1), z, ALU.subtract).then_inc(S["row_in"], 1)

            def conv(q):
                for b in (2 * q, 2 * q + 1):
                    nc.vector.tensor_scalar(tmp(b), pj[:, DQ + b, :], tap(b, 1), None, ALU.mult)
                dve.drain()
                for b in (2 * q, 2 * q + 1):
                    for a, e in STREAMS:
                        nc.vector.scalar_tensor_tensor(tmp(b)[:, a + 1:e], pj[:, DQ + b, a:e - 1], tap(b, 0),
                                                       tmp(b)[:, a + 1:e], ALU.mult, ALU.add)
                dve.drain()
                for b in (2 * q, 2 * q + 1):
                    for a, e in STREAMS:
                        nc.vector.scalar_tensor_tensor(tmp(b)[:, a:e - 1], pj[:, DQ + b, a + 1:e], tap(b, 2),
                                                       tmp(b)[:, a:e - 1], ALU.mult, ALU.add)
                dve.drain().then_inc(S["conv_ready"], 1)

            def tap(b, c):
                return par[:, l, C_CONV + 3 * b + c:C_CONV + 3 * b + c + 1]

            def silu(q):
                dve.wait_ge(S["conv_exp"], 3 * l + q + 1)
                x, y = pj[:, DQ + 2 * q:DQ + 2 * q + 2, :], wk[:, 2 * q * T:(2 * q + 2) * T]
                nc.vector.tensor_tensor(x, y.rearrange("p (b t) -> p b t", b=2),
                                        CONV_E[q].rearrange("p (b t) -> p b t", b=2), ALU.mult)
                dve.drain()
                if q < 2:
                    nc.vector.tensor_tensor(y.rearrange("p (b t) -> p b t", b=2), x, x,
                                            ALU.mult).then_inc(S["conv_sq"], 1)

            def spread(n):
                dve.wait_ge(S["spread_ready"], 2 * l + n + 1)
                for j in range(0, 4, 2):
                    nc.vector.tensor_copy(scan[:, 4 - 4 * n + j, :], pair(j)).then_inc(S["spread_free_v"], 1)

            conv(0)
            conv(1)
            dve.wait_ge(S["row_exp"], l + 1)
            nc.vector.scalar_tensor_tensor(z, z, 0.0, row(1), ALU.max, ALU.add)
            dve.drain()
            nc.vector.tensor_scalar(z, z, row(3)[:, 0:1], -1.0, ALU.mult, ALU.mult)
            dve.drain()
            scan_chunks(row(4), z, 0, 64, 96)
            scan_chunks(row(4), z, 1, 96, 128)
            dve.drain().then_inc(S["row_scanned"], 1)
            silu(0)
            spread(0)
            conv(2)
            silu(1)
            spread(1)
            for q in range(2):
                dve.wait_ge(S["conv_r"], 2 * l + q + 1)
                for b in (2 * q, 2 * q + 1):
                    x = pj[:, DQ + b, :]
                    nc.vector.scalar_tensor_tensor(x, x, L ** -0.5 if q == 0 else 1.0, tmp(b), ALU.mult, ALU.mult)
                if q == 0:
                    silu(2)
            meet("dve", dve)

        def conv_pe(pe, l):
            for n, (r, rows_, src) in enumerate(((R_BETA, 8, row(2)), (None, 4, row(4)))):
                pe.wait_ge(S["row_exp" if n == 0 else "row_scanned"], l + 1)
                if n:
                    pe.wait_ge(S["spread_free_v"], 4 * l + 2)
                    pe.wait_ge(S["spread_free_a"], 4 * l + 2)
                for j in range(4):
                    r0 = R_DEC[j // 2] if r is None else r
                    for a, b in PIECES:
                        mm = nc.tensor.matmul(pair(j)[:, a:b], sel[r0:r0 + rows_, j, :], src[r0:r0 + rows_, a:b],
                                              start=True, stop=True)
                mm.then_inc(S["spread_ready"], 1)
            pe.wait_ge(S["spread_free_v"], 4 * l + 4)
            pe.wait_ge(S["spread_free_a"], 4 * l + 4)
            for q in range(2):
                pe.wait_ge(S["conv_sq"], 2 * l + q + 1)
                for b in (2 * q, 2 * q + 1):
                    for p0, p1 in PIECES:
                        mm = nc.tensor.matmul(pair(b)[:, p0:p1], blk[:, :], tmp(b)[:, p0:p1], start=True, stop=True)
                mm.then_inc(S["conv_sum"], 1)
            meet("pe", pe)

        def conv_act(act, l):
            zero, one = par[:, l, C_ZERO:C_ZERO + 1], par[:, l, C_ONE:C_ONE + 1]

            def spread(n):
                act.wait_ge(S["spread_ready"], 2 * l + n + 1)
                for j in range(1, 4, 2):
                    nc.scalar.copy(scan[:, 4 - 4 * n + j, :], pair(j)).then_inc(S["spread_free_a"], 1)

            act.wait_ge(S["row_in"], l + 1)
            nc.scalar.activation(row(1), row(1), ACT.Exp, bias=zero)
            nc.scalar.activation(row(3)[:, 0:1], par[:, l, C_ALOG:C_ALOG + 1], ACT.Exp, bias=zero, scale=1.0)
            sigmoid(act, l, row(2), pj[:, SMALL, :])
            nc.scalar.activation(row(1), row(1), ACT.Ln, bias=one, scale=1.0)
            act.drain().then_inc(S["row_exp"], 1)
            for q in range(3):
                act.wait_ge(S["conv_ready"], 3 * l + q + 1)
                if q == 2:
                    act.wait_ge(S["conv_sq"], 2 * l + 1)
                sigmoid(act, l, CONV_E[q], wk[:, 2 * q * T:(2 * q + 2) * T]).then_inc(S["conv_exp"], 1)
                if q == 1:
                    spread(0)
            spread(1)
            for q in range(2):
                act.wait_ge(S["conv_sum"], 2 * l + q + 1)
                for b in (2 * q, 2 * q + 1):
                    nc.scalar.activation(tmp(b), pair(b), ACT.Ln, bias=par[:, l, C_EPS:C_EPS + 1], scale=1.0)
                act.drain()
                r = wk[:, 2 * q * T:(2 * q + 2) * T]
                nc.scalar.activation(r, r, ACT.Exp, bias=zero, scale=-0.5).then_inc(S["conv_r"], 1)
            meet("act", act)

        (D_Q, D_K, D_KE, D_VB, D_KB, D_QD, D_GB, D_BB, D_E, D_DF, D_AT, D_QK, D_KES, D_VBS, D_ATL, D_X, D_XT, D_US,
         D_R, D_U, D_EG, D_LV1) = range(22)

        def w3(n, d):
            return buf(n)[:, P * d:P * d + P].rearrange("p (g c) -> p g c", g=2)

        def bc(c):
            return c.unsqueeze(2).to_broadcast([P, 2, L])

        D_LV = (D_ATL, D_LV1)

        def alternate(x, v, which):
            return x.rearrange("p (n two s) -> p n two s", two=2, s=2 ** v)[:, :, which, :]

        def gdn_front_dve(dve, l, s, it, i, ahead, part):
            ts = chunks(i, s, ahead)
            tt = nc.vector.tensor_tensor
            if part == 0:
                for d, t in enumerate(ts):
                    at = bass.ds(t, L)
                    nc.vector.tensor_copy(w3(D_GB, d), scan[:, 2 * d:2 * d + 2, at])
                    nc.vector.tensor_copy(w3(D_K, d), pj[:, DK:DK + 2, at])
                    nc.vector.tensor_copy(w3(D_BB, d), scan[:, 4 + 2 * d:6 + 2 * d, at])
                    tt(w3(D_VB, d), pj[:, DV:DV + 2, at], scan[:, 4 + 2 * d:6 + 2 * d, at], ALU.mult)
            elif part == 1:
                for d, t in enumerate(ts):
                    for h in range(2):
                        hs = slice(64 * h, 64 * h + 64)
                        tt(w3(D_DF, d)[hs], w3(D_GB, d)[hs], ident[hs, hs].unsqueeze(1).to_broadcast([64, 2, L]),
                           ALU.mult)
                    last = L - 1 if d == 0 else 0
                    nc.vector.tensor_copy(cols[:, 4 + 2 * d:6 + 2 * d].unsqueeze(2), w3(D_GB, d)[:, :, last:last + 1])
                    nc.vector.tensor_copy(w3(D_Q, d), pj[:, DQ:DQ + 2, bass.ds(t, L)])
                dve.drain()
                for d in range(2):
                    nc.vector.tensor_reduce(cols[:, 2 * d:2 * d + 2], w3(D_DF, d), AX.X, ALU.add)
                    tt(w3(D_E, d), bc(cols[:, 4 + 2 * d:6 + 2 * d]), w3(D_GB, d), ALU.subtract)
            elif part == 2:
                for d in range(2):
                    tt(w3(D_DF, d), w3(D_GB, d), bc(cols[:, 2 * d:2 * d + 2]), ALU.subtract)
                dve.drain()
                for d in range(2):
                    tt(w3(D_DF, d), w3(D_DF, d), incl[:, d], ALU.mult).then_inc(S["gdn_dif"][d], 1)
            elif part == 3:
                for d in range(2):
                    dve.wait_ge(S["gdn_staged_a"][d], it + 1)
                    tt(wd(D_KE, d), wd(D_K, d), wd(D_E, d), ALU.mult).then_inc(S["gdn_staged_v"][d], 1)
            else:
                for d in range(2):
                    tt(wd(D_KB, d), wd(D_K, d), wd(D_EG, d), ALU.mult)
                    tt(w3(D_DF, d), w3(D_DF, d), incl[:, d], ALU.mult)
                    for h in range(2):
                        hs = slice(64 * h, 64 * h + 64)
                        nc.vector.tensor_copy(w3(D_X, d)[hs], ident[hs, hs].unsqueeze(1).to_broadcast([64, 2, L]))
                dve.drain()
                for d in range(2):
                    tt(wd(D_KB, d), wd(D_KB, d), wd(D_BB, d), ALU.mult)
                    tt(wd(D_BB, d), wd(D_BB, d), wd(D_DF, d), ALU.mult)

        def gdn_dve(dve, l, s, it, i, front):
            ts = chunks(i, s)
            tt = nc.vector.tensor_tensor
            for d in range(2):
                dve.wait_ge(S["gdn_prod"][d], it + 1)
                tt(wd(D_AT, d), fd(d, 0), wd(D_BB, d), ALU.mult)
                tt(wd(D_QK, d), fd(d, 0, 1), wd(D_DF, d), ALU.mult)
                dve.drain()
                tt(w3(D_LV[0], d), w3(D_AT, d), lvl[:, 0, d], ALU.mult).then_inc(S["gdn_at"][d], 1)
            for d in range(2):
                tt(wd(D_QD, d), wd(D_EG, d), wd(D_Q, d), ALU.mult)
                nc.vector.tensor_copy(cols[:, 8 + 2 * d:10 + 2 * d], cols[:, 12 + 2 * d:14 + 2 * d])
            dve.drain()
            for d in range(2):
                tt(wd(D_XT, d), wd(D_X, d), wd(D_LV[0], d), ALU.subtract)
            for v in range(6):
                for d in range(2):
                    if v < 5:
                        tt(w3(D_LV[(v + 1) % 2], d), w3(D_AT, d), lvl[:, v + 1, d], ALU.mult)
                    if v == 0:
                        dve.wait_ge(S["gdn_u"][d], it * 6 + 1)
                        tt(wd(D_X, d), wd(D_X, d), fd(d, 2), ALU.subtract).then_inc(S["gdn_xs"][d], 1)
                        continue
                    dve.wait_ge(S["gdn_x"][d], it * 5 + v)
                    if v < 5:
                        x = alternate(wd(D_X, d), v, d)
                        tt(x, x, alternate(fd(d, 3), v, d), ALU.subtract)
                    x = alternate(wd(D_XT, d), v, 1 - d)
                    tt(x, x, alternate(fd(d, 3, 1), v, 1 - d), ALU.subtract).then_inc(S["gdn_xs"][d], 1)
                if v < 4:
                    front(v)
                dve.drain()
            for d in range(2):
                dve.wait_ge(S["gdn_tok"][d], it + 1)
                dve.wait_ge(S["gdn_r0"][d], it + 1)
                tt(wd(D_R, d), wd(D_VBS, d), fd(d, 0, 2), ALU.subtract).then_inc(S["gdn_rs"][d], 1)
            front(4)
            for d, t in enumerate(ts):
                st = st_d[s][:, d]
                o = hT[:, OD:OD + 2, bass.ds(t, L)]
                dve.wait_ge(S["gdn_o"][d], it + 1)
                tt(st, st, bc(cols[:, 8 + 2 * d:10 + 2 * d]), ALU.mult)
                tt(o, o, pd(d, 2), ALU.add)
                dve.drain()
                tt(st, st, pd(d, 2, 1), ALU.add).then_inc(S["gdn_done"][d], 1)

        def gdn_front_act(act, l, it):
            zero = par[:, l, C_ZERO:C_ZERO + 1]
            for d in range(2):
                act.wait_ge(S["gdn_dif"][d], it + 1)
                nc.scalar.activation(wd(D_E, d), wd(D_E, d), ACT.Exp, bias=zero)
                nc.scalar.activation(wd(D_DF, d), wd(D_DF, d), ACT.Exp, bias=zero)
                nc.scalar.activation(cols[:, 12 + 2 * d:14 + 2 * d], cols[:, 4 + 2 * d:6 + 2 * d], ACT.Exp, bias=zero)
                nc.scalar.activation(wd(D_EG, d), wd(D_GB, d), ACT.Exp, bias=zero).then_inc(S["gdn_staged_a"][d], 1)

        def gdn_act(act, l, s, it, i, front):
            for d in range(2):
                act.wait_ge(S["gdn_prod"][d], it + 1)
                nc.scalar.copy(wd(D_KES, d), fd(d, 1))
                nc.scalar.copy(wd(D_VBS, d), fd(d, 1, 1)).then_inc(S["gdn_tok"][d], 1)
            for v in range(1, 6):
                for d in range(2):
                    act.wait_ge(S["gdn_u"][d], it * 6 + (v + 1))
                    nc.scalar.copy(wd(D_US, d), fd(d, 2)).then_inc(S["gdn_us"][d], 1)
                if v == 3:
                    front()
            for d in range(2):
                act.wait_ge(S["gdn_u1"][d], it + 1)
                nc.scalar.copy(wd(D_U, d), fd(d, 1, 2)).then_inc(S["gdn_us1"][d], 1)

        def gdn_front_pe(pe, it):
            for d in range(2):
                pe.wait_ge(S["gdn_staged_v"][d], it + 1)
                waited(pe, corner(d, 0))
                for g, h in units(d):
                    nc.tensor.matmul(pd(d, 0)[h, g], w4(D_K)[h, d, g], w4(D_K)[h, d, g], start=True, stop=True)
                    nc.tensor.matmul(pd(d, 0, 1)[h, g], w4(D_K)[h, d, g], w4(D_Q)[h, d, g], start=True, stop=True)
                    nc.tensor.matmul(pd(d, 1)[h, g], w4(D_KE)[h, d, g], ident[h, h], start=True, stop=True)
                    mm = nc.tensor.matmul(pd(d, 1, 1)[h, g], w4(D_VB)[h, d, g], ident[h, h], start=True, stop=True)
                mm.then_inc(S["gdn_prod"][d], 1)

        def gdn_pe(pe, s, it, front):
            for v in range(6):
                for d in range(2):
                    if v == 0:
                        pe.wait_ge(S["gdn_at"][d], it + 1)
                    else:
                        pe.wait_ge(S["gdn_xs"][d], it * 6 + v)
                    waited(pe, corner(d, 2))
                    for g, h in units(d):
                        mm = nc.tensor.matmul(pd(d, 2)[h, g], w4(D_LV[v % 2])[h, d, g],
                                              ident[h, h] if v == 0 else w4(D_X)[h, d, g], start=True, stop=True)
                    mm.then_inc(S["gdn_u"][d], 1)
                for d in range(2):
                    if v == 0:
                        continue
                    pe.wait_ge(S["gdn_us"][d], it * 5 + v)
                    waited(pe, corner(d, 3))
                    for g, h in units(d):
                        if v < 5:
                            nc.tensor.matmul(alternate(pd(d, 3)[h, g], v, d), w4(D_XT)[h, d, g],
                                             alternate(w4(D_US)[h, d, g], v, d), start=True, stop=True)
                        mm = nc.tensor.matmul(alternate(pd(d, 3, 1)[h, g], v, 1 - d), w4(D_US)[h, d, g],
                                              alternate(w4(D_XT)[h, d, g], v, 1 - d), start=True, stop=True)
                    mm.then_inc(S["gdn_x"][d], 1)
                if v == 0:
                    for d in range(2):
                        pe.wait_ge(S["gdn_at"][d], it + 1)
                        pe.wait_ge(S["gdn_done"][d], it + 1)
                        waited(pe, corner(d, 0))
                        for g, h in units(d):
                            mm = nc.tensor.matmul(pd(d, 0, 2)[h, g], w4(D_KB)[h, d, g], st_d[s][h, d, g],
                                                  start=True, stop=True)
                        mm.then_inc(S["gdn_r0"][d], 1)
            for d in range(2):
                pe.wait_ge(S["gdn_tok"][d], it + 1)
                pe.wait_ge(S["gdn_xs"][d], it * 6 + 6)
                pe.wait_ge(S["gdn_rs"][d], it + 1)
                waited(pe, corner(d, 1))
                for g, h in units(d):
                    mm = nc.tensor.matmul(pd(d, 1, 2)[h, g], w4(D_XT)[h, d, g], w4(D_R)[h, d, g],
                                          start=True, stop=True)
                mm.then_inc(S["gdn_u1"][d], 1)
            for d in range(2):
                pe.wait_ge(S["gdn_us1"][d], it + 1)
                waited(pe, corner(d, 2))
                for g, h in units(d):
                    nc.tensor.matmul(pd(d, 2)[h, g], st_d[s][h, d, g], w4(D_QD)[h, d, g], start=True, stop=False)
                    nc.tensor.matmul(pd(d, 2)[h, g], w4(D_U)[h, d, g], w4(D_QK)[h, d, g], start=False, stop=True)
                    mm = nc.tensor.matmul(pd(d, 2, 1)[h, g], w4(D_KES)[h, d, g], w4(D_U)[h, d, g],
                                          start=True, stop=True)
                mm.then_inc(S["gdn_o"][d], 1)
            front()

        def gdn_all_dve(dve, l):
            def front(s, it, i, ahead):
                for part in range(5):
                    gdn_front_dve(dve, l, s, it, i, ahead, part)
                    dve.drain()
            loop_pipelined(dve, l, front, lambda s, it, i, more: gdn_dve(
                dve, l, s, it, i, lambda part: gdn_front_dve(dve, l, s, it + 1, i, 1, part) if more else None))

        def gdn_all_act(act, l):
            loop_pipelined(act, l, lambda s, it, i, ahead: gdn_front_act(act, l, it),
                           lambda s, it, i, more: gdn_act(
                               act, l, s, it, i, lambda: gdn_front_act(act, l, it + 1) if more else None))

        def gdn_all_pe(pe, l):
            loop_pipelined(pe, l, lambda s, it, i, ahead: gdn_front_pe(pe, it),
                           lambda s, it, i, more: gdn_pe(
                               pe, s, it, lambda: gdn_front_pe(pe, it + 1) if more else None))

        def attn_units():
            for t in range(5):
                for kind in "BC":
                    for h in range(4):
                        if kind == "B":
                            p, q, k, o, c, vc = h // 2, SQ + h % 2, SK, OB + h % 2, 0, L * (h // 2)
                            loc = [0] if t == 0 else list(range(max(1, t - 1), min(4, t + 1) + 1))
                        else:
                            p, q, k, o, c, vc = h % 2, NQ + h // 2, NK + h // 2, OC + h // 2, 1 + h // 2, P + L * h
                            loc = [0] if t == 0 else [1, 2, 3, 4]
                        yield dict(t=t, kind=kind, h=h, hs=slice(64 * p, 64 * p + 64), q=q, k=k, o=o, c=c, vc=vc,
                                   loc=loc, ctx=0 if t == 0 else 2, nl=P * len(loc), n=P * len(loc) + (PAST if t else 0))

        UN = list(attn_units())
        NU = len(UN)

        def lbuf(u):
            return wk[:, (u % 3) * 800:(u % 3) * 800 + 800]

        def ptbuf(u):
            return wk[:, 2400 + (u % 2) * 768:2400 + (u % 2) * 768 + 768]

        def attn_scores(pe, u, base):
            x = UN[u]
            if u >= 2:
                pe.wait_ge(S["lg_ready"], base + u - 1)
            q = pj[x["hs"], x["q"], x["t"] * P:(x["t"] + 1) * P]
            b = 2 * (u % 2)
            mm = nc.tensor.matmul(bank(b)[:, 0:x["nl"]], q,
                                  pj[x["hs"], x["k"], x["loc"][0] * P:(x["loc"][-1] + 1) * P], start=True, stop=True)
            if x["ctx"]:
                mm = nc.tensor.matmul(bank(b + 1)[:, 0:PAST], q, ck[x["hs"], x["c"], :], start=True, stop=True)
            mm.then_inc(S["sc_ready"], 1)

        def attn_pv(pe, u, base):
            x = UN[u]
            pe.wait_ge(S["pt_copied"], base + u + 1)
            if u >= 2:
                pe.wait_ge(S["pv_free"], base + u - 1)
            vs = [vtok[:, t, x["vc"]:x["vc"] + L] for t in x["loc"]] + [cv[:, j, x["vc"]:x["vc"] + L]
                                                                       for j in range(x["ctx"])]
            for j, v in enumerate(vs):
                mm = nc.tensor.matmul(bank(6 + u % 2)[x["hs"], 0:P], v, ptbuf(u)[:, j * P:(j + 1) * P],
                                      start=(j == 0), stop=(j == len(vs) - 1))
            mm.then_inc(S["pv_ready"], 1)

        def attn_pe(pe, l):
            base = l * NU
            pe.wait_ge(S["cache_in"], 80 * (l + 1))
            attn_scores(pe, 0, base)
            attn_scores(pe, 1, base)
            for u in range(NU):
                if u + 2 < NU:
                    attn_scores(pe, u + 2, base)
                pe.wait_ge(S["pn_ready"], base + u + 1)
                if base + u > 0:
                    pe.wait_ge(S["pt_copied"], base + u)
                for j in range(UN[u]["n"] // P):
                    mm = nc.tensor.transpose(ps[:, 4 * 512 + j * P:4 * 512 + (j + 1) * P],
                                             lbuf(u)[:, j * P:(j + 1) * P], ident[:, :])
                mm.then_inc(S["pt_ready"], 1)
                if u > 0:
                    attn_pv(pe, u - 1, base)
            attn_pv(pe, NU - 1, base)
            meet("pe", pe)

        def attn_dve(dve, l):
            base = l * NU
            dve.wait_ge(S["rpb_loaded"], 16 * (l + 1))
            r3 = rpb.rearrange("p h m c -> p (h m) c")
            nc.vector.tensor_tensor(r3, r3, nmask[:, 0, :].unsqueeze(1).to_broadcast([P, 64, L]), ALU.mult)
            dve.drain()
            nc.vector.tensor_tensor(r3, r3, nmask[:, 1, :].unsqueeze(1).to_broadcast([P, 64, L]), ALU.add)
            dve.drain()

            def logits(u):
                x = UN[u]
                if u >= 3:
                    dve.wait_ge(S["pt_ready"], base + u - 2)
                dve.wait_ge(S["sc_ready"], base + u + 1)
                lg, b, nl, n = lbuf(u), 2 * (u % 2), x["nl"], x["n"]
                if x["t"] == 0:
                    nc.vector.tensor_scalar(lg[:, 0:nl], bank(b)[:, 0:nl], L ** -0.5, None, ALU.mult)
                elif x["kind"] == "B":
                    m0 = (x["loc"][0] - x["t"] + 1) * P
                    nc.vector.scalar_tensor_tensor(lg[:, 0:nl], bank(b)[:, 0:nl], L ** -0.5, swamask[:, m0:m0 + nl],
                                                   ALU.mult, ALU.add)
                else:
                    t = x["t"] - 1
                    bias = rpb[:, x["h"], 7 - 2 * t:15 - 2 * t, :].rearrange("p m c -> p (m c)")
                    nc.vector.scalar_tensor_tensor(lg[:, 0:nl], bank(b)[:, 0:nl], L ** -0.5, bias, ALU.mult, ALU.add)
                if x["ctx"]:
                    nc.vector.tensor_scalar(lg[:, nl:n], bank(b + 1)[:, 0:PAST], L ** -0.5, None, ALU.mult)
                w = n
                if x["kind"] == "B":
                    c = C_SINK + x["h"]
                    nc.vector.tensor_copy(lg[:, n:n + 1], par[:, l, c:c + 1])
                    w = n + 1
                dve.drain()
                a = 4 * (u % 3)
                nc.vector.tensor_reduce(att[:, a + 3:a + 4], lg[:, 0:w], AX.X, ALU.max)
                dve.drain()
                nc.vector.tensor_scalar(att[:, a:a + 1], att[:, a + 3:a + 4], -1.0, None,
                                        ALU.mult).then_inc(S["lg_ready"], 1)

            def normalise(u):
                a = 4 * (u % 3)
                dve.wait_ge(S["p_ready"], base + u + 1)
                nc.vector.reciprocal(att[:, a + 2:a + 3], att[:, a + 1:a + 2])
                dve.drain()
                n = UN[u]["n"]
                nc.vector.tensor_scalar(lbuf(u)[:, 0:n], lbuf(u)[:, 0:n], att[:, a + 2:a + 3], None,
                                        ALU.mult).then_inc(S["pn_ready"], 1)

            for u in range(NU + 1):
                if u < NU:
                    logits(u)
                if u > 0:
                    normalise(u - 1)
            meet("dve", dve)

        def attn_act(act, l):
            base = l * NU

            def output(u):
                x = UN[u]
                act.wait_ge(S["pv_ready"], base + u + 1)
                nc.scalar.copy(hT[x["hs"], x["o"], x["t"] * P:(x["t"] + 1) * P],
                               bank(6 + u % 2)[x["hs"], 0:P]).then_inc(S["pv_free"], 1)

            for u in range(NU + 1):
                if u < NU:
                    a = 4 * (u % 3)
                    n = UN[u]["n"] + (UN[u]["kind"] == "B")
                    act.wait_ge(S["lg_ready"], base + u + 1)
                    nc.scalar.activation(lbuf(u)[:, 0:n], lbuf(u)[:, 0:n], ACT.Exp, bias=att[:, a:a + 1],
                                         accum_out=att[:, a + 1:a + 2]).then_inc(S["p_ready"], 1)
                if u > 0:
                    v = u - 1
                    act.wait_ge(S["pt_ready"], base + v + 1)
                    if v >= 2:
                        output(v - 2)
                    n = UN[v]["n"]
                    nc.scalar.copy(ptbuf(v)[:, 0:n], ps[:, 4 * 512:4 * 512 + n]).then_inc(S["pt_copied"], 1)
            output(NU - 2)
            output(NU - 1)
            act.drain().then_inc(S["attn_done"], 1)
            meet("act", act)

        def out_pe(pe, l):
            hp = split_h("mix")
            for d in range(KT):
                n = base_out[l] + d // 2
                pe.wait_ge(w_used, n + 1)
                if d >= 4:
                    pe.wait_ge(S["out_free"], l * KT + d - 3)
                w = w3k(split_slot("mix", n))
                m = slice(d % 2 * P, d % 2 * P + P)
                for a, b in PIECES:
                    for k in range(KT):
                        mm = mm3(pair(d)[:, a:b], [x[:, k, m] for x in w], [x[:, k, a:b] for x in hp],
                                 k == 0, k == KT - 1)
                mm.then_inc(S["out_ready"], 1)
            meet("pe", pe)

        def out_act(act, l):
            for i in range(N_OUT):
                if i >= 2:
                    act.wait_ge(S["out_ready"], l * KT + 2 * (i - 1))
                split_hi(act, "mix", base_out[l] + i)
            meet("act", act)

        def residual(d, src, g):
            for s, (a, b) in enumerate(STREAMS):
                ins = nc.vector.scalar_tensor_tensor(xT[:, d, a:b], src[:, a:b], mod[:, g + d, s:s + 1],
                                                     xT[:, d, a:b], ALU.mult, ALU.add)
            return ins

        def out_dve(dve, l):
            split_lo(dve, "mix", base_out[l])
            split_lo(dve, "mix", base_out[l] + 1)
            for d in range(KT):
                dve.wait_ge(S["out_ready"], l * KT + d + 1)
                residual(d, pair(d), 16).then_inc(S["out_free"], 1)
                if d % 2 and d // 2 + 2 < N_OUT:
                    split_lo(dve, "mix", base_out[l] + d // 2 + 2)
            meet("dve", dve)

        flat = pj[:, :, :].rearrange("p a b -> p (a b)")
        lg3 = wk[:, 0:5 * NE].rearrange("p (t e) -> p t e", t=5)
        ge3 = wk[:, 64:64 + 5 * NE].rearrange("p (t e) -> p t e", t=5)
        chosen = wk[:, 128:128 + 5 * NE]
        cmp = wk[:, 256:256 + 5 * 64].rearrange("p (t e f) -> p t e f", t=5, e=NE)
        ceq = wk[:, 640:640 + 5 * 64].rearrange("p (t e f) -> p t e f", t=5, e=NE)
        before32 = wk[:, 1664:1664 + P]
        TB = 2 * SLOT
        count_up = wk[:, TB:TB + CAP]
        slot_of = wk[:, TB + 256:TB + 256 + 5 * BLOCKS].rearrange("p (t b) -> p t b", t=5)
        gate_parts = wk[:, TB + 320:TB + 320 + 8 * BLOCKS].bitcast(F16)[:, 0:15 * BLOCKS].rearrange(
            "p (t b j) -> p t b j", t=5, j=3)
        slot_now = wk[:, TB + 448:TB + 453]
        gates_now = wk[:, TB + 456:TB + 464].bitcast(F16)[:, 0:15].rearrange("p (t j) -> p t j", t=5)
        slot_gates = wk[:, TB + 464:TB + 466]
        htok = [x.rearrange("p (t d) -> p t d", t=5) for x in halves(flat[:, 16 * T:24 * T], 5 * D)]

        def router_pe(pe):
            for t in range(5):
                for k in range(KT):
                    nc.tensor.matmul(ps[:, t * NE:(t + 1) * NE], hT[:, k, t * P:(t + 1) * P], rt[:, k, :],
                                     start=(k == 0), stop=(k == KT - 1))
            for _ in range(4):
                meet("pe", pe)
            for t in range(6):
                for u in range(min(t + 1, 5)):
                    nc.tensor.matmul(ps[:, t * NE:(t + 1) * NE], before32 if u == t else ones[:, :],
                                     chosen[:, u * NE:(u + 1) * NE], start=(u == 0), stop=(u == min(t, 4)))
            meet("pe", pe)
            for g in range(10):
                if g == 0:
                    pe.wait_ge(S["blocks_ready"], 1)
                if g >= 8:
                    pe.wait_ge(S["ht_lo"], g - 7)
                t = g // 2
                for j in range(4):
                    k = 4 * (g % 2) + j
                    mm = nc.tensor.transpose(bank(g % 8)[:, j * P:(j + 1) * P], hT[:, k, t * P:(t + 1) * P], ident[:, :])
                mm.then_inc(S["ht_ready"], 1)

        def router_dve(dve):
            tt, ts = nc.vector.tensor_tensor, nc.vector.tensor_scalar
            meet("dve", dve)
            nc.vector.tensor_copy(wk[:, 0:5 * NE], ps[:, 0:5 * NE])
            nc.vector.tensor_copy(before32, before[:, :])
            dve.drain()
            nc.vector.tensor_reduce(att[:, 0:5], lg3, AX.X, ALU.max)
            for t in range(5):
                le = lg3[:, t].unsqueeze(2).to_broadcast([P, NE, NE])
                lf = lg3[:, t].unsqueeze(1).to_broadcast([P, NE, NE])
                tt(cmp[:, t], lf, le, ALU.is_gt)
                tt(ceq[:, t], lf, le, ALU.is_equal)
            dve.drain()
            tt(lg3, lg3, att[:, 0:5].unsqueeze(2).to_broadcast([P, 5, NE]), ALU.subtract)
            for t in range(5):
                tt(ceq[:, t], ceq[:, t], tri[:, :, :], ALU.mult)
            meet("dve", dve)
            for t in range(5):
                tt(cmp[:, t], cmp[:, t], ceq[:, t], ALU.add)
            dve.drain()
            nc.vector.tensor_reduce(chosen, cmp.rearrange("p t e f -> p (t e) f"), AX.X, ALU.add)
            dve.drain()
            ts(chosen, chosen, float(TOP), None, ALU.is_lt)
            meet("dve", dve)
            tt(wk[:, 64:64 + 5 * NE], wk[:, 64:64 + 5 * NE], chosen, ALU.mult)
            dve.drain()
            nc.vector.tensor_reduce(att[:, 5:10], ge3, AX.X, ALU.add)
            dve.drain()
            nc.vector.reciprocal(att[:, 5:10], att[:, 5:10])
            dve.drain()
            tt(ge3, ge3, att[:, 5:10].unsqueeze(2).to_broadcast([P, 5, NE]), ALU.mult)
            meet("dve", dve)
            one = ones[:, 0:1].to_broadcast([P, CAP])
            nc.vector.tensor_tensor_scan(count_up, one, one, 0.0, ALU.mult, ALU.add)
            dve.drain()
            small = flat[:, 9216:9216 + 128]
            first, numbers = small[:, 0:BLOCKS], small[:, 16:16 + BLOCKS]
            blocks, base, end, t0 = (small[:, 32 + NE * j:40 + NE * j] for j in range(4))
            ts(first, count_up[:, 0:BLOCKS], 1.0, float(CAP), ALU.subtract, ALU.mult)
            ts(numbers, count_up[:, 0:BLOCKS], 1.0, None, ALU.subtract)
            meet("dve", dve)
            count = ps[:, 5 * NE:6 * NE]
            ts(blocks, count, 0.5, None, ALU.is_gt)
            for j in range(1, -(-T // CAP)):
                ts(t0, count, CAP * j + 0.5, None, ALU.is_gt)
                dve.drain()
                tt(blocks, blocks, t0, ALU.add)
                dve.drain()
            c = cmp[:, 0]
            tt(c, blocks.unsqueeze(1).to_broadcast([P, NE, NE]), tri[:, :, :], ALU.mult)
            dve.drain()
            nc.vector.tensor_reduce(base, c, AX.X, ALU.add)
            dve.drain()
            tt(end, base, blocks, ALU.add)
            dve.drain()
            cb = flat[:, 9344:9344 + NE * BLOCKS].rearrange("p (b e) -> p b e", e=NE)
            tt(cb, end.unsqueeze(1).to_broadcast([P, BLOCKS, NE]), numbers.unsqueeze(2).to_broadcast([P, BLOCKS, NE]),
               ALU.is_le)
            dve.drain()
            nc.vector.tensor_reduce(numbers, cb, AX.X, ALU.add)
            dve.drain()
            ts(numbers, numbers, NE - 1.0, None, ALU.min)
            dve.drain()
            nc.vector.tensor_copy(block_expert[:, :], numbers)
            far = 16384.0
            pos = flat[:, 8448:8448 + 5 * NE].rearrange("p (t e) -> p t e", t=5)
            for t in range(5):
                nc.vector.scalar_tensor_tensor(pos[:, t], base, float(CAP), ps[:, t * NE:(t + 1) * NE], ALU.mult, ALU.add)
            dve.drain().then_inc(S["blocks_ready"], 1)
            pf = flat[:, 8448:8448 + 5 * NE]
            nc.vector.scalar_tensor_tensor(pf, chosen, -far, pf, ALU.mult, ALU.add)
            dve.drain()
            ts(pf, pf, far, None, ALU.add)
            dve.drain()
            n = NE * BLOCKS
            d4, v4, u4 = (flat[:, a:a + 5 * n] for a in (0, 512, 1024))

            def tbe(x, t):
                return x[:, t * n:(t + 1) * n].rearrange("p (b e) -> p b e", e=NE)
            for t in range(5):
                tt(tbe(d4, t), pos[:, t].unsqueeze(1).to_broadcast([P, BLOCKS, NE]),
                   first.unsqueeze(2).to_broadcast([P, BLOCKS, NE]), ALU.subtract)
            dve.drain()
            ts(v4, d4, -0.5, None, ALU.is_gt)
            ts(u4, d4, CAP - 0.5, None, ALU.is_lt)
            dve.drain()
            tt(v4, v4, u4, ALU.mult)
            dve.drain()
            nc.vector.scalar_tensor_tensor(d4, d4, 1.0, v4, ALU.add, ALU.mult)
            for t in range(5):
                tt(tbe(u4, t), tbe(v4, t), ge3[:, t].unsqueeze(1).to_broadcast([P, BLOCKS, NE]), ALU.mult)
            dve.drain()
            nc.vector.tensor_reduce(slot_of.rearrange("p t b -> p (t b)"), d4.rearrange("p (a e) -> p a e", e=NE),
                                    AX.X, ALU.add)
            gb = flat[:, 9600:9600 + 5 * BLOCKS]
            nc.vector.tensor_reduce(gb, u4.rearrange("p (a e) -> p a e", e=NE), AX.X, ALU.add)
            dve.drain()
            ts(gb, gb, W_SCALE, None, ALU.mult)
            dve.drain()
            parts = gate_parts.rearrange("p t b j -> p (t b) j")
            for j in range(3):
                nc.vector.tensor_copy(parts[:, :, j:j + 1], gb.unsqueeze(2))
                dve.drain()
                if j < 2:
                    tt(gb.unsqueeze(2), gb.unsqueeze(2), parts[:, :, j:j + 1], ALU.subtract)
                    dve.drain()
            for g in range(10):
                dve.wait_ge(S["ht_hi"], g + 1)
                at = slice(512 * (g % 2), 512 * (g % 2) + 512)
                tt(htok[1][:, g // 2, at], bank(g % 8), htok[0][:, g // 2, at], ALU.subtract).then_inc(S["ht_lo"], 1)

        def router_act(act):
            meet("act", act)
            meet("act", act)
            nc.scalar.activation(wk[:, 64:64 + 5 * NE], wk[:, 0:5 * NE], ACT.Exp, bias=par[:, 1, C_ZERO:C_ZERO + 1])
            meet("act", act)
            meet("act", act)
            meet("act", act)
            for g in range(10):
                act.wait_ge(S["ht_ready"], g + 1)
                at = slice(512 * (g % 2), 512 * (g % 2) + 512)
                nc.scalar.copy(htok[0][:, g // 2, at], bank(g % 8)).then_inc(S["ht_hi"], 1)

        MOE_ORDER = ("U", 0), ("U", 1), ("D", 0), ("U", 2), ("D", 1), ("U", 3), ("D", 2), ("D", 3)
        STAGE = {x: n + 1 for n, x in enumerate(MOE_ORDER)}
        LAST = len(MOE_ORDER)
        load_stage = [STAGE[k, i] for k, i in MOE_ORDER for _ in range(2 if k == "U" else 1)]
        first_load = {x: load_stage.index(n) for x, n in STAGE.items()}
        xg = w3k(halves(flat[:, 0:2048], 2048))
        yparts = w3k(halves(flat[:, 2048:4096], 2048), 2)
        onehot = flat[:, 7168:7808].bitcast(F16).rearrange("p (t s) -> p t s", t=5)
        onehot_t = flat[:, 7808:8448].bitcast(F16).rearrange("p (a t) -> p a t", a=2)

        def e_buf(i):
            return flat[:, 5120 + 512 * (i % 2):5632 + 512 * (i % 2)]

        def hid_buf(i):
            return halves(flat[:, 6144 + 512 * (i % 2):6656 + 512 * (i % 2)], 512)

        def up_bank(i, j):
            return bank(4 + 2 * (i % 2) + j)

        def moe_split(who, eng, b, n, following=False):
            if following:
                m = n + len(MOE_LOADS)
                prod = LAST + load_stage[m - NSLOT]
            else:
                m = n
                prod = LAST + load_stage[n - NSLOT] if n >= NSLOT else None
            if who == "act":
                if prod is not None:
                    eng.wait_ge(S["moe_prod"], b * LAST + prod)
                split_hi(eng, "ffn", base_ffn[1] + m, b * 3)
            else:
                n_hi["dve"] = hi_base["dve"] + m
                split_lo(eng, "ffn", base_ffn[1] + m, 0, b * len(MOE_LOADS))
                n_hi["dve"] = hi_base["dve"]

        hi_base = {"dve": 0}

        def gather_pe(pe, b):
            pe.wait_ge(S["onehot_ready"], b + 1)
            if not (isinstance(b, int) and b == 0):
                pe.wait_ge(S["up_free"], b * 4)
            for g in range(8):
                if g >= 4:
                    pe.wait_ge(S["gath_free_a" if g % 2 == 0 else "gath_free_v"], b * 4 + ((g - 4) // 2 + 1))
                for j in range(2):
                    k = 2 * (g // 2) + j
                    for t in range(5):
                        mm = nc.tensor.matmul(bank(4 + g % 4)[:, j * CAP:(j + 1) * CAP],
                                              htok[g % 2][:, t, k * P:(k + 1) * P], onehot[:, t, :],
                                              start=(t == 0), stop=(t == 4))
                mm.then_inc(S["gathered"], 1)

        def gather_evac(who, eng, b):
            part = 0 if who == "act" else 1
            for g in range(part, 8, 2):
                eng.wait_ge(S["gathered"], b * 8 + (g + 1))
                dst = xg[part][:, 2 * (g // 2):2 * (g // 2) + 2, :].rearrange("p k s -> p (k s)")
                if who == "act":
                    nc.scalar.copy(dst, bank(4 + g % 4)).then_inc(S["gath_free_a"], 1)
                else:
                    nc.vector.tensor_copy(dst, bank(4 + g % 4)).then_inc(S["gath_free_v"], 1)

        def onehot_dve(dve, b):
            nc.vector.tensor_copy(slot_now.unsqueeze(2), slot_of[:, :, bass.ds(b, 1)])
            nc.vector.tensor_copy(gates_now.unsqueeze(2), gate_parts[:, :, bass.ds(b, 1), :])
            dve.drain()
            for t in range(5):
                ins = nc.vector.tensor_scalar(onehot[:, t, :], count_up, slot_now[:, t:t + 1], None, ALU.is_equal)
            ins.then_inc(S["onehot_ready"], 1)

        def moe_pe(pe, b, more):
            for kind, i in MOE_ORDER:
                n = first_load[kind, i]
                if kind == "U":
                    if i == 0:
                        pe.wait_ge(S["gath_free_a"], b * 4 + 4)
                        pe.wait_ge(S["gath_free_v"], b * 4 + 4)
                    if i >= 2:
                        pe.wait_ge(S["up_free"], b * 4 + (i - 1))
                    pe.wait_ge(w_used, b * len(MOE_LOADS) + (base_ffn[1] + n + 2))
                    for j in range(2):
                        w = w3k(split_slot("ffn", base_ffn[1] + n + j))
                        for c in range(2):
                            for k in range(KT):
                                mm = mm3(up_bank(i, j)[:, c * CAP:(c + 1) * CAP], [x[:, k, c * P:(c + 1) * P] for x in w],
                                         [x[:, k, :] for x in xg], k == 0, k == KT - 1)
                    mm.then_inc(S["moe_prod"], 1)
                    if i == 0:
                        pe.wait_ge(S["scat_free"], b * KT + 1)
                        for a in range(2):
                            for t in range(5):
                                lhs = onehot[:, t, a * P:(a + 1) * P]
                                nc.tensor.matmul(pair(a)[:, t * P:(t + 1) * P], lhs, ident16, start=True, stop=True)
                            for t in range(5):
                                mm = nc.tensor.matmul(ps[:, a * 1024 + T:a * 1024 + T + 3], onehot[:, t, a * P:(a + 1) * P],
                                                      gates_now[:, t, :], start=(t == 0), stop=(t == 4))
                        mm.then_inc(S["spread_t"], 1)
                else:
                    pe.wait_ge(w_used, b * len(MOE_LOADS) + (base_ffn[1] + n + 1))
                    pe.wait_ge(S["moe_hid"], b * 4 + (3 + i))
                    if i == 0:
                        pe.wait_ge(S["gt_copied"], b + 1)
                        pe.wait_ge(S["slot_gate"], b + 1)
                    w = w3k(split_slot("ffn", base_ffn[1] + n), 2)
                    hid = [x.rearrange("p (c s) -> p c s", c=2) for x in hid_buf(i)]
                    for a in range(2):
                        for half in range(2):
                            cs = slice(512 * half, 512 * half + 512)
                            for c in range(2):
                                mm = mm3(bank(2 * a + half), [x[:, c, a * P:(a + 1) * P] for x in hid],
                                         [x[:, c, cs] for x in w], i == 0 and c == 0, i == 3 and c == 1)
                    mm.then_inc(S["moe_prod"], 1)
            if more:
                gather_pe(pe, b + 1)
            pe.wait_ge(S["y_low"], b * 4 + 4)
            for d in range(KT):
                if d >= 2:
                    pe.wait_ge(S["scat_free"], b * KT + d)
                for p0, p1 in PIECES:
                    for m, (part, a) in enumerate(((0, 0), (0, 1), (1, 0), (1, 1))):
                        mm = nc.tensor.matmul(pair(d % 2)[:, p0:p1], yparts[part][:, a, d * P:(d + 1) * P],
                                              onehot_t[:, a, p0:p1], start=(m == 0), stop=(m == 3))
                mm.then_inc(S["scat_ready"], 1)

        def moe_silu_act(act, b, i):
            act.wait_ge(S["moe_prod"], b * LAST + (LAST + STAGE["U", i]))
            act.wait_ge(S["moe_hid"], b * 4 + (i + 1))
            sigmoid(act, 1, e_buf(i), up_bank(i, 0), 1.0 / W_SCALE).then_inc(S["e_ready"], 1)

        def moe_silu_dve(dve, b, i):
            hi, lo = hid_buf(i)
            e = e_buf(i)
            dve.wait_ge(S["e_ready"], b * 4 + (i + 1))
            nc.vector.scalar_tensor_tensor(e, up_bank(i, 0), 1.0 / W_SCALE, e, ALU.mult, ALU.mult)
            dve.drain()
            nc.vector.scalar_tensor_tensor(e, up_bank(i, 1), 1.0 / W_SCALE, e, ALU.mult,
                                           ALU.mult).then_inc(S["up_free"], 1)
            used = STAGE["D", i - 2] if i >= 2 else STAGE["D", i + 2] - LAST
            dve.drain()
            dve.wait_ge(S["moe_prod"], b * LAST + (LAST + used))
            nc.vector.tensor_copy(hi, e)
            dve.drain()
            nc.vector.tensor_tensor(lo, e, hi, ALU.subtract).then_inc(S["moe_hid"], 1)

        def moe_act(act, b, more):
            def split(*ns, following=False):
                for n in ns:
                    moe_split("act", act, b, n, following)
            moe_silu_act(act, b, 0)
            split(4)
            act.wait_ge(S["spread_t"], b + 1)
            for a in range(2):
                ins = nc.scalar.copy(onehot_t[:, a, :], pair(a))
            ins.then_inc(S["gt_copied"], 1)
            split(5, 6)
            moe_silu_act(act, b, 1)
            split(7, 8, 9)
            moe_silu_act(act, b, 2)
            split(10, 11)
            moe_silu_act(act, b, 3)
            if more:
                split(0, 1, 2, following=True)
            act.wait_ge(S["moe_prod"], b * LAST + 2 * LAST)
            for q in range(4):
                a, cs = q // 2, slice(512 * (q % 2), 512 * (q % 2) + 512)
                nc.scalar.mul(yparts[0][:, a, cs], bank(q), slot_gates[:, a:a + 1]).then_inc(S["y_high"], 1)
            if more:
                gather_evac("act", act, b + 1)
                split(3, following=True)

        def moe_dve(dve, b, more):
            def split(*ns, following=False):
                for n in ns:
                    moe_split("dve", dve, b, n, following)
            moe_silu_dve(dve, b, 0)
            split(4)
            dve.wait_ge(S["gt_copied"], b + 1)
            for a in range(2):
                nc.vector.tensor_reduce(slot_gates[:, a:a + 1], ps[:, a * 1024 + T:a * 1024 + T + 3], AX.X, ALU.add)
            dve.drain()
            nc.vector.tensor_scalar(slot_gates, slot_gates, Y_SCALE / W_SCALE / W_SCALE, None,
                                    ALU.mult).then_inc(S["slot_gate"], 1)
            split(5, 6)
            moe_silu_dve(dve, b, 1)
            split(7, 8, 9)
            moe_silu_dve(dve, b, 2)
            split(10, 11)
            moe_silu_dve(dve, b, 3)
            if more:
                onehot_dve(dve, b + 1)
                split(0, 1, 2, following=True)
            for q in range(4):
                dve.wait_ge(S["y_high"], b * 4 + (q + 1))
                a, cs = q // 2, slice(512 * (q % 2), 512 * (q % 2) + 512)
                nc.vector.scalar_tensor_tensor(yparts[1][:, a, cs], bank(q), slot_gates[:, a:a + 1], yparts[0][:, a, cs],
                                               ALU.mult, ALU.subtract).then_inc(S["y_low"], 1)
            if more:
                gather_evac("dve", dve, b + 1)
            for d in range(KT):
                dve.wait_ge(S["scat_ready"], b * KT + (d + 1))
                residual(d, pair(d % 2), 40).then_inc(S["scat_free"], 1)
            if more:
                split(3, following=True)

        ident16 = before[:, :].bitcast(F16)

        def moe(who, eng):
            if who == "pe":
                eng.drain().then_inc(S["moe_prod"], LAST)
                gather_pe(eng, 0)
                step = moe_pe
            elif who == "act":
                for n in range(NSLOT):
                    moe_split("act", eng, 0, n)
                gather_evac("act", eng, 0)
                step = moe_act
            else:
                eng.drain().then_inc(S["moe_hid"], 2)
                nc.vector.tensor_copy(ident16, ident[:, :])
                eng.drain().then_inc(S["scat_free"], 1)
                onehot_dve(eng, 0)
                hi_base["dve"] = n_hi["dve"]
                for n in range(NSLOT):
                    moe_split("dve", eng, 0, n)
                gather_evac("dve", eng, 0)
                step = moe_dve
            with eng.Fori(0, BLOCKS - 1) as b:
                step(eng, b, True)
            step(eng, BLOCKS - 1, False)
            meet(who, eng)

        def act_buf(i):
            return w3k(halves(pj[:, 8 + 2 * (i % 2):10 + 2 * (i % 2), :].rearrange("p a b -> p (a b)"), 2 * T), 2)

        def up_pe(pe, n, q0):
            hp = split_h("ffn")
            pe.wait_ge(w_used, n + 2)
            w = [w3k(split_slot("ffn", n + i)) for i in range(2)]
            for c in range(2):
                for i in range(2):
                    q = q0 + 2 * c + i
                    if q >= 4:
                        pe.wait_ge(S["f_free"], q - 3)
                    for a, e in PIECES:
                        for k in range(KT):
                            mm = mm3(pair(q)[:, a:e], [x[:, k, c * P:(c + 1) * P] for x in w[i]],
                                     [x[:, k, a:e] for x in hp], k == 0, k == KT - 1)
                    mm.then_inc(S["f_ready"], 1)

        def down_pe(pe, n, item, q0):
            pe.wait_ge(w_used, n + 1)
            pe.wait_ge(S["hid_ready"], 2 * item + 2)
            w = w3k(split_slot("ffn", n), 2)
            hid = act_buf(item)
            for d in range(KT):
                q = q0 + d
                pe.wait_ge(S["f_free"], q - 3)
                for a, e in PIECES:
                    for c in range(2):
                        mm = mm3(pair(q)[:, a:e], [x[:, c, d * P:(d + 1) * P] for x in w],
                                 [x[:, c, a:e] for x in hid], c == 0, c == 1)
                mm.then_inc(S["f_ready"], 1)

        def up_act(act, item, q0):
            for c in range(2):
                q = q0 + 2 * c
                act.wait_ge(S["f_ready"], q + 1)
                if item > 0:
                    act.wait_ge(S["hid_ready"], 2 * item + c - 1)
                sigmoid(act, 0, pj[:, 12 + c, :], pair(q), 1.0 / W_SCALE).then_inc(S["f_exp"], 1)

        def up_dve(dve, item, q0):
            hi, lo = act_buf(item)
            for c in range(2):
                e = pj[:, 12 + c, :]
                q = q0 + 2 * c
                dve.wait_ge(S["f_exp"], 2 * item + c + 1)
                nc.vector.scalar_tensor_tensor(e, pair(q), 1.0 / W_SCALE, e, ALU.mult,
                                               ALU.mult).then_inc(S["f_free"], 1)
                dve.drain()
                dve.wait_ge(S["f_ready"], q + 2)
                nc.vector.scalar_tensor_tensor(e, pair(q + 1), 1.0 / W_SCALE, e, ALU.mult,
                                               ALU.mult).then_inc(S["f_free"], 1)
                dve.drain()
                nc.vector.tensor_copy(hi[:, c, :], e)
                dve.drain()
                nc.vector.tensor_tensor(lo[:, c, :], e, hi[:, c, :], ALU.subtract).then_inc(S["hid_ready"], 1)

        def down_dve(dve, q0):
            for d in range(KT):
                dve.wait_ge(S["f_ready"], q0 + d + 1)
                residual(d, pair(q0 + d), 40).then_inc(S["f_free"], 1)
            dve.drain()

        def ffn(up, down, split):
            for n in range(2, 4):
                split(n, None)
            up(0, 0, 0)
            split(4, 4)
            for i in range(DENSE_ITEMS):
                q, more = 4 + 12 * i, i + 2 < DENSE_ITEMS
                if more:
                    split(5 + 3 * i, 12 * i + 4)
                if i + 1 < DENSE_ITEMS:
                    up(i + 1, q, 2 + 3 * i)
                    if more:
                        split(6 + 3 * i, 12 * i + 8)
                        split(7 + 3 * i, 12 * i + 8)
                    else:
                        split(5 + 3 * i, 12 * i + 8)
                    down(i, q + 4, 4 + 3 * i)
                else:
                    down(i, q, 2 + 3 * i)

        def ffn_pe(pe, l):
            b = base_ffn[l]
            ffn(lambda i, q, n: up_pe(pe, b + n, q), lambda i, q, n: down_pe(pe, b + n, i, q), lambda *a: None)
            meet("pe", pe)

        def ffn_dve(dve, l):
            ffn(lambda i, q, n: up_dve(dve, i, q), lambda i, q, n: down_dve(dve, q),
                lambda n, after: split_lo(dve, "ffn", base_ffn[l] + n))
            meet("dve", dve)

        def ffn_act(act, l):
            def split(n, after):
                if after is not None:
                    act.wait_ge(S["f_ready"], after)
                split_hi(act, "ffn", base_ffn[l] + n)
            ffn(lambda i, q, n: up_act(act, i, q), lambda *a: None, split)
            meet("act", act)

        def early_in(l):
            return [("mix", base_in[l] + n) for n in range(2)]

        def early_ffn(l):
            return [("ffn", base_ffn[l] + n) for n in range(2)] if l == 0 else []

        @block.tensor
        def _(pe):
            pe.wait_ge(c_loaded, 32)
            meet("pe", pe)
            for l in range(DEPTH):
                mod_pe(pe, l)
                norm_pe(pe, 2 * l)
                split_pe(pe)
                in_pe(pe, l)
                front_pe(pe, l)
                gla_all_pe(pe, l)
                scan_out_pe(pe)
                conv_pe(pe, l)
                gdn_all_pe(pe, l)
                scan_out_pe(pe)
                attn_pe(pe, l)
                split_pe(pe)
                out_pe(pe, l)
                norm_pe(pe, 2 * l + 1)
                if l == 1:
                    router_pe(pe)
                    meet("pe", pe)
                    moe("pe", pe)
                else:
                    split_pe(pe)
                    ffn_pe(pe, l)

        @block.scalar
        def _(act):
            act.wait_ge(c_loaded, 32)
            nc.scalar.preload_act_table_set("natural_log_exp_and_others")
            nc.scalar.activation(cE[:], cT[:], ACT.Exp, bias=par[:, 0, C_ZERO:C_ZERO + 1], scale=-1.0)
            meet("act", act)
            for l in range(DEPTH):
                mod_act(act, l)
                if l == 0:
                    act.wait_ge(consts_loaded, 16 * N_CONST)
                norm_act(act, 2 * l, l, early_in(l))
                split_act(act, "mix")
                in_evac("act", act, l)
                front_act(act, l)
                gla_all_act(act, l)
                scan_out_act(act, l, AR)
                conv_act(act, l)
                gdn_all_act(act, l)
                scan_out_act(act, l, DR)
                attn_act(act, l)
                split_act(act, "mix")
                out_act(act, l)
                norm_act(act, 2 * l + 1, l, early_ffn(l))
                if l == 1:
                    router_act(act)
                    meet("act", act)
                    moe("act", act)
                else:
                    split_act(act, "ffn")
                    ffn_act(act, l)

        @block.vector
        def _(dve):
            dve.wait_ge(c_loaded, 32)
            meet("dve", dve)
            nc.vector.tensor_scalar(cE[:], cE[:], 1.0, None, ALU.add)
            dve.drain()
            nc.vector.reciprocal(cE[:], cE[:])
            dve.drain()
            nc.vector.tensor_tensor(cT[:], cT[:], cE[:], ALU.mult)
            dve.drain()
            for d in range(2):
                dve.drain().then_inc(S["gla_done"][d], 1)
                dve.drain().then_inc(S["gla_staging"][d], 1)
                dve.drain().then_inc(S["gdn_done"][d], 1)
            for l in range(DEPTH):
                mod_dve(dve, l)
                if l == 0:
                    dve.wait_ge(consts_loaded, 16 * N_CONST)
                norm_dve(dve, 2 * l, early_in(l))
                split_dve(dve, "mix")
                in_evac("dve", dve, l)
                dve.drain().then_inc(S["proj_done"], 1)
                if l > 0:
                    dve.wait_ge(S["states_out"], 80 * l)
                nc.vector.memset(st_a[0][:], 0.0)
                nc.vector.memset(st_d[0][:], 0.0)
                front_dve(dve, l)
                dve.wait_ge(S["cache_in"], 80 * (l + 1))
                gla_all_dve(dve, l)
                scan_out_dve(dve, l, OA, AR, C_AON)
                conv_dve(dve, l)
                dve.drain().then_inc(S["mixer_a_done"], 1)
                gdn_all_dve(dve, l)
                dve.drain().then_inc(S["mixer_d_done"], 1)
                scan_out_dve(dve, l, OD, DR, C_DON)
                attn_dve(dve, l)
                split_dve(dve, "mix")
                out_dve(dve, l)
                dve.wait_ge(S["states_out"], 80 * (l + 1))
                norm_dve(dve, 2 * l + 1, early_ffn(l))
                if l == 1:
                    router_dve(dve)
                    meet("dve", dve)
                    moe("dve", dve)
                else:
                    split_dve(dve, "ffn")
                    ffn_dve(dve, l)
            dve.drain().then_inc(S["final_x"], 1)


N_CONST = 15


def constants():
    def bits(m):
        return (m * 0x3F80).astype(np.uint16)
    i = np.arange(P)
    f, j = i % L, i // L
    c = {"ident": np.eye(P), "ones": np.ones((P, P)), "blk": (j[:, None] == j[None, :]) * 1.0}
    sel = np.zeros((P, 4, P))
    for d in range(2):
        for h in range(4):
            for r in (R_BETA + 4 * d + h, R_DEC[d] + h):
                sel[r, 2 * d + h // 2, L * (h % 2):L * (h % 2) + L] = 1.0
    c["sel"] = sel
    src = np.where(f % 32 < 16, i + 16, i - 16)
    rot = np.zeros((P, P))
    rot[src, i] = np.where(f % 32 < 16, -1.0, 1.0)
    c["rot"] = rot
    tok = np.arange(NS_TOK)
    pos = np.where((f < 32)[:, None], (tok // L)[None, :], (tok % L)[None, :]).astype(np.float32)
    inv = (1.0 / (np.float32(10000.0) ** (np.arange(16, dtype=np.float32) / np.float32(16))))[f % 16]
    ang = pos * inv[:, None].astype(np.float32)
    c["cossin"] = np.stack([np.cos(ang), np.sin(ang)], 1)
    t = np.arange(T)
    c["cmask"] = np.broadcast_to(np.stack([t % L != 0, t % L != L - 1])[None], (P, 2, T))
    a, b = f[:, None], np.arange(L)[None, :]
    inc = np.stack([a <= b, a >= b], 1)
    c["incl"] = np.broadcast_to(inc[:, :, None, :], (P, 2, 2, L))
    lv = []
    for s in (1, 2, 4, 8, 16, 32):
        fwd = ((b // s) % 2 == 1) & (a // s == b // s - 1)
        bwd = ((a // s) % 2 == 1) & (b // s == a // s - 1)
        lv.append(np.stack([fwd, bwd], 1))
    c["lvl"] = np.broadcast_to(np.stack(lv, 1)[:, :, :, None, :], (P, 6, 2, 2, L))
    q, k = i[:, None], np.arange(3 * P)[None, :] - P
    c["swamask"] = np.where(abs(q - k) <= P, 0.0, NEG)
    col = np.arange(L)
    cs = np.clip(col - 8, 0, L - 16)
    m = ((col[None, :] >= cs[:, None]) & (col[None, :] < cs[:, None] + 16))[f]
    c["nmask"] = np.stack([m * 1.0, np.where(m, 0.0, NEG)], 1)
    c["tri"] = np.broadcast_to((np.arange(NE)[None, :] < np.arange(NE)[:, None])[None], (P, NE, NE))
    c["before"] = i[:, None] < i[None, :]
    return {n: np.ascontiguousarray(bits(v) if n in BITS else v.astype(np.float32)) for n, v in c.items()}


def layouts(x):
    f32 = np.float32

    def feat(a):
        return np.moveaxis(a.reshape(a.shape[:-1] + (KT, P)), (-1, -2), (0, 1))

    def rows(w, width):
        s = w.shape[:-2]
        w = w.reshape(s + (KT, P, w.shape[-1] // width, width))
        k = len(s)
        return np.moveaxis(w, (k + 2, k + 1, k, k + 3), (k, k + 1, k + 2, k + 3)).reshape(s + (-1, P, KT * width))

    def down(w):
        s = w.shape[:-2]
        w = w.reshape(s + (w.shape[-2] // WCOL, 2, P, D))
        return np.swapaxes(w, -3, -2).reshape(s + (-1, P, 2 * D))

    o = constants()
    o["xT"] = feat(np.concatenate([x["x_prompt"][0], x["x_sample"][0]]))
    o["cT"] = feat(np.stack([x["c_ctx"], x["c"][0]]))
    o["wmod"] = rows(x["w_mod"], WCOL)
    w = x["w_in"]
    cut = [0] + list(np.cumsum([256] * 4 + [16] * 2 + [256, 128, 128] + [256] * 3 + [256] * 4 + [4] * 4))
    part = [w[:, :, a:b] for a, b in zip(cut[:-1], cut[1:])]
    aq, ak, av, ar, alf, alb, sq, sk, sv, nq, nk, nv, dq, dk, dv, dr, daf, dab, dbf, dbb = part

    def z(n):
        return np.zeros((DEPTH, D, n), f32)
    sq = sq.reshape(DEPTH, D, 2, 2, L).transpose(0, 1, 3, 2, 4).reshape(DEPTH, D, 256)
    small = np.concatenate([alf, alb, dbf, dbb, z(24), daf, z(28), dab, z(28)], -1)
    o["win"] = rows(np.concatenate([aq, ak, av, ar, sq, sk, nq, nk, dq, dk, dv, dr, small], -1), WCOL)
    o["wv"] = rows(np.concatenate([sv, nv, z(2 * WCOL - V_COLS)], -1), WCOL)
    wo = x["w_out"].reshape(DEPTH, 4, 256, D).copy()
    wo[:, 1] = wo[:, 1].reshape(DEPTH, 2, 2, L, D).transpose(0, 2, 1, 3, 4).reshape(DEPTH, 256, D)
    o["wout"] = rows(wo.reshape(DEPTH, D, D), WCOL)
    o["d1"], o["d3"], o["d2"] = rows(x["ffn_w1"][0], WCOL), rows(x["ffn_w3"][0], WCOL), down(x["ffn_w2"][0])
    o["e1"] = rows(x["moe_w1"][0], WCOL).reshape(-1, P, SLOT)
    o["e3"] = rows(x["moe_w3"][0], WCOL).reshape(-1, P, SLOT)
    o["e2"] = down(x["moe_w2"][0]).reshape(-1, P, SLOT)
    o["router"] = x["moe_router"][0].reshape(KT, P, NE).transpose(1, 0, 2)

    par = np.zeros((P, DEPTH, NPAR), f32)
    for l in range(DEPTH):
        def put(c, a):
            par[:, l, c:c + a.shape[1]] = a
        put(C_N1, x["norm1_g"][l].reshape(KT, P).T)
        put(C_N2, x["norm2_g"][l].reshape(KT, P).T)
        put(C_BMOD, x["b_mod"][l].reshape(48, P).T)
        put(C_BUP, x["gla_bup"][l].reshape(4, P).T)
        for c, n in ((C_AON, "gla_onorm"), (C_SQN, "swa_qnorm"), (C_SKN, "swa_knorm"), (C_NQN, "na_qnorm"),
                     (C_NKN, "na_knorm"), (C_DON, "gdn_onorm")):
            put(c, np.tile(x[n][l], 2)[:, None])
        put(C_SINK, np.broadcast_to(x["swa_sink"][l][None], (P, 4)))
        put(C_CONV, x["gdn_conv"][l].reshape(3, 6, P).transpose(2, 1, 0).reshape(P, 18))
        for d in range(2):
            par[R_DEC[d]:R_DEC[d] + 4, l, C_ALOG] = x["gdn_alog"][l, d]
            par[R_DEC[d]:R_DEC[d] + 4, l, C_DTB] = x["gdn_dtbias"][l, d]
        par[:, l, C_EPS], par[:, l, C_ONE] = EPS, 1.0
    o["par"] = par
    wup = np.zeros((32, DEPTH, 4, P), f32)
    for d in range(2):
        wup[16 * d:16 * d + 16, :, 2 * d:2 * d + 2] = x["gla_wup"][:, d].reshape(DEPTH, 16, 2, P).transpose(1, 0, 2, 3)
    o["wup"] = wup
    sk_, nk_ = x["cache_swa_k"][0], x["cache_na_k"][0]
    o["ck"] = np.concatenate([sk_.transpose(0, 1, 3, 2).reshape(DEPTH, 1, P, PAST),
                              nk_.transpose(0, 1, 3, 2).reshape(DEPTH, 2, P, PAST)], 1).transpose(0, 2, 1, 3)
    v = np.concatenate([x["cache_swa_v"][0], x["cache_na_v"][0]], 1)
    o["cv"] = v.reshape(DEPTH, 6, 2, P, L).transpose(0, 3, 2, 1, 4).reshape(DEPTH, P, 2, V_COLS)
    for n, s in (("sta", "state_gla"), ("std", "state_gdn")):
        o[n] = x[s][0].reshape(DEPTH, 2, 2, P, L).transpose(0, 3, 1, 2, 4)
    r = np.pad(x["na_rpb"], ((0, 0), (0, 0), (1, 1), (48, 48)))
    q, k, m = np.arange(L)[:, None], np.arange(L)[None, :], np.arange(16)
    win = r[:, :, :, k - q + 63]
    o["rpb"] = np.stack([win[:, :, m + 1 - rr].transpose(0, 3, 1, 2, 4) for rr in range(2)], 1).reshape(DEPTH, P, 4096)
    return {n: np.ascontiguousarray(a) for n, a in o.items()}


BITS = ("cmask", "incl", "lvl", "tri", "before")


OUTS = {"yT": (P, KT, T), "new_k": (DEPTH, P, NP_TOK), "new_nk": (DEPTH, P, 2, NP_TOK), "new_v": (DEPTH, P, V_COLS),
        "new_sta": (DEPTH, P, 2, 2, L), "new_std": (DEPTH, P, 2, 2, L)}


def declare(nc, arrays):
    A = {n: nc.dram_tensor(f"in_{n}", a.shape, mybir.dt.from_np(a.dtype), kind="ExternalInput").ap()
         for n, a in arrays.items()}
    for n in BITS:
        A[n] = A[n].bitcast(BF16)
    A |= {n: nc.dram_tensor(n, s, F32, kind="ExternalOutput").ap() for n, s in OUTS.items()}
    build(nc, A)


def kernel(**inputs):
    import concourse.bacc as bacc
    from concourse.bass_utils import run_bass_kernel_spmd
    arrays = layouts({n: np.asarray(a) for n, a in inputs.items()})
    nc = bacc.Bacc("TRN2", target_bir_lowering=False, num_devices=1)
    declare(nc, arrays)
    r = run_bass_kernel_spmd(nc, [{f"in_{n}": a for n, a in arrays.items()}], core_ids=[0]).results[0]
    return results(r)


def results(r):
    y = np.moveaxis(r["yT"], (1, 0), (1, 2)).reshape(T, D)
    k = r["new_k"].reshape(DEPTH, 2, L, NP_TOK).transpose(0, 1, 3, 2)[None]
    nk = r["new_nk"].reshape(DEPTH, 2, L, 2, NP_TOK).transpose(0, 3, 1, 4, 2).reshape(1, DEPTH, 4, NP_TOK, L)
    v = r["new_v"].reshape(DEPTH, P, 6, L).transpose(0, 2, 1, 3)
    sta, std = (r[n].transpose(0, 2, 3, 1, 4).reshape(1, DEPTH, 2, 4, L, L) for n in ("new_sta", "new_std"))
    out = (y[None, :NP_TOK], y[None, NP_TOK:], k, v[None, :, 0:2], nk, v[None, :, 2:6], sta, std)
    return tuple(np.ascontiguousarray(a) for a in out)
```
